# Optimizing a Trainium2 kernel written in Bass

```python
import jax, jax.numpy as jnp
from jax import lax
import numpy as np

D_MODEL = 1024
BATCH = 1
SEQ = 256
DEPTH = 1

N_MIXERS = 4
HEAD_DIM = 64
N_Q_HEADS = D_MODEL // HEAD_DIM
N_KV_HEADS = 4
GQA_GROUP = N_Q_HEADS // N_KV_HEADS
ATTN_Q_DIM = N_Q_HEADS * HEAD_DIM
ATTN_KV_DIM = N_KV_HEADS * HEAD_DIM
ATTN_IN_DIM = ATTN_Q_DIM + 2 * ATTN_KV_DIM
SWA_WINDOW = 128
SWA_BLOCK = 128
MOBA_BLOCK = 256
MOBA_TOP_K = 3
MOBA_Q_CHUNK = 64
GLA_HEADS = 4
GLA_KEY_DIM = D_MODEL // (2 * GLA_HEADS)
GLA_VAL_DIM = D_MODEL // GLA_HEADS
GLA_GATE_RANK = 16
GLA_GATE_TEMP = 16.0
GLA_IN_DIM = 2 * GLA_HEADS * GLA_KEY_DIM + 2 * GLA_HEADS * GLA_VAL_DIM + GLA_GATE_RANK
HGRN_EXPAND = 128
HGRN_HEADS = D_MODEL // HGRN_EXPAND
HGRN_KEY_DIM = HGRN_EXPAND
HGRN_VAL_DIM = D_MODEL // HGRN_HEADS
HGRN_IN_DIM = 4 * D_MODEL
LIN_CHUNK = 64
D_FF = ((8 * D_MODEL + 3 * 256 - 1) // (3 * 256)) * 256
RMS_EPS = 1e-6


def rms_norm(x, w):
    xf = x.astype(jnp.float32)
    y = xf * lax.rsqrt(jnp.mean(xf * xf, axis=-1, keepdims=True) + RMS_EPS)
    return (y * w.astype(jnp.float32)).astype(x.dtype)

def head_rms_norm(o, w):
    return o * lax.rsqrt(jnp.mean(o * o, axis=-1, keepdims=True) + RMS_EPS) * w.astype(jnp.float32)

def alibi_slopes(n_heads):
    return jnp.exp2(-8.0 * jnp.arange(1, n_heads + 1, dtype=jnp.float32) / n_heads)

def split_qkv(h, w_in):
    B, T, _ = h.shape
    proj = h @ w_in
    q = proj[..., :ATTN_Q_DIM].reshape(B, T, N_KV_HEADS, GQA_GROUP, HEAD_DIM)
    k = proj[..., ATTN_Q_DIM:ATTN_Q_DIM + ATTN_KV_DIM].reshape(B, T, N_KV_HEADS, HEAD_DIM)
    v = proj[..., ATTN_Q_DIM + ATTN_KV_DIM:].reshape(B, T, N_KV_HEADS, HEAD_DIM)
    return q, k, v

def sliding_window_sink_attention(h, w_in, sinks, w_out):
    B, T, _ = h.shape
    L = SWA_BLOCK
    nb = T // L
    q, k, v = split_qkv(h, w_in)
    qb = q.reshape(B, nb, L, N_KV_HEADS, GQA_GROUP, HEAD_DIM)

    def with_prev(a):
        a = a.reshape(B, nb, L, N_KV_HEADS, HEAD_DIM)
        prev = jnp.concatenate([jnp.zeros_like(a[:, :1]), a[:, :-1]], axis=1)
        return jnp.concatenate([prev, a], axis=2)

    kw, vw = with_prev(k), with_prev(v)
    s = jnp.einsum('bnqhgd,bnkhd->bnhgqk', qb, kw, preferred_element_type=jnp.float32) * (HEAD_DIM ** -0.5)
    dist = (L + jnp.arange(L))[:, None] - jnp.arange(2 * L)[None, :]
    band = (dist >= 0) & (dist < SWA_WINDOW)
    has_prev = (jnp.arange(nb)[:, None, None] > 0) | (jnp.arange(2 * L)[None, None, :] >= L)
    mask = band[None] & has_prev
    slopes = alibi_slopes(N_Q_HEADS).reshape(N_KV_HEADS, GQA_GROUP)
    s = s - slopes[:, :, None, None] * dist.astype(jnp.float32)
    s = jnp.where(mask[None, :, None, None], s, -jnp.inf)
    sink = sinks.astype(jnp.float32).reshape(N_KV_HEADS, GQA_GROUP)[:, :, None, None]
    m = jnp.maximum(jnp.max(s, axis=-1, keepdims=True), sink)
    p = jnp.exp(s - m)
    denom = jnp.sum(p, axis=-1, keepdims=True) + jnp.exp(sink - m)
    o = jnp.einsum('bnhgqk,bnkhd->bnqhgd', p / denom, vw.astype(jnp.float32))
    return o.reshape(B, T, ATTN_Q_DIM).astype(h.dtype) @ w_out

def moba_attention(h, w_in, w_out):
    B, T, _ = h.shape
    Lb, Qc = MOBA_BLOCK, MOBA_Q_CHUNK
    q, k, v = split_qkv(h, w_in)
    Tp = ((T + Lb - 1) // Lb) * Lb
    pad = Tp - T
    q = jnp.pad(q.astype(jnp.float32), ((0, 0), (0, pad), (0, 0), (0, 0), (0, 0))) * (HEAD_DIM ** -0.5)
    k = jnp.pad(k.astype(jnp.float32), ((0, 0), (0, pad), (0, 0), (0, 0)))
    v = jnp.pad(v.astype(jnp.float32), ((0, 0), (0, pad), (0, 0), (0, 0)))
    nblk, nq = Tp // Lb, Tp // Qc
    n_sel = min(MOBA_TOP_K, nblk)
    kb = k.reshape(B, nblk, Lb, N_KV_HEADS, HEAD_DIM).transpose(0, 3, 1, 2, 4)
    vb = v.reshape(B, nblk, Lb, N_KV_HEADS, HEAD_DIM).transpose(0, 3, 1, 2, 4)
    k_mean = jnp.mean(kb, axis=3)
    gate = jnp.einsum('bthgd,bhnd->bhtn', q, k_mean)
    t_blk = jnp.arange(Tp) // Lb
    past = jnp.arange(nblk)[None, :] < t_blk[:, None]
    gate = jnp.where(past, gate, -jnp.inf)
    _, sel_idx = lax.top_k(gate, n_sel)
    sel_valid = jnp.arange(n_sel)[None, :] < t_blk[:, None]
    q_chunks = q.reshape(B, nq, Qc, N_KV_HEADS, GQA_GROUP, HEAD_DIM).transpose(1, 0, 2, 3, 4, 5)
    idx_chunks = sel_idx.reshape(B, N_KV_HEADS, nq, Qc, n_sel).transpose(2, 0, 1, 3, 4)
    valid_chunks = sel_valid.reshape(nq, Qc, n_sel)
    slopes = alibi_slopes(N_Q_HEADS).reshape(N_KV_HEADS, GQA_GROUP)
    gather_blocks = jax.vmap(jax.vmap(lambda blocks, ix: blocks[ix]))

    def attend(args):
        c, qc, idx, valid = args
        t_q = c * Qc + jnp.arange(Qc)
        own = (c * Qc) // Lb
        k_own = lax.dynamic_index_in_dim(kb, own, axis=2, keepdims=False)
        v_own = lax.dynamic_index_in_dim(vb, own, axis=2, keepdims=False)
        k_sel = gather_blocks(kb, idx)
        v_sel = gather_blocks(vb, idx)
        s_sel = jnp.einsum('bqhgd,bhqnkd->bhgqnk', qc, k_sel)
        dist_sel = (t_q[:, None, None] - (idx[..., None] * Lb + jnp.arange(Lb))).astype(jnp.float32)
        s_sel = s_sel - slopes[None, :, :, None, None, None] * dist_sel[:, :, None]
        s_sel = jnp.where(valid[:, :, None], s_sel, -jnp.inf)
        s_own = jnp.einsum('bqhgd,bhkd->bhgqk', qc, k_own)
        dist_own = t_q[:, None] - (own * Lb + jnp.arange(Lb))[None, :]
        s_own = s_own - slopes[:, :, None, None] * dist_own.astype(jnp.float32)
        s_own = jnp.where(dist_own >= 0, s_own, -jnp.inf)
        s_all = jnp.concatenate([s_sel.reshape(B, N_KV_HEADS, GQA_GROUP, Qc, n_sel * Lb), s_own], axis=-1)
        p = jax.nn.softmax(s_all, axis=-1)
        p_sel = p[..., :n_sel * Lb].reshape(B, N_KV_HEADS, GQA_GROUP, Qc, n_sel, Lb)
        p_own = p[..., n_sel * Lb:]
        return (jnp.einsum('bhgqnk,bhqnkd->bqhgd', p_sel, v_sel)
                + jnp.einsum('bhgqk,bhkd->bqhgd', p_own, v_own))

    o = lax.map(attend, (jnp.arange(nq), q_chunks, idx_chunks, valid_chunks))
    o = o.transpose(1, 0, 2, 3, 4, 5).reshape(B, Tp, ATTN_Q_DIM)[:, :T]
    return o.astype(h.dtype) @ w_out

def chunked_gated_linear_attention(q, k, v, log_g):
    B, T, H, K = q.shape
    V = v.shape[-1]
    L = LIN_CHUNK
    nc = T // L

    def to_chunks(a):
        return a.astype(jnp.float32).reshape(B, nc, L, H, a.shape[-1]).transpose(1, 0, 3, 2, 4)

    causal = jnp.tril(jnp.ones((L, L), dtype=bool))

    def step(S, inp):
        qc, kc, vc, gc = inp
        b = jnp.cumsum(gc, axis=2)
        b_last = b[:, :, -1:, :]
        q_dec = qc * jnp.exp(b)
        attn = jnp.einsum('bhtk,bhsk->bhts', q_dec, kc * jnp.exp(-b))
        attn = jnp.where(causal, attn, 0.0)
        o = jnp.einsum('bhts,bhsv->bhtv', attn, vc) + jnp.einsum('bhtk,bhkv->bhtv', q_dec, S)
        S = S * jnp.exp(b_last).swapaxes(-1, -2) + jnp.einsum('bhsk,bhsv->bhkv', kc * jnp.exp(b_last - b), vc)
        return S, o

    S0 = jnp.zeros((B, H, K, V), jnp.float32)
    _, o = lax.scan(step, S0, (to_chunks(q), to_chunks(k), to_chunks(v), to_chunks(log_g)))
    return o.transpose(1, 0, 3, 2, 4).reshape(B, T, H, V)

def gla_mixer(h, w_in, w_decay_up, b_decay, out_norm, w_out):
    B, T, _ = h.shape
    proj = h @ w_in
    dk, dv = GLA_HEADS * GLA_KEY_DIM, GLA_HEADS * GLA_VAL_DIM
    q = proj[..., :dk].reshape(B, T, GLA_HEADS, GLA_KEY_DIM).astype(jnp.float32) * (GLA_KEY_DIM ** -0.5)
    k = proj[..., dk:2 * dk].reshape(B, T, GLA_HEADS, GLA_KEY_DIM)
    v = proj[..., 2 * dk:2 * dk + dv].reshape(B, T, GLA_HEADS, GLA_VAL_DIM)
    g = proj[..., 2 * dk + dv:2 * dk + 2 * dv].reshape(B, T, GLA_HEADS, GLA_VAL_DIM)
    a = proj[..., 2 * dk + 2 * dv:]
    log_alpha = jax.nn.log_sigmoid((a @ w_decay_up + b_decay).astype(jnp.float32)) / GLA_GATE_TEMP
    log_alpha = log_alpha.reshape(B, T, GLA_HEADS, GLA_KEY_DIM)
    o = chunked_gated_linear_attention(q, k, v, log_alpha)
    o = head_rms_norm(o, out_norm) * jax.nn.silu(g.astype(jnp.float32))
    return o.reshape(B, T, dv).astype(h.dtype) @ w_out

def hgrn2_mixer(h, w_in, lower_bound, out_norm, w_out):
    B, T, _ = h.shape
    proj = h @ w_in
    d = D_MODEL
    q = jax.nn.silu(proj[..., :d].astype(jnp.float32)) * (HGRN_KEY_DIM ** -0.5)
    f = lower_bound + (1.0 - lower_bound) * jax.nn.sigmoid(proj[..., d:2 * d].astype(jnp.float32))
    i = proj[..., 2 * d:3 * d]
    g = proj[..., 3 * d:]
    shp_k = (B, T, HGRN_HEADS, HGRN_KEY_DIM)
    o = chunked_gated_linear_attention(q.reshape(shp_k), (1.0 - f).reshape(shp_k),
                                       i.reshape(B, T, HGRN_HEADS, HGRN_VAL_DIM), jnp.log(f).reshape(shp_k))
    o = head_rms_norm(o, out_norm) * jax.nn.silu(g.astype(jnp.float32)).reshape(B, T, HGRN_HEADS, HGRN_VAL_DIM)
    return o.reshape(B, T, HGRN_HEADS * HGRN_VAL_DIM).astype(h.dtype) @ w_out

def swiglu_ffn(h, w_gate_up, w_down):
    gu = h @ w_gate_up
    return (jax.nn.silu(gu[..., :D_FF]) * gu[..., D_FF:]) @ w_down

def first_inputs(seed: int = 0) -> dict:
    key = jax.random.key(seed)
    ks = jax.random.split(key, 20)
    n_a, n_b, n_c, n_d = [(DEPTH - kind + N_MIXERS - 1) // N_MIXERS for kind in range(N_MIXERS)]

    def normal(k, shape):
        return jax.random.normal(k, shape, jnp.float32)

    def dense(k, shape, fan_in):
        return normal(k, shape) * (fan_in ** -0.5)

    def gain(k, shape):
        return 1.0 + 0.02 * normal(k, shape)

    return {
        'x': normal(ks[0], (BATCH, SEQ, D_MODEL)),
        'norm_mix': gain(ks[1], (DEPTH, D_MODEL)),
        'norm_ffn': gain(ks[2], (DEPTH, D_MODEL)),
        'swa_w_in': dense(ks[3], (n_a, D_MODEL, ATTN_IN_DIM), D_MODEL),
        'swa_sinks': 0.5 * normal(ks[4], (n_a, N_Q_HEADS)),
        'swa_w_out': dense(ks[5], (n_a, ATTN_Q_DIM, D_MODEL), ATTN_Q_DIM),
        'moba_w_in': dense(ks[6], (n_b, D_MODEL, ATTN_IN_DIM), D_MODEL),
        'moba_w_out': dense(ks[7], (n_b, ATTN_Q_DIM, D_MODEL), ATTN_Q_DIM),
        'gla_w_in': dense(ks[8], (n_c, D_MODEL, GLA_IN_DIM), D_MODEL),
        'gla_w_decay_up': dense(ks[9], (n_c, GLA_GATE_RANK, GLA_HEADS * GLA_KEY_DIM), GLA_GATE_RANK),
        'gla_b_decay': 0.1 * normal(ks[10], (n_c, GLA_HEADS * GLA_KEY_DIM)),
        'gla_out_norm': gain(ks[11], (n_c, GLA_VAL_DIM)),
        'gla_w_out': dense(ks[12], (n_c, GLA_HEADS * GLA_VAL_DIM, D_MODEL), GLA_HEADS * GLA_VAL_DIM),
        'hgrn_w_in': dense(ks[13], (n_d, D_MODEL, HGRN_IN_DIM), D_MODEL),
        'hgrn_lb_logits': 0.5 * normal(ks[14], (DEPTH, HGRN_HEADS * HGRN_KEY_DIM)),
        'hgrn_out_norm': gain(ks[15], (n_d, HGRN_VAL_DIM)),
        'hgrn_w_out': dense(ks[16], (n_d, HGRN_HEADS * HGRN_VAL_DIM, D_MODEL), HGRN_HEADS * HGRN_VAL_DIM),
        'ffn_w_gate_up': dense(ks[17], (DEPTH, D_MODEL, 2 * D_FF), D_MODEL),
        'ffn_w_down': dense(ks[18], (DEPTH, D_FF, D_MODEL), D_FF),
        'final_norm': gain(ks[19], (D_MODEL,)),
    }

def first_block(x, norm_mix, norm_ffn, swa_w_in, swa_sinks, swa_w_out, moba_w_in, moba_w_out,
              gla_w_in, gla_w_decay_up, gla_b_decay, gla_out_norm, gla_w_out,
              hgrn_w_in, hgrn_lb_logits, hgrn_out_norm, hgrn_w_out,
              ffn_w_gate_up, ffn_w_down, final_norm):
    lb_p = jax.nn.softmax(hgrn_lb_logits.astype(jnp.float32), axis=0)
    lb_table = jnp.cumsum(lb_p, axis=0) - lb_p[0]
    for i in range(DEPTH):
        kind, j = i % N_MIXERS, i // N_MIXERS
        h = rms_norm(x, norm_mix[i])
        if kind == 0:
            mix = sliding_window_sink_attention(h, swa_w_in[j], swa_sinks[j], swa_w_out[j])
        elif kind == 1:
            mix = moba_attention(h, moba_w_in[j], moba_w_out[j])
        elif kind == 2:
            mix = gla_mixer(h, gla_w_in[j], gla_w_decay_up[j], gla_b_decay[j], gla_out_norm[j], gla_w_out[j])
        else:
            mix = hgrn2_mixer(h, hgrn_w_in[j], lb_table[i], hgrn_out_norm[j], hgrn_w_out[j])
        x = x + mix.astype(x.dtype)
        x = x + swiglu_ffn(rms_norm(x, norm_ffn[i]), ffn_w_gate_up[i], ffn_w_down[i]).astype(x.dtype)
    return rms_norm(x, final_norm)


DEPTH_2 = 2

N_EVEN = (DEPTH_2 + 1) // 2
N_ODD = DEPTH_2 // 2

A_WIDTH = D_MODEL // 2
A_HEADS = 4
A_HEAD_DIM = A_WIDTH // A_HEADS
MLSTM_CHUNK = 128
CONV_WIDTH = 5

B_WIDTH = D_MODEL - A_WIDTH
B_GROUPS = 4
B_GROUP_DIM = B_WIDTH // B_GROUPS
SGU_CHUNK = 128

AB_IN = 4 * A_WIDTH + 4 * A_HEADS + 2 * B_WIDTH

C_HEADS = 16
C_NOPE = 64
C_ROPE = 32
C_V = 64
Q_LORA = 384
KV_LORA = 256
C_IN = Q_LORA + KV_LORA + C_ROPE
ROPE_BASE = 10000.0
Q_BLOCK = 128

D_FF_2 = 4 * D_MODEL

EPS = 1e-6


def rms_norm_2(x, g):
    xf = x.astype(jnp.float32)
    y = xf * lax.rsqrt(jnp.mean(xf * xf, axis=-1, keepdims=True) + EPS)
    return (y * g.astype(jnp.float32)).astype(x.dtype)

def centred_dwconv(x, w):
    pad = (w.shape[0] - 1) // 2
    return lax.conv_general_dilated(
        x, w[:, None, :].astype(x.dtype), window_strides=(1,),
        padding=[(pad, pad)], dimension_numbers=("NWC", "WIO", "NWC"),
        feature_group_count=x.shape[-1])

def mlstm_scan(q, k, v, log_i, log_f):
    bsz, nh, seq, dh = q.shape
    L = MLSTM_CHUNK
    nc = seq // L

    def to_chunks(t):
        return jnp.moveaxis(t.reshape(bsz, nh, nc, L, *t.shape[3:]), 2, 0)

    lower = jnp.tril(jnp.ones((L, L), dtype=bool))

    def step(carry, xs):
        C, n, m = carry
        qc, kc, vc, li, lf = xs
        b = jnp.cumsum(lf, axis=-1)
        dmat = jnp.where(lower, b[..., :, None] - b[..., None, :] + li[..., None, :], -jnp.inf)
        m_t = jnp.maximum(b + m[..., None], jnp.max(dmat, axis=-1))
        inter = jnp.exp(b + m[..., None] - m_t)
        s = jnp.einsum("bhtd,bhsd->bhts", qc, kc) * jnp.exp(dmat - m_t[..., None])
        num = (jnp.einsum("bhts,bhse->bhte", s, vc)
               + inter[..., None] * jnp.einsum("bhtd,bhde->bhte", qc, C))
        den = jnp.sum(s, axis=-1) + inter * jnp.einsum("bhtd,bhd->bht", qc, n)
        h = num / jnp.maximum(jnp.abs(den), jnp.exp(-m_t))[..., None]
        g = b[..., -1]
        w_log = g[..., None] - b + li
        m_new = jnp.maximum(g + m, jnp.max(w_log, axis=-1))
        decay = jnp.exp(g + m - m_new)
        w = jnp.exp(w_log - m_new[..., None])
        C_new = decay[..., None, None] * C + jnp.einsum("bhs,bhsd,bhse->bhde", w, kc, vc)
        n_new = decay[..., None] * n + jnp.einsum("bhs,bhsd->bhd", w, kc)
        return (C_new, n_new, m_new), h

    init = (jnp.zeros((bsz, nh, dh, dh), jnp.float32),
            jnp.zeros((bsz, nh, dh), jnp.float32),
            jnp.zeros((bsz, nh), jnp.float32))
    _, h = lax.scan(step, init, (to_chunks(q), to_chunks(k), to_chunks(v),
                                 to_chunks(log_i), to_chunks(log_f)))
    return jnp.moveaxis(h, 0, 2).reshape(bsz, nh, seq, dh)

def ab_mixer(h, w_in, conv_w, gate_b, head_g, v_g, ws, bs, w_out):
    bsz, seq, _ = h.shape
    p = h @ w_in
    qk, va, oa, gates, uv = jnp.split(
        p, [2 * A_WIDTH, 3 * A_WIDTH, 4 * A_WIDTH, 4 * A_WIDTH + 4 * A_HEADS], axis=-1)

    qk = jax.nn.silu(centred_dwconv(qk, conv_w))

    def heads(t):
        return t.reshape(bsz, seq, A_HEADS, A_HEAD_DIM).transpose(0, 2, 1, 3).astype(jnp.float32)

    q = heads(qk[..., :A_WIDTH]) * (A_HEAD_DIM ** -0.5)
    k = heads(qk[..., A_WIDTH:])
    v = heads(va)
    g = (gates + gate_b).astype(jnp.float32).reshape(bsz, seq, 4, A_HEADS).transpose(2, 0, 3, 1)
    li_f, lf_f = g[0], jax.nn.log_sigmoid(g[1])
    li_b, lf_b = g[2], jax.nn.log_sigmoid(g[3])
    h_fwd = mlstm_scan(q, k, v, li_f, lf_f)
    fl = lambda t: jnp.flip(t, axis=2)
    h_bwd = fl(mlstm_scan(fl(q), fl(k), fl(v), jnp.flip(li_b, -1), jnp.flip(lf_b, -1)))
    ha = rms_norm_2(h_fwd + h_bwd, head_g.reshape(A_HEADS, 1, A_HEAD_DIM))
    ha = ha.transpose(0, 2, 1, 3).reshape(bsz, seq, A_WIDTH).astype(h.dtype) * jax.nn.sigmoid(oa)

    u, vb = jnp.split(jax.nn.gelu(uv), 2, axis=-1)
    vb = rms_norm_2(vb.reshape(bsz, seq, B_GROUPS, B_GROUP_DIM), v_g.reshape(B_GROUPS, B_GROUP_DIM))
    vb = vb.reshape(bsz, seq // SGU_CHUNK, SGU_CHUNK, B_GROUPS, B_GROUP_DIM)
    sp = jnp.einsum("gts,bnsgc->bntgc", ws, vb) + bs.T[:, :, None]
    hb = u * sp.reshape(bsz, seq, B_WIDTH)

    return jnp.concatenate([ha, hb], axis=-1) @ w_out

def apply_rope(x, cos, sin):
    half = x.shape[-1] // 2
    x1, x2 = x[..., :half], x[..., half:]
    return jnp.concatenate([x1 * cos - x2 * sin, x1 * sin + x2 * cos], axis=-1).astype(x.dtype)

def mla_mixer(h, positions, w_in, q_g, kv_g, w_uq, w_ukv, w_out):
    bsz, seq, _ = h.shape
    cq, ckv, kr = jnp.split(h @ w_in, [Q_LORA, Q_LORA + KV_LORA], axis=-1)
    q = (rms_norm_2(cq, q_g) @ w_uq).reshape(bsz, seq, C_HEADS, C_NOPE + C_ROPE)
    kv = (rms_norm_2(ckv, kv_g) @ w_ukv).reshape(bsz, seq, C_HEADS, C_NOPE + C_V)

    half = C_ROPE // 2
    freq = ROPE_BASE ** (-jnp.arange(half, dtype=jnp.float32) / half)
    ang = positions.astype(jnp.float32)[..., None] * freq
    cos = jnp.cos(ang)[:, :, None, :]
    sin = jnp.sin(ang)[:, :, None, :]
    q_rope = apply_rope(q[..., C_NOPE:], cos, sin)
    k_rope = apply_rope(kr[:, :, None, :], cos, sin)
    qf = jnp.concatenate([q[..., :C_NOPE], q_rope], axis=-1)
    kf = jnp.concatenate([kv[..., :C_NOPE],
                          jnp.broadcast_to(k_rope, (bsz, seq, C_HEADS, C_ROPE))], axis=-1)
    v = kv[..., C_NOPE:]
    scale = (C_NOPE + C_ROPE) ** -0.5

    qb = jnp.moveaxis(qf.reshape(bsz, seq // Q_BLOCK, Q_BLOCK, C_HEADS, C_NOPE + C_ROPE), 1, 0)

    def attend(qblk):
        s = jnp.einsum("bqhd,bkhd->bhqk", qblk, kf, preferred_element_type=jnp.float32) * scale
        pr = jax.nn.softmax(s, axis=-1)
        return jnp.einsum("bhqk,bkhd->bqhd", pr.astype(v.dtype), v)

    o = lax.map(attend, qb)
    o = jnp.moveaxis(o, 0, 1).reshape(bsz, seq, C_HEADS * C_V)
    return o @ w_out

def second_inputs(seed: int = 0) -> dict:
    key = jax.random.key(seed)
    ks = iter(jax.random.split(key, 40))
    f32 = jnp.float32

    def nrm(shape, scale):
        return jax.random.normal(next(ks), shape, f32) * scale

    def gain(shape):
        return 1.0 + 0.02 * jax.random.normal(next(ks), shape, f32)

    x = jax.random.normal(next(ks), (BATCH, SEQ, D_MODEL), f32)
    offsets = jax.random.randint(next(ks), (BATCH, 1), 0, 1024, dtype=jnp.int32)
    positions = offsets + jnp.arange(SEQ, dtype=jnp.int32)[None, :]

    forget_b = jnp.linspace(3.0, 6.0, A_HEADS, dtype=f32)
    gate_b = jnp.concatenate([
        nrm((N_EVEN, A_HEADS), 0.1),
        forget_b + nrm((N_EVEN, A_HEADS), 0.1),
        nrm((N_EVEN, A_HEADS), 0.1),
        forget_b + nrm((N_EVEN, A_HEADS), 0.1)], axis=-1)

    return {
        "x": x,
        "positions": positions,
        "ab_norm": gain((N_EVEN, D_MODEL)),
        "ab_w_in": nrm((N_EVEN, D_MODEL, AB_IN), D_MODEL ** -0.5),
        "ab_conv": nrm((N_EVEN, CONV_WIDTH, 2 * A_WIDTH), CONV_WIDTH ** -0.5),
        "ab_gate_b": gate_b,
        "ab_head_g": gain((N_EVEN, A_WIDTH)),
        "ab_v_g": gain((N_EVEN, B_WIDTH)),
        "ab_ws": nrm((N_EVEN, B_GROUPS, SGU_CHUNK, SGU_CHUNK), SGU_CHUNK ** -0.5),
        "ab_bs": gain((N_EVEN, B_GROUPS, SGU_CHUNK)),
        "ab_w_out": nrm((N_EVEN, A_WIDTH + B_WIDTH, D_MODEL), (A_WIDTH + B_WIDTH) ** -0.5),
        "c_norm": gain((N_ODD, D_MODEL)),
        "c_w_in": nrm((N_ODD, D_MODEL, C_IN), D_MODEL ** -0.5),
        "c_q_g": gain((N_ODD, Q_LORA)),
        "c_kv_g": gain((N_ODD, KV_LORA)),
        "c_w_uq": nrm((N_ODD, Q_LORA, C_HEADS * (C_NOPE + C_ROPE)), Q_LORA ** -0.5),
        "c_w_ukv": nrm((N_ODD, KV_LORA, C_HEADS * (C_NOPE + C_V)), KV_LORA ** -0.5),
        "c_w_out": nrm((N_ODD, C_HEADS * C_V, D_MODEL), (C_HEADS * C_V) ** -0.5),
        "ffn_norm": gain((DEPTH_2, D_MODEL)),
        "ffn_w1": nrm((DEPTH_2, D_MODEL, D_FF_2), D_MODEL ** -0.5),
        "ffn_w2": nrm((DEPTH_2, D_FF_2, D_MODEL), D_FF_2 ** -0.5),
        "final_norm": gain((D_MODEL,)),
    }

def second_block(x, positions, ab_norm, ab_w_in, ab_conv, ab_gate_b, ab_head_g, ab_v_g,
              ab_ws, ab_bs, ab_w_out, c_norm, c_w_in, c_q_g, c_kv_g, c_w_uq, c_w_ukv,
              c_w_out, ffn_norm, ffn_w1, ffn_w2, final_norm):
    for layer in range(DEPTH_2):
        j = layer // 2
        if layer % 2 == 0:
            x = x + ab_mixer(rms_norm_2(x, ab_norm[j]), ab_w_in[j], ab_conv[j], ab_gate_b[j],
                             ab_head_g[j], ab_v_g[j], ab_ws[j], ab_bs[j], ab_w_out[j])
        else:
            x = x + mla_mixer(rms_norm_2(x, c_norm[j]), positions, c_w_in[j], c_q_g[j],
                              c_kv_g[j], c_w_uq[j], c_w_ukv[j], c_w_out[j])
        hf = rms_norm_2(x, ffn_norm[layer])
        x = x + jnp.square(jax.nn.relu(hf @ ffn_w1[layer])) @ ffn_w2[layer]
    return rms_norm_2(x, final_norm)


def setup_inputs(seed=0):
    out = dict(first_inputs(seed))
    for name, value in second_inputs(seed + 1).items():
        if name != "x":
            out[name + "_2"] = value
    return out


def reference(
    x, norm_mix, norm_ffn, swa_w_in, swa_sinks, swa_w_out, moba_w_in, moba_w_out, gla_w_in,
    gla_w_decay_up, gla_b_decay, gla_out_norm, gla_w_out, hgrn_w_in, hgrn_lb_logits,
    hgrn_out_norm, hgrn_w_out, ffn_w_gate_up, ffn_w_down, final_norm, positions_2, ab_norm_2,
    ab_w_in_2, ab_conv_2, ab_gate_b_2, ab_head_g_2, ab_v_g_2, ab_ws_2, ab_bs_2, ab_w_out_2,
    c_norm_2, c_w_in_2, c_q_g_2, c_kv_g_2, c_w_uq_2, c_w_ukv_2, c_w_out_2, ffn_norm_2, ffn_w1_2,
    ffn_w2_2, final_norm_2,
):
    x = first_block(
        x, norm_mix, norm_ffn, swa_w_in, swa_sinks, swa_w_out, moba_w_in, moba_w_out, gla_w_in,
        gla_w_decay_up, gla_b_decay, gla_out_norm, gla_w_out, hgrn_w_in, hgrn_lb_logits,
        hgrn_out_norm, hgrn_w_out, ffn_w_gate_up, ffn_w_down, final_norm,
    )
    return second_block(
        x, positions_2, ab_norm_2, ab_w_in_2, ab_conv_2, ab_gate_b_2, ab_head_g_2, ab_v_g_2,
        ab_ws_2, ab_bs_2, ab_w_out_2, c_norm_2, c_w_in_2, c_q_g_2, c_kv_g_2, c_w_uq_2,
        c_w_ukv_2, c_w_out_2, ffn_norm_2, ffn_w1_2, ffn_w2_2, final_norm_2,
    )


_drawn_inputs = setup_inputs


def setup_inputs(seed=0):
    import zlib

    import numpy as np

    out = dict(_drawn_inputs(seed))
    spreads = {}
    factors = {'norm_mix': 3.932,
     'norm_ffn': 3.049,
     'ab_norm_2': 3.131,
     'ab_head_g_2': 8.0,
     'ab_v_g_2': 6.694,
     'ab_bs_2': 6.406,
     'c_norm_2': 8.0,
     'c_q_g_2': 8.0,
     'c_kv_g_2': 8.0,
     'ffn_norm_2': 2.67,
     'final_norm_2': 2.84}
    for name, (base, spread) in spreads.items():
        noise = np.random.default_rng([zlib.crc32(name.encode()), seed]).standard_normal(out[name].shape)
        drawn = base * np.exp(spread * noise) if base else spread * noise
        out[name] = __import__('jax').numpy.asarray(drawn.astype(out[name].dtype))
    for name, factor in factors.items():
        out[name] = (out[name] * factor).astype(out[name].dtype)
    return out
```

```python
import math
from contextlib import ExitStack

import concourse.bass as bass
from concourse import mybir

F32 = mybir.dt.float32
F32R = mybir.dt.float32r
I32 = mybir.dt.int32
ALU = mybir.AluOpType
ACT = mybir.ActivationFunctionType
AX = mybir.AxisListType.X

P = 128
SEQ = 256
NT = SEQ // P
DM = 1024
KT = DM // P
EPS = 1e-6
NQH, NKV, HD = 16, 4, 64
SWA_COLS = P + 2 * P
BIG = 3.0e38
FF1 = 2816
FF2 = 4096
CW = 256
N1 = FF1 // CW
N2 = FF2 // CW
AH, AD = 4, 128
AW = AH * AD
BG = 4
CONV = 5
CH, CN, CR, CV = 16, 64, 32, 64
CD = CN + CR
QL, KVL = 384, 256
CIN = QL + KVL + CR
CKT = (QL + KVL) // P
HALF = CR // 2
ROPE_BASE = 10000.0
SLOTS = 4
SLOT = 2048


class Chunk:

    def __init__(self, index, slot, use, prev, shape):
        self.index, self.slot, self.use, self.prev, self.shape = index, slot, use, prev, shape


def weight_schedule():
    uses = {s: [] for s in range(SLOTS)}
    count = [0]
    last = [SLOTS - 1]
    sched = {}

    def add(phase, shape, slot=None):
        if slot is None:
            slot = (last[0] + 1) % SLOTS
        last[0] = slot
        c = count[0]
        count[0] += 1
        prev = uses[slot][-1] if uses[slot] else None
        sched.setdefault(phase, []).append(Chunk(c, slot, len(uses[slot]), prev, shape))
        uses[slot].append(c)

    for _ in range(6):
        add("swa_in", (KT, CW))
    for _ in range(4):
        add("swa_out", (2, DM))
    first = last[0] + 2
    up, gate, down = [(first + 1) % SLOTS, (first - 1) % SLOTS, first % SLOTS]
    add("ffn1", (KT, CW), down)
    add("ffn1", (KT, CW), up)
    for _ in range(N1 - 1):
        add("ffn1", (KT, CW), gate)
        add("ffn1", (2, DM), down)
        add("ffn1", (KT, CW), up)
    add("ffn1", (2, DM), down)
    add("ab_in", (KT, 16))
    for _ in range(12):
        add("ab_in", (KT, CW))
    for _ in range(4):
        add("ab_out", (2, DM))

    def squared_relu(phase):
        add(phase, (KT, CW))
        add(phase, (KT, CW))
        for _ in range(N2 - 2):
            add(phase, (2, DM))
            add(phase, (KT, CW))
        add(phase, (2, DM))
        add(phase, (2, DM))

    squared_relu("ffn2a")
    for n in (CW, CW, CIN - 2 * CW):
        add("c_in", (KT, n))
    for _ in range(3):
        add("c_uq", (QL // P, 512))
    for _ in range(2):
        add("c_ukv", (KVL // P, DM))
    for _ in range(4):
        add("c_out", (2, DM))
    squared_relu("ffn2b")
    return sched, count[0]


def build(nc, t_in, out):
    sched, n_chunks = weight_schedule()
    order = [c for phase in sched.values() for c in phase]
    ctx = ExitStack()
    with ctx:
        def sb(name, shape, dt=F32):
            return ctx.enter_context(nc.sbuf_tensor(name, shape, dt))

        w_raw = [sb(f"w_raw{s}", [P, SLOT]) for s in range(SLOTS)]
        w_hi = [sb(f"w_hi{s}", [P, SLOT], F32R) for s in range(SLOTS)]
        w_lo = [sb(f"w_lo{s}", [P, SLOT], F32R) for s in range(SLOTS)]

        def view(ring, ch):
            k, n = ch.shape
            return ring[ch.slot][:, 0:k * n].rearrange("p (k n) -> p k n", k=k)

        x_res = sb("x_res", [P, NT, DM])
        x_norm = sb("x_norm", [P, NT, DM])
        xT_hi = sb("xT_hi", [P, NT, KT, P], F32R)
        xT_lo = sb("xT_lo", [P, NT, KT, P], F32R)
        gain = sb("gain", [P, 2, DM])
        ssq = sb("ssq", [P, NT])
        mean_sq = sb("mean_sq", [P, NT])
        rstd = sb("rstd", [P, NT])
        minus_half = sb("minus_half", [P, 16])
        ident = sb("ident", [P, P])
        sel = sb("sel", [AH, AH, P])
        one = sb("one", [AH, 1])
        dist = sb("dist", [P, SWA_COLS])
        sinks = sb("sinks", [P, NQH])
        pcols = sb("pcols", [P, 48])
        gate_b = sb("gate_b", [16, 1])
        wsT = sb("wsT", [P, BG, P])
        bs_all = sb("bs_all", [P, BG, P])
        pos_i = sb("pos_i", [P, NT], I32)
        pos_f = sb("pos_f", [P, NT])
        freq = sb("freq", [P, HALF])
        ang = sb("ang", [P, NT, HALF])
        turns = sb("turns", [P, NT, HALF])
        cosr = sb("cosr", [P, NT, HALF])
        cos = sb("cos", [P, NT, HALF])
        sin = sb("sin", [P, NT, HALF])
        ff_hi = [sb(f"ff_hi{i}", [P, 2, SEQ], F32R) for i in range(2)]
        ff_lo = [sb(f"ff_lo{i}", [P, 2, SEQ], F32R) for i in range(2)]

        ARENA = 13700
        arena = sb("arena", [P, ARENA])
        used = [0]

        def take(parts, *shape):
            n = math.prod(shape)
            a = arena[0:parts, used[0]:used[0] + n]
            used[0] += n
            assert used[0] <= ARENA, used[0]
            if len(shape) == 1:
                return a
            names = "abcd"[:len(shape)]
            return a.rearrange(f"p ({' '.join(names)}) -> p {' '.join(names)}",
                               **{names[i]: shape[i] for i in range(len(shape))})

        ff_act = take(P, 2, SEQ)
        ff_h = take(P, 2, SEQ)
        used[0] = 0
        prows = take(48, P)
        ws = take(P, BG, P)
        swa_qT = take(P, 8, SEQ)
        swa_kT = take(P, NKV, SEQ)
        swa_v = take(P, NT, NKV * HD)
        swa_s = take(P, 2, 4, SWA_COLS)
        swa_pT = take(P, 2, 12, P)
        swa_mx = take(P, NT, NQH)
        swa_m = take(P, NT, NQH)
        swa_nm = take(P, NT, NQH)
        swa_sum = take(P, NT, NQH)
        swa_sk = take(P, NT, NQH)
        swa_den = take(P, NT, NQH)
        swa_rden = take(P, NT, NQH)
        used[0] = 0
        PADW = SEQ + CONV - 1
        ab_pad = take(P, 8, PADW)
        ab_cv = take(P, 8, SEQ)
        ab_v1 = take(P, NT, AH, AD + 1)
        ab_u = take(P, BG, SEQ)
        ab_vb = take(P, NT, BG * P)
        ab_sig = take(P, AH, SEQ)
        ab_e = take(P, 2, 2, SWA_COLS)
        num_at = used[0]
        ab_num = take(P, 2, AH, NT, AD + 1)
        ab_sq = take(P, NT * BG, P)
        ab_ss = take(P, 8)
        ab_ms = take(P, 8)
        ab_rs = take(P, 8)
        ab_t = take(P, NT, 4, AH)
        ab_em = take(P, 2, NT, AH)
        ab_rd = take(P, 2, AH, NT)
        ab_dd = take(P, 2, AH, NT)
        used[0] = num_at
        g_raw = take(16, SEQ)
        g_w = take(AH, 2, SEQ)
        g_B = take(AH, 2, SEQ)
        g_M = take(AH, 2, SEQ)
        g4 = x_norm[0:AH, 0, :].rearrange("p (k t) -> p k t", k=4)
        g_am = x_norm[0:AH, 1, :].rearrange("p (k t) -> p k t", k=4)
        g_nM = x_norm[0:AH, 0, 0:2 * SEQ].rearrange("p (d t) -> p d t", d=2)
        used[0] = 0
        c_lat = take(P, NT, CIN)
        c_q = take(P, NT, CH * CD)
        c_k = take(P, NT, CH * CD)
        c_v = take(P, NT, CH * CV)
        c_qkT = take(P, 2, 4, P)
        c_p = take(P, 2, NT, SEQ)
        c_pT = take(P, 2, 4, P)
        c_tmp = c_p.rearrange("p a b c -> p (a b c)").rearrange("p (i n) -> p i n", i=4)
        c_gain = take(P, QL + KVL)
        c_kr = take(P, NT, CR)
        c_krt = take(P, 4, NT, HALF)
        c_ss = take(P, NT, 2)
        c_ms = take(P, NT, 2)
        c_rs = take(P, NT, 2)
        c_mx = take(P, CH, NT)
        c_nm = take(P, CH, NT)
        c_sum = take(P, NT, CH)
        c_rden = take(P, NT, CH)

        bank = [ctx.enter_context(nc.psum_tensor(f"bank{i}", [P, 512], F32)) for i in range(8)]

        S = {n: ctx.enter_context(nc.semaphore(n)) for n in (
            "hi_done lo_done mm_done acc0_done x_loaded sinks_loaded small_loaded ws_loaded pos_loaded "
            "gain_loaded cgain_loaded consts_ready dist_step "
            "resid_ready ssq_ready rstd_step rstd_ready xn_ready t_psum xTh_ready xTl_ready "
            "params_psum params_ready wsT_psum wsT_ready rope_angle rope_ready "
            "act_chain dve_chain pool_chain "
            "ff1_sg ff1_h ff1_hi ff1_lo ff2_relu ff2_h ff2_hi ff2_lo "
            "swa_q_ready swa_k_ready swa_v_ready swa_scores swa_biased swa_nmax swa_probs swa_pt_psum "
            "swa_pt_ready swa_o_psum swa_sinkdiff swa_sinkexp swa_o_ready "
            "g_raw_ready g4_loaded g_abs_ready g_ln_ready g_rows_ready g_cols_psum g_cols_ready g_em_ready "
            "qk_padded conv_ready qk_ready v1_ready u_ready vb_ready sig_ready "
            "vb_sumsq vb_rstd vn_ready sp_psum nM_psum e_exp e_ready st_psum w_ready num_psum num_ready "
            "h_sumsq h_rstd hn_ready hT_psum ab_full ab_hi ab_lo pads_ready "
            "c_lat_ready c_ssq c_rstd c_cn_ready c_t_psum c_xh c_xl c_q_ready c_q1_ready c_kv_ready c_rope_ready "
            "c_qkT_psum c_qkT_ready c_scores c_nmax c_probs c_pt_psum c_pt_ready c_o_psum c_o_ready "
            "out_stored"
        ).split()}
        loaded = [ctx.enter_context(nc.semaphore(f"slot{s}_loaded")) for s in range(SLOTS)]
        block = ctx.enter_context(nc.Block())

        ffn_phases = ("ffn2a", "ffn2b")
        ab_slot = (4, 5, 6, 7, 0, 1, 2, 3)
        phase_of_norm = {1: "swa_out", 2: "ffn1", 4: "ab_out", 5: "ffn2a", 6: "c_out", 7: "ffn2b"}
        additions = {n: i for i, n in enumerate(phase_of_norm)}

        def kv_parts(i, n, t):
            src = bank[(2 + 4 * i + 2 * n + t) % 8][:].rearrange("p (h e) -> p h e", e=CN + CV)
            h0 = 8 * i + 4 * n
            k = c_k[:, t, h0 * CD:(h0 + 4) * CD].rearrange("p (h e) -> p h e", e=CD)
            v = c_v[:, t, h0 * CV:(h0 + 4) * CV].rearrange("p (h e) -> p h e", e=CV)
            return (src[:, :, 0:CN], k[:, :, 0:CN]), (src[:, :, CN:CN + CV], v)

        @block.sync
        def _(sp):
            sp.dma_start(x_res[:], t_in["x"][0].rearrange("(t p) d -> p t d", p=P)).then_inc(S["x_loaded"], 16)

            def load(ch, src, it=0, stride=0):
                if ch.prev is not None:
                    sp.wait_ge(S["lo_done"], ch.prev + 1 + it * stride)
                sp.dma_start(view(w_raw, ch), src).then_inc(loaded[ch.slot], 16)

            def cols(w, at, n):
                return w.rearrange("(k p) c -> p k c", p=P)[:, :, at:at + n]

            def by_cols(w):
                return w.rearrange("(k p) (i c) -> p k i c", p=P, c=CW)

            def by_rows(w):
                return w.rearrange("(i k p) c -> p i k c", p=P, k=2)

            w = t_in["swa_w_in"][0]
            for i, ch in enumerate(sched["swa_in"]):
                load(ch, cols(w, i * CW, CW))
            w = by_rows(t_in["swa_w_out"][0])
            for i, ch in enumerate(sched["swa_out"]):
                load(ch, w[:, i])
            gu, dn = by_cols(t_in["ffn_w_gate_up"][0]), by_rows(t_in["ffn_w_down"][0])
            c = sched["ffn1"]
            load(c[0], gu[:, :, 0])
            load(c[1], gu[:, :, N1])
            load(c[2], gu[:, :, 1])
            load(c[3], dn[:, 0])
            load(c[4], gu[:, :, N1 + 1])
            with sp.Fori(0, N1 - 2) as it:
                load(c[5], gu[:, :, it + 2], it, 3)
                load(c[6], dn[:, it + 1], it, 3)
                load(c[7], gu[:, :, it + (N1 + 2)], it, 3)
            load(c[-1], dn[:, N1 - 1])

            w = t_in["ab_w_in_2"][0]
            at = [4 * AW] + [i * CW for i in range(6)] + [4 * AW + 16 + i * CW for i in range(4)] + [3 * AW, 3 * AW + CW]
            for a, ch in zip(at, sched["ab_in"]):
                load(ch, cols(w, a, ch.shape[1]))
            w = by_rows(t_in["ab_w_out_2"][0])
            for i, ch in enumerate(sched["ab_out"]):
                load(ch, w[:, i])

            def squared_relu(layer):
                c = sched[ffn_phases[layer]]
                w1, w2 = by_cols(t_in["ffn_w1_2"][layer]), by_rows(t_in["ffn_w2_2"][layer])
                load(c[0], w1[:, :, 0])
                load(c[1], w1[:, :, 1])
                with sp.Fori(0, N2 // 2 - 1) as it:
                    load(c[2], w2[:, 2 * it], it, 4)
                    load(c[3], w1[:, :, 2 * it + 2], it, 4)
                    load(c[4], w2[:, 2 * it + 1], it, 4)
                    load(c[5], w1[:, :, 2 * it + 3], it, 4)
                load(c[-2], w2[:, N2 - 2])
                load(c[-1], w2[:, N2 - 1])

            squared_relu(0)
            w = t_in["c_w_in_2"][0]
            for i, ch in enumerate(sched["c_in"]):
                load(ch, cols(w, i * CW, ch.shape[1]))
            for i, ch in enumerate(sched["c_uq"]):
                load(ch, cols(t_in["c_w_uq_2"][0], i * 512, 512))
            for i, ch in enumerate(sched["c_ukv"]):
                load(ch, cols(t_in["c_w_ukv_2"][0], i * DM, DM))
            w = by_rows(t_in["c_w_out_2"][0])
            for i, ch in enumerate(sched["c_out"]):
                load(ch, w[:, i])
            squared_relu(1)
            o = out[0].rearrange("(t p) d -> p t d", p=P)
            for t in range(NT):
                sp.wait_ge(S["xn_ready"], 2 * 7 + t + 1)
                sp.dma_start(o[:, t], x_norm[:, t]).then_inc(S["out_stored"], 16)
            sp.wait_ge(S["out_stored"], 16 * NT)

        norm_gain = [t_in["norm_mix"][0], t_in["norm_ffn"][0], t_in["final_norm"], t_in["ab_norm_2"][0],
                     t_in["ffn_norm_2"][0], t_in["c_norm_2"][0], t_in["ffn_norm_2"][1], t_in["final_norm_2"]]

        @block.gpsimd
        def _(pool):
            chain = [0]

            def step(ins):
                chain[0] += 1
                ins.then_inc(S["pool_chain"], 1)
                pool.wait_ge(S["pool_chain"], chain[0])

            def load_gain(n):
                src = norm_gain[n].rearrange("(a d) -> a d", a=1).broadcast_to([P, DM])
                pool.dma_start(gain[:, n % 2], src).then_inc(S["gain_loaded"], 16)

            pool.memset(minus_half[:], -0.5)
            load_gain(0)
            step(pool.memset(ident[:], 0.0))
            pool.affine_select(out=ident[:], in_=ident[:], compare_op=ALU.not_equal, fill=1.0, base=0,
                               pattern=[[-1, P]], channel_multiplier=1).then_inc(S["consts_ready"], 1)
            pool.wait_ge(S["gain_loaded"], 16)
            load_gain(1)
            step(pool.memset(sel[:], 0.0))
            pool.affine_select(out=sel[:], in_=sel[:], compare_op=ALU.not_equal, fill=1.0, base=0,
                               pattern=[[-1, AH], [0, P]], channel_multiplier=1).then_inc(S["consts_ready"], 1)
            pool.memset(one[:], 1.0)
            for i in range(HALF):
                last = pool.memset(freq[:, i:i + 1], float(ROPE_BASE ** (-i / HALF)))
            last.then_inc(S["consts_ready"], 1)

            def norm(n):
                for t in range(NT):
                    pool.wait_ge(S["ssq_ready"], 2 * n + t + 1)
                    step(pool.tensor_scalar(mean_sq[:, t:t + 1], ssq[:, t:t + 1], 1.0 / DM, EPS, ALU.mult, ALU.add))
                    pool.tensor_tensor(rstd[:, t:t + 1], mean_sq[:, t:t + 1], minus_half[:, 0:1],
                                       ALU.pow).then_inc(S["rstd_ready"], 1)
                if n + 2 < len(norm_gain):
                    pool.wait_ge(S["xn_ready"], 2 * (n + 1))
                    pool.wait_ge(S["gain_loaded"], 16 * (n + 2))
                    load_gain(n + 2)

            step(pool.iota(dist[:, 0:P], pattern=[[-1, P]], base=0, channel_multiplier=1,
                           allow_small_or_imprecise_dtypes=True))
            step(pool.iota(dist[:, P:3 * P], pattern=[[-1, 2 * P]], base=P, channel_multiplier=1,
                           allow_small_or_imprecise_dtypes=True))
            for at, sign, op in ((0, -1, ALU.is_ge), (P, 1, ALU.is_gt), (2 * P, -1, ALU.is_ge)):
                d = dist[:, at:at + P]
                ins = pool.affine_select(out=d, in_=d, compare_op=op, fill=BIG, base=0,
                                         pattern=[[sign, P]], channel_multiplier=-sign)
                ins.then_inc(S["dist_step"], 1)
            norm(0)
            norm(1)
            norm(2)
            norm(3)
            pool.memset(ab_pad[:, :, 0:2], 0.0)
            pool.memset(ab_pad[:, :, 2 + SEQ:PADW], 0.0)
            pool.memset(ab_v1[:, :, :, AD:AD + 1], 1.0).then_inc(S["pads_ready"], 1)
            def masks(h):
                pool.wait_ge(S["e_exp"], 4 * (h + 1))
                for d, at, sign in ((0, 0, 1), (0, 2 * P, 1), (1, 0, -1), (1, 2 * P, -1)):
                    e = ab_e[:, h % 2, d, at:at + P]
                    last = pool.affine_select(out=e, in_=e, compare_op=ALU.is_ge, fill=0.0, base=0,
                                              pattern=[[sign, P]], channel_multiplier=-sign)
                    last.then_inc(S["e_ready"], 1)

            def group_rstd(sumsq, ready):
                pool.wait_ge(S[sumsq], 1)
                step(pool.tensor_scalar(ab_ms, ab_ss, 1.0 / P, EPS, ALU.mult, ALU.add))
                pool.tensor_tensor(ab_rs, ab_ms, minus_half[:, 0:8], ALU.pow).then_inc(S[ready], 1)

            group_rstd("vb_sumsq", "vb_rstd")
            for h in range(AH):
                masks(h)
            pool.wait_ge(S["vn_ready"], 1)
            group_rstd("h_sumsq", "h_rstd")
            norm(4)
            pool.dma_start(c_gain[:, 0:QL], t_in["c_q_g_2"].broadcast_to([P, QL])).then_inc(S["cgain_loaded"], 16)
            pool.dma_start(c_gain[:, QL:QL + KVL], t_in["c_kv_g_2"].broadcast_to([P, KVL])).then_inc(S["cgain_loaded"], 16)
            norm(5)
            pool.wait_ge(S["c_ssq"], 4)
            for j, n in ((0, QL), (1, KVL)):
                step(pool.tensor_scalar(c_ms[:, :, j], c_ss[:, :, j], 1.0 / n, EPS, ALU.mult, ALU.add))
            pool.tensor_tensor(c_rs.rearrange("p a b -> p (a b)"), c_ms.rearrange("p a b -> p (a b)"),
                               minus_half[:, 0:4], ALU.pow).then_inc(S["c_rstd"], 1)
            norm(6)
            norm(7)

        @block.scalar
        def _(act):
            chain = [0]

            def step(ins):
                chain[0] += 1
                ins.then_inc(S["act_chain"], 1)
                act.wait_ge(S["act_chain"], chain[0])

            split = [0]

            def high(ch, it=0, stride=0):
                act.wait_ge(loaded[ch.slot], 16 * (ch.use + 1) + it * (16 if stride else 0))
                if ch.prev is not None:
                    act.wait_ge(S["mm_done"], ch.prev + 1 + it * stride)
                act.activation(view(w_hi, ch), view(w_raw, ch), ACT.Copy).then_inc(S["hi_done"], 1)

            def high_upto(index):
                while split[0] < min(index, n_chunks):
                    high(order[split[0]])
                    split[0] += 1

            act.dma_start(pos_i[:], t_in["positions_2"][0].rearrange("(t p) -> p t", p=P),
                          allow_slow_non_contiguous=True).then_inc(S["pos_loaded"], 16)
            act.dma_start(sinks[:], t_in["swa_sinks"].broadcast_to([P, NQH])).then_inc(S["sinks_loaded"], 16)
            act.dma_start(prows[0:40, :], t_in["ab_conv_2"][0].rearrange("j (f c) -> (j f) c", c=P)).then_inc(S["small_loaded"], 16)
            act.dma_start(prows[40:44, :], t_in["ab_head_g_2"][0].rearrange("(f c) -> f c", c=P)).then_inc(S["small_loaded"], 16)
            act.dma_start(prows[44:48, :], t_in["ab_v_g_2"][0].rearrange("(f c) -> f c", c=P)).then_inc(S["small_loaded"], 16)
            act.dma_start(gate_b[:], t_in["ab_gate_b_2"][0].rearrange("(a b) -> a b", b=1),
                          allow_slow_non_contiguous=True).then_inc(S["small_loaded"], 16)
            act.dma_start(ws[:], t_in["ab_ws_2"][0].rearrange("g t s -> t g s")).then_inc(S["ws_loaded"], 16)
            act.dma_start(bs_all[:],
                          t_in["ab_bs_2"].broadcast_to([P, BG, P])).then_inc(S["ws_loaded"], 16)
            high_upto(1)

            def sum_squares(n):
                for t in range(NT):
                    if n == 0:
                        act.wait_ge(S["x_loaded"], 16)
                    elif n == 3:
                        act.wait_ge(S["xn_ready"], 2 * 2 + t + 1)
                    else:
                        act.wait_ge(S["resid_ready"], 2 * additions[n] + t + 1)
                    if n or t:
                        act.wait_ge(S["ssq_ready"], 2 * n + t)
                    act.activation(x_norm[:, t], x_res[:, t], ACT.Square, accum_out=ssq[:, t:t + 1]).then_inc(S["ssq_ready"], 1)

            def transposed_high(n):
                for t in range(NT):
                    for half in range(2):
                        act.wait_ge(S["t_psum"], 4 * n + 2 * t + half + 1)
                        act.activation(xT_hi[:, t, 4 * half:4 * half + 4, :].rearrange("p k c -> p (k c)"),
                                       bank[2 * t + half][:], ACT.Copy).then_inc(S["xTh_ready"], 1)

            sum_squares(0)
            act.wait_ge(S["rope_angle"], 1)
            act.activation(sin[:], ang[:], ACT.Sin)
            act.activation(cos[:], cosr[:], ACT.Sin).then_inc(S["rope_ready"], 1)
            high_upto(3)
            transposed_high(0)
            high_upto(4)

            c = sched["swa_in"]
            for i in range(4):
                act.wait_ge(S["mm_done"], c[i].index + 1)
                act.activation(swa_qT[:, 2 * i:2 * i + 2, :].rearrange("p a b -> p (a b)"), bank[4 + i][:],
                               ACT.Copy, scale=HD ** -0.5).then_inc(S["swa_q_ready"], 1)
                high_upto(c[i].index + 1 + SLOTS)
            act.wait_ge(S["mm_done"], c[5].index + 1)
            act.activation(swa_v.rearrange("p a b -> p (a b)"), bank[1][:], ACT.Copy).then_inc(S["swa_v_ready"], 1)
            high_upto(c[5].index + 1 + SLOTS)

            def swa_probabilities(g):
                act.wait_ge(S["swa_nmax"], g + 1)
                for j in range(4):
                    h = 4 * g + j
                    for t, a, b in ((0, 0, P), (1, P, SWA_COLS)):
                        s = swa_s[:, g % 2, j, a:b]
                        act.activation(s, s, ACT.Exp, bias=swa_nm[:, t, h:h + 1],
                                       accum_out=swa_sum[:, t, h:h + 1]).then_inc(S["swa_probs"], 1)

            def swa_transposed(g):
                for u in range(3):
                    act.wait_ge(S["swa_pt_psum"], 3 * g + u + 1)
                    if g >= 2 and u == 0:
                        act.wait_ge(S["swa_o_psum"], g - 1)
                    act.activation(swa_pT[:, g % 2, 4 * u:4 * u + 4, :].rearrange("p a b -> p (a b)"),
                                   bank[(3 * g + u) % 2][:], ACT.Copy).then_inc(S["swa_pt_ready"], 1)

            def sink_exp(half):
                act.wait_ge(S["swa_sinkdiff"], half + 1)
                hs = slice(8 * half, 8 * half + 8)
                act.activation(swa_sk[:, :, hs], swa_sk[:, :, hs], ACT.Exp).then_inc(S["swa_sinkexp"], 1)

            for g in range(5):
                if g < 4:
                    swa_probabilities(g)
                if g >= 1:
                    swa_transposed(g - 1)
                if g == 1:
                    sink_exp(0)
            sink_exp(1)
            transposed_high(1)
            c = sched["swa_out"]
            for ch in c:
                high_upto(ch.index + 1 + (SLOTS if ch is not c[-1] else 3))
            sum_squares(1)
            transposed_high(2)
            c = sched["ffn1"]

            def silu_gate(ch, i, it=0):
                act.wait_ge(S["mm_done"], ch.index + 1 + 3 * it)
                act.activation(ff_act[:], bank[0][:].rearrange("p (a b) -> p a b", a=2),
                               ACT.Silu).then_inc(S["ff1_sg"], 1)

            def hidden_high(i, it=0):
                act.wait_ge(S["ff1_h"], i + 1 + it)
                act.activation(ff_hi[0][:], ff_h[:], ACT.Copy).then_inc(S["ff1_hi"], 1)

            silu_gate(c[0], 0)
            high_upto(c[3].index + 1)
            hidden_high(0)
            high_upto(c[4].index + 1)
            silu_gate(c[2], 1)
            high(c[5])
            high(c[6])
            hidden_high(1)
            high(c[7])
            with act.Fori(0, N1 - 3) as it:
                silu_gate(c[5], 2, it)
                high(c[8], it, 3)
                high(c[9], it, 3)
                hidden_high(2, it)
                high(c[10], it, 3)
            silu_gate(c[-4], N1 - 1)
            high(c[-1])
            hidden_high(N1 - 1)
            split[0] = c[-1].index + 1
            high_upto(c[-1].index + 1 + 2)

            sum_squares(2)
            sum_squares(3)
            transposed_high(3)
            c = sched["ab_in"]
            high_upto(c[0].index + SLOTS)
            act.wait_ge(S["small_loaded"], 64)
            act.wait_ge(S["mm_done"], c[0].index + 1)
            act.activation(g_raw, bank[0][0:16, 0:SEQ], ACT.Identity, bias=gate_b[:]).then_inc(S["g_raw_ready"], 1)
            act.wait_ge(S["g_raw_ready"], 1)
            for k in range(4):
                act.dma_start(g4[:, k, :], g_raw[4 * k:4 * k + 4, :]).then_inc(S["g4_loaded"], 16)
            act.wait_ge(S["pads_ready"], 1)
            high_upto(c[0].index + 1 + SLOTS)
            for i in range(4):
                ch = c[1 + i]
                act.wait_ge(S["mm_done"], ch.index + 1)
                act.activation(ab_pad[:, 2 * i:2 * i + 2, 2:2 + SEQ], bank[1 + i][:].rearrange("p (a b) -> p a b", a=2),
                               ACT.Copy).then_inc(S["qk_padded"], 1)
                high_upto(ch.index + 1 + SLOTS)
            for i in range(2):
                ch = c[5 + i]
                act.wait_ge(S["mm_done"], ch.index + 1)
                for t in range(NT):
                    last = act.activation(ab_v1[:, t, 2 * i:2 * i + 2, 0:AD],
                                          bank[5 + i][:, t * 256:t * 256 + 256].rearrange("p (a b) -> p a b", a=2), ACT.Copy)
                last.then_inc(S["v1_ready"], 1)
                high_upto(ch.index + 1 + SLOTS)
            act.wait_ge(S["conv_ready"], 4)
            act.activation(ab_pad[:, :, 0:SEQ], ab_cv[:], ACT.Silu).then_inc(S["qk_ready"], 1)
            act.wait_ge(S["g_abs_ready"], 1)
            step(act.activation(g_w, g_w, ACT.Exp))
            act.activation(g_w, g_w, ACT.Ln, bias=1.0).then_inc(S["g_ln_ready"], 1)
            for i in range(2):
                ch = c[7 + i]
                act.wait_ge(S["mm_done"], ch.index + 1)
                act.activation(ab_u[:, 2 * i:2 * i + 2, :], bank[(7 + i) % 8][:].rearrange("p (a b) -> p a b", a=2),
                               ACT.Gelu_apprx_tanh).then_inc(S["u_ready"], 1)
                high_upto(ch.index + 1 + SLOTS)
            for i in range(2):
                ch = c[9 + i]
                act.wait_ge(S["mm_done"], ch.index + 1)
                act.activation(ab_vb[:, :, i * CW:(i + 1) * CW], bank[1 + i][:].rearrange("p (a b) -> p a b", a=2),
                               ACT.Gelu_apprx_tanh).then_inc(S["vb_ready"], 1)
                high_upto(ch.index + 1 + SLOTS)
            for i in range(2):
                ch = c[11 + i]
                act.wait_ge(S["mm_done"], ch.index + 1)
                act.activation(ab_sig[:, 2 * i:2 * i + 2, :], bank[3 + i][:].rearrange("p (a b) -> p a b", a=2),
                               ACT.Sigmoid).then_inc(S["sig_ready"], 1)
                high_upto(ch.index + 1 + SLOTS)
            act.wait_ge(S["g_cols_ready"], 1)
            act.activation(ab_em.rearrange("p d t h -> p t d h"), ab_t[:, :, 2:4, :], ACT.Exp, scale=-1.0).then_inc(S["g_em_ready"], 1)

            def decay_weights(h):
                act.wait_ge(S["nM_psum"], h + 1)
                b = bank[h % 2]
                for d, t, src, at in ((0, 0, 0, 0), (0, 1, P, 2 * P), (1, 0, SEQ, 0), (1, 1, SEQ, P)):
                    n = SEQ if (d, t) in ((0, 0), (1, 1)) else P
                    act.activation(ab_e[:, h % 2, d, at:at + n], b[:, src:src + n], ACT.Exp,
                                   bias=ab_t[:, t, d, h:h + 1]).then_inc(S["e_exp"], 1)

            def numerators(h):
                for d in range(2):
                    act.wait_ge(S["num_psum"], 2 * h + d + 1)
                    act.activation(ab_num[:, d, h], bank[4 + (2 * h + d) % 4][:, 0:2 * (AD + 1)].rearrange("p (t v) -> p t v", t=NT),
                                   ACT.Copy).then_inc(S["num_ready"], 1)

            for h in range(AH + 1):
                if h < AH:
                    decay_weights(h)
                if h >= 1:
                    numerators(h - 1)

            def full_high(j):
                act.wait_ge(S["ab_full"], j + 1)
                k = ab_slot[j]
                act.activation(xT_hi[:, :, k, :], ab_cv[:, j, :].rearrange("p (t c) -> p t c", t=NT),
                               ACT.Copy).then_inc(S["ab_hi"], 1)

            for j in range(8):
                full_high(j)
            c = sched["ab_out"]
            for ch in c:
                high_upto(ch.index + 1 + SLOTS)

            def relu_square(f, ch, i, buf, it=0):
                act.wait_ge(S["mm_done"], ch.index + 1 + 4 * it)
                if not (f == 0 and i == 0):
                    act.wait_ge(S["ff2_lo"], N2 * f + i + 2 * it)
                act.activation(ff_act[:], bank[buf][:].rearrange("p (a b) -> p a b", a=2), ACT.Relu).then_inc(S["ff2_relu"], 1)
                act.wait_ge(S["ff2_relu"], N2 * f + i + 1 + 2 * it)
                act.activation(ff_hi[buf][:], ff_act[:], ACT.Square).then_inc(S["ff2_hi"], 1)

            def squared_relu(f, after):
                c = sched[ffn_phases[f]]
                high_upto(c[3].index + 1)
                relu_square(f, c[0], 0, 0)
                high_upto(c[4].index + 1)
                relu_square(f, c[1], 1, 1)
                high_upto(c[5].index + 1)
                with act.Fori(0, N2 // 2 - 2) as it:
                    high(c[6], it, 4)
                    relu_square(f, c[3], 2, 0, it)
                    high(c[7], it, 4)
                    high(c[8], it, 4)
                    relu_square(f, c[5], 3, 1, it)
                    high(c[9], it, 4)
                split[0] = c[-3].index + 1
                high_upto(c[-2].index + 1)
                relu_square(f, c[-5], N2 - 2, 0)
                high_upto(c[-1].index + 2)
                relu_square(f, c[-3], N2 - 1, 1)
                high_upto(c[-1].index + 1 + after)

            sum_squares(4)
            transposed_high(4)
            squared_relu(0, 3)

            sum_squares(5)
            transposed_high(5)
            c = sched["c_in"]
            high_upto(c[0].index + SLOTS)
            high_upto(c[0].index + SLOTS + 1)
            act.wait_ge(S["mm_done"], c[2].index + 1)
            for t in range(NT):
                act.activation(c_lat[:, t, 0:512], bank[4 + 2 * t][:], ACT.Copy).then_inc(S["c_lat_ready"], 1)
                act.activation(c_lat[:, t, 512:CIN], bank[5 + 2 * t][:, 0:CIN - 512], ACT.Copy).then_inc(S["c_lat_ready"], 1)
            act.wait_ge(S["c_lat_ready"], 4)
            for t in range(NT):
                for j, a, b in ((0, 0, QL), (1, QL, QL + KVL)):
                    if j or t:
                        act.wait_ge(S["c_ssq"], 2 * t + j)
                    act.activation(x_norm[:, t, a:b], c_lat[:, t, a:b], ACT.Square, accum_out=c_ss[:, t, j:j + 1]).then_inc(S["c_ssq"], 1)
            high_upto(c[2].index + 1 + SLOTS)
            for t in range(NT):
                for half, n in ((0, 4), (1, 1)):
                    act.wait_ge(S["c_t_psum"], 2 * t + half + 1)
                    act.activation(xT_hi[:, t, 4 * half:4 * half + n, :].rearrange("p k c -> p (k c)"),
                                   bank[2 * t + half][:, 0:n * P], ACT.Copy).then_inc(S["c_xh"], 1)
            c = sched["c_uq"]
            for i, ch in enumerate(c):
                act.wait_ge(S["mm_done"], ch.index + 1)
                t = 0
                act.activation(c_q[:, t, i * 512:(i + 1) * 512], bank[(4 + 2 * i + t) % 8][:], ACT.Copy).then_inc(S["c_q_ready"], 1)
                high_upto(ch.index + 1 + SLOTS)
            c = sched["c_ukv"]
            for i, ch in enumerate(c):
                act.wait_ge(S["mm_done"], ch.index + 1)
                for n in range(2):
                    for src, dst in kv_parts(i, n, 0):
                        last = act.activation(dst, src, ACT.Copy)
                last.then_inc(S["c_kv_ready"], 1)
                high_upto(ch.index + 1 + SLOTS)

            def mla_probabilities(h):
                act.wait_ge(S["c_nmax"], h + 1)
                for t in range(NT):
                    act.activation(c_p[:, h % 2, t], bank[2 + h % 2][:, t * SEQ:(t + 1) * SEQ], ACT.Exp, scale=CD ** -0.5,
                                   bias=c_nm[:, h, t:t + 1], accum_out=c_sum[:, t, h:h + 1]).then_inc(S["c_probs"], 1)

            def mla_transposed_p(h):
                act.wait_ge(S["c_pt_psum"], h + 1)
                act.activation(c_pT[:, h % 2].rearrange("p a b -> p (a b)"), bank[4 + h % 2][:], ACT.Copy).then_inc(S["c_pt_ready"], 1)

            for h in range(CH + 1):
                if h < CH:
                    mla_probabilities(h)
                if h >= 1:
                    mla_transposed_p(h - 1)
            transposed_high(6)
            c = sched["c_out"]
            for ch in c:
                high_upto(ch.index + 1 + SLOTS)
            sum_squares(6)
            transposed_high(7)
            squared_relu(1, 0)
            sum_squares(7)

        @block.vector
        def _(dve):
            chain = [0]

            def step(ins):
                chain[0] += 1
                ins.then_inc(S["dve_chain"], 1)
                dve.wait_ge(S["dve_chain"], chain[0])

            split = [0]

            def low(ch, it=0, stride=0):
                dve.wait_ge(S["hi_done"], ch.index + 1 + it * stride)
                dve.tensor_tensor(view(w_lo, ch), view(w_raw, ch), view(w_hi, ch).bitcast(F32),
                                  ALU.subtract).then_inc(S["lo_done"], 1)

            def low_upto(index):
                while split[0] < min(index, n_chunks):
                    low(order[split[0]])
                    split[0] += 1

            def normalise(n, dst):
                dve.wait_ge(S["gain_loaded"], 16 * (n + 1))
                for t in range(NT):
                    dve.wait_ge(S["rstd_ready"], 2 * n + t + 1)
                    dve.scalar_tensor_tensor(out=dst[:, t], in0=x_res[:, t], scalar=rstd[:, t:t + 1],
                                             in1=gain[:, n % 2], op0=ALU.mult, op1=ALU.mult).then_inc(S["xn_ready"], 1)

            def transposed_low(n):
                for t in range(NT):
                    for half in range(2):
                        dve.wait_ge(S["xTh_ready"], 4 * n + 2 * t + half + 1)
                        k = slice(4 * half, 4 * half + 4)
                        dve.tensor_tensor(xT_lo[:, t, k, :].rearrange("p k c -> p (k c)"), bank[2 * t + half][:],
                                          xT_hi[:, t, k, :].rearrange("p k c -> p (k c)").bitcast(F32),
                                          ALU.subtract).then_inc(S["xTl_ready"], 1)

            def add_residual(n):
                for t in range(NT):
                    if t == 0:
                        dve.wait_ge(S["acc0_done"], additions[n] + 1)
                    else:
                        dve.wait_ge(S["mm_done"], sched[phase_of_norm[n]][-1].index + 1)
                    for j in range(2):
                        xs = x_res[:, t, 512 * j:512 * j + 512]
                        last = dve.tensor_tensor(xs, xs, bank[4 + 2 * t + j][:], ALU.add)
                        if j == 0:
                            step(last)
                    last.then_inc(S["resid_ready"], 1)

            dve.wait_ge(S["pos_loaded"], 16)
            dve.wait_ge(S["consts_ready"], 3)
            step(dve.tensor_copy(pos_f[:], pos_i[:]))
            for t in range(NT):
                step(dve.tensor_scalar(ang[:, t], freq[:], pos_f[:, t:t + 1], None, ALU.mult))
            magic = 1.5 * 2 ** 23
            step(dve.tensor_scalar(turns[:], ang[:], 1.0 / (2 * math.pi), magic, ALU.mult, ALU.add))
            step(dve.tensor_scalar(turns[:], turns[:], -magic, None, ALU.add))
            two_pi = (6.28125, 1.93500518798828125e-3, 3.01992e-7)
            two_pi = (two_pi[0], two_pi[1], 2 * math.pi - two_pi[0] - two_pi[1])
            for part in two_pi:
                step(dve.scalar_tensor_tensor(out=ang[:], in0=turns[:], scalar=-part, in1=ang[:],
                                              op0=ALU.mult, op1=ALU.add))
            limit = 3.141592
            step(dve.tensor_scalar(ang[:], ang[:], limit, -limit, ALU.min, ALU.max))
            step(dve.scalar_tensor_tensor(out=cosr[:], in0=ang[:], scalar=-1.0, in1=ang[:], op0=ALU.mult, op1=ALU.min))
            dve.tensor_scalar(cosr[:], cosr[:], math.pi / 2, None, ALU.add).then_inc(S["rope_angle"], 1)

            normalise(0, x_norm)
            low_upto(1)
            transposed_low(0)
            low_upto(4)
            dve.wait_ge(S["params_psum"], 1)
            dve.tensor_copy(pcols[:], bank[5][:, 0:48]).then_inc(S["params_ready"], 1)
            dve.wait_ge(S["wsT_psum"], 1)
            dve.tensor_copy(wsT[:], bank[6][:].rearrange("p (a b) -> p a b", a=BG)).then_inc(S["wsT_ready"], 1)

            c = sched["swa_in"]
            for i in range(4):
                low_upto(c[i].index + 1 + SLOTS)
            dve.wait_ge(S["mm_done"], c[4].index + 1)
            k_ps = bank[0][:].rearrange("p (f t) -> p f t", f=2)
            k_dst = swa_kT.rearrange("p (f r) t -> p f r t", r=2)
            for half in range(2):
                for dst in range(2):
                    last = dve.tensor_copy(k_dst[64 * dst:64 * dst + 64, :, half, :], k_ps[64 * half:64 * half + 64, :, :])
            last.then_inc(S["swa_k_ready"], 1)
            low_upto(c[5].index + 1 + SLOTS)
            dve.wait_ge(S["dist_step"], 3)
            dve.wait_ge(S["sinks_loaded"], 16)

            def swa_bias(g):
                for j in range(4):
                    h = 4 * g + j
                    dve.wait_ge(S["swa_scores"], h + 1)
                    if g >= 2 and j == 0:
                        dve.wait_ge(S["swa_pt_psum"], 3 * (g - 1))
                    slope = 2.0 ** (-8.0 * (h + 1) / NQH)
                    dve.scalar_tensor_tensor(out=swa_s[:, g % 2, j], in0=dist[:], scalar=-slope,
                                             in1=bank[4 + h % 4][:, 0:SWA_COLS], op0=ALU.mult,
                                             op1=ALU.add).then_inc(S["swa_biased"], 1)
                dve.wait_ge(S["swa_biased"], 4 * g + 4)
                hs = slice(4 * g, 4 * g + 4)
                dve.tensor_reduce(swa_mx[:, 0, hs], swa_s[:, g % 2, :, 0:P], axis=AX, op=ALU.max)
                step(dve.tensor_reduce(swa_mx[:, 1, hs], swa_s[:, g % 2, :, P:SWA_COLS], axis=AX, op=ALU.max))
                for t in range(NT):
                    last = dve.tensor_tensor(swa_m[:, t, hs], swa_mx[:, t, hs], sinks[:, hs], ALU.max)
                step(last)
                dve.tensor_scalar(swa_nm[:, :, hs], swa_m[:, :, hs], -1.0, None, ALU.mult).then_inc(S["swa_nmax"], 1)

            def swa_output(half):
                hs = slice(8 * half, 8 * half + 8)
                dve.wait_ge(S["swa_sinkexp"], half + 1)
                dve.wait_ge(S["swa_probs"], 16 * (half + 1))
                step(dve.tensor_tensor(swa_den[:, :, hs], swa_sum[:, :, hs], swa_sk[:, :, hs], ALU.add))
                step(dve.reciprocal(swa_rden[:, :, hs], swa_den[:, :, hs]))
                dve.wait_ge(S["swa_o_psum"], 2 * half + 2)
                for t in range(NT):
                    r = swa_rden[:, t, hs].unsqueeze(2).broadcast_to([P, 8, HD])
                    dve.tensor_tensor(x_norm[:, t, 512 * half:512 * half + 512].rearrange("p (h d) -> p h d", d=HD),
                                      bank[2 + t][:].rearrange("p (h d) -> p h d", d=HD), r,
                                      ALU.mult).then_inc(S["swa_o_ready"], 1)

            def sink_difference(half):
                hs = slice(8 * half, 8 * half + 8)
                for t in range(NT):
                    last = dve.tensor_tensor(swa_sk[:, t, hs], sinks[:, hs], swa_m[:, t, hs], ALU.subtract)
                last.then_inc(S["swa_sinkdiff"], 1)

            for g in range(4):
                swa_bias(g)
                if g % 2:
                    sink_difference(g // 2)
            swa_output(0)
            swa_output(1)
            transposed_low(1)
            c = sched["swa_out"]
            low_upto(c[-1].index + 1 + 3)
            add_residual(1)
            normalise(1, x_norm)
            transposed_low(2)

            c = sched["ffn1"]

            def hidden(ch, i, it=0):
                dve.wait_ge(S["ff1_sg"], i + 1 + it)
                dve.wait_ge(S["mm_done"], ch.index + 1 + 3 * it)
                dve.tensor_tensor(ff_h[:], ff_act[:], bank[1][:].rearrange("p (a b) -> p a b", a=2),
                                  ALU.mult).then_inc(S["ff1_h"], 1)
                dve.wait_ge(S["ff1_hi"], i + 1 + it)
                dve.tensor_tensor(ff_lo[0][:], ff_h[:], ff_hi[0][:].bitcast(F32), ALU.subtract).then_inc(S["ff1_lo"], 1)

            low_upto(c[3].index + 1)
            hidden(c[1], 0)
            low_upto(c[4].index + 1)
            low(c[5])
            low(c[6])
            hidden(c[4], 1)
            low(c[7])
            with dve.Fori(0, N1 - 3) as it:
                low(c[8], it, 3)
                low(c[9], it, 3)
                hidden(c[7], 2, it)
                low(c[10], it, 3)
            low(c[-1])
            hidden(c[-2], N1 - 1)
            split[0] = c[-1].index + 1
            low_upto(c[-1].index + 1 + 2)
            add_residual(2)

            dve.wait_ge(S["gain_loaded"], 16 * 3)
            for t in range(NT):
                dve.wait_ge(S["rstd_ready"], 2 * 2 + t + 1)
                dve.scalar_tensor_tensor(out=x_res[:, t], in0=x_res[:, t], scalar=rstd[:, t:t + 1],
                                         in1=gain[:, 0], op0=ALU.mult, op1=ALU.mult).then_inc(S["xn_ready"], 1)
            normalise(3, x_norm)
            transposed_low(3)
            c = sched["ab_in"]
            low_upto(c[0].index + SLOTS)
            dve.wait_ge(S["params_ready"], 1)
            low_upto(c[0].index + 1 + SLOTS)

            def conv(i):
                dve.wait_ge(S["qk_padded"], i + 1)
                for j in range(CONV):
                    for f in (2 * i, 2 * i + 1):
                        w = pcols[:, 8 * j + f:8 * j + f + 1]
                        src = ab_pad[:, f, j:j + SEQ]
                        if j == 0:
                            ins = dve.tensor_scalar(ab_cv[:, f], src, w, None, ALU.mult)
                        else:
                            ins = dve.scalar_tensor_tensor(out=ab_cv[:, f], in0=src, scalar=w, in1=ab_cv[:, f],
                                                           op0=ALU.mult, op1=ALU.add)
                    if j < CONV - 1:
                        step(ins)
                    else:
                        ins.then_inc(S["conv_ready"], 1)

            conv(0)
            low_upto(c[1].index + 1 + SLOTS)
            dve.wait_ge(S["g4_loaded"], 64)
            forget = g4[:, 1:4:2, :]
            dve.scalar_tensor_tensor(out=g_w, in0=forget, scalar=-1.0, in1=forget, op0=ALU.mult,
                                     op1=ALU.min).then_inc(S["g_abs_ready"], 1)
            for i in range(1, 4):
                conv(i)
                low_upto(c[1 + i].index + 1 + SLOTS)
            for ch in c[5:7]:
                low_upto(ch.index + 1 + SLOTS)
            dve.wait_ge(S["g_ln_ready"], 1)
            step(dve.scalar_tensor_tensor(out=g_w, in0=g4[:, 1:4:2, :], scalar=0.0, in1=g_w,
                                          op0=ALU.min, op1=ALU.subtract))
            ways = (slice(None), slice(None, None, -1))
            for d, w in enumerate(ways):
                last = dve.tensor_tensor_scan(g_B[:, d, w], one[:].broadcast_to([AH, SEQ]), g_w[:, d, w], 0.0, ALU.mult, ALU.add)
            step(last)
            step(dve.tensor_tensor(g_am[:, 0:2], g4[:, 0:4:2, :], g_B, ALU.subtract))
            for d, w in enumerate(ways):
                last = dve.tensor_tensor_scan(g_M[:, d, w], g_am[:, d, w], g_am[:, d, w], 0.0, ALU.max, ALU.max)
            step(last)
            dve.tensor_tensor(g_am[:, 2:4], g_B, g_M, ALU.add)
            dve.tensor_scalar(g_nM, g_M, -1.0, None, ALU.mult).then_inc(S["g_rows_ready"], 1)
            for ch in c[7:9]:
                low_upto(ch.index + 1 + SLOTS)
            for ch in c[9:11]:
                low_upto(ch.index + 1 + SLOTS)
            dve.wait_ge(S["vb_ready"], 2)
            vb = ab_vb.rearrange("p t (g c) -> p (t g) c", c=P)
            step(dve.tensor_tensor(ab_sq[:], vb, vb, ALU.mult))
            dve.tensor_reduce(ab_ss, ab_sq[:], axis=AX, op=ALU.add).then_inc(S["vb_sumsq"], 1)
            dve.wait_ge(S["g_cols_psum"], 1)
            dve.tensor_copy(ab_t.rearrange("p t k h -> p (t k h)"), bank[7][:, 0:32]).then_inc(S["g_cols_ready"], 1)
            low_upto(c[11].index + 1 + SLOTS)
            dve.wait_ge(S["vb_rstd"], 1)
            dve.tensor_tensor(vb, vb, ab_rs.unsqueeze(2).broadcast_to([P, 8, P]), ALU.mult).then_inc(S["vn_ready"], 1)
            low_upto(c[12].index + 1 + SLOTS)

            def weighted_scores(h):
                dve.wait_ge(S["st_psum"], h + 1)
                dve.wait_ge(S["e_ready"], 4 * (h + 1))
                b = bank[2 + h % 2]
                for d, src, at, n in ((0, 0, 0, SEQ), (0, SEQ + P, 2 * P, P), (1, 0, 0, P), (1, SEQ, P, SEQ)):
                    e = ab_e[:, h % 2, d, at:at + n]
                    last = dve.scalar_tensor_tensor(out=e, in0=b[:, src:src + n], scalar=AD ** -0.5, in1=e,
                                                    op0=ALU.mult, op1=ALU.mult)
                last.then_inc(S["w_ready"], 1)

            for h in range(AH):
                weighted_scores(h)
            for g in range(BG):
                if g == 0:
                    dve.wait_ge(S["sp_psum"], 1)
                    dve.wait_ge(S["u_ready"], 2)
                    dve.wait_ge(S["ws_loaded"], 32)
                    dve.wait_ge(S["qk_ready"], 1)
                sp_out = bank[g // 2][:, (g % 2) * SEQ:(g % 2) * SEQ + SEQ].rearrange("p (n t) -> p n t", n=NT)
                tmp = ab_sq[:, 2 * g:2 * g + 2, :]
                step(dve.scalar_tensor_tensor(out=tmp, in0=sp_out, scalar=pcols[:, 44 + g:45 + g],
                                              in1=bs_all[:, g:g + 1, :].broadcast_to([P, NT, P]),
                                              op0=ALU.mult, op1=ALU.add))
                dve.tensor_tensor(ab_cv[:, g].rearrange("p (n t) -> p n t", n=NT), tmp,
                                  ab_u[:, g].rearrange("p (n t) -> p n t", n=NT), ALU.mult).then_inc(S["ab_full"], 1)

            def full_low(j):
                dve.wait_ge(S["ab_hi"], j + 1)
                k = ab_slot[j]
                dve.tensor_tensor(xT_lo[:, :, k, :], ab_cv[:, j, :].rearrange("p (t c) -> p t c", t=NT),
                                  xT_hi[:, :, k, :].bitcast(F32), ALU.subtract).then_inc(S["ab_lo"], 1)

            dve.wait_ge(S["num_ready"], 8)
            dve.wait_ge(S["g_em_ready"], 1)
            for d in range(2):
                den = ab_num[:, d, :, :, AD]
                step(dve.scalar_tensor_tensor(out=ab_dd[:, d], in0=den, scalar=-1.0, in1=den,
                                              op0=ALU.mult, op1=ALU.max))
                step(dve.tensor_tensor(ab_dd[:, d], ab_dd[:, d], ab_em[:, d].rearrange("p t h -> p h t"), ALU.max))
            step(dve.reciprocal(ab_rd[:], ab_dd[:]))
            for d in range(2):
                n = ab_num[:, d, :, :, 0:AD]
                last = dve.tensor_tensor(n, n, ab_rd[:, d].unsqueeze(3).broadcast_to([P, AH, NT, AD]), ALU.mult)
            step(last)
            hsum = ab_num[:, 0, :, :, 0:AD]
            step(dve.tensor_tensor(hsum, hsum, ab_num[:, 1, :, :, 0:AD], ALU.add))
            sq = ab_sq.rearrange("p (h t) c -> p h t c", t=NT)
            step(dve.tensor_tensor(sq, hsum, hsum, ALU.mult))
            dve.tensor_reduce(ab_ss, ab_sq[:], axis=AX, op=ALU.add).then_inc(S["h_sumsq"], 1)
            for j in range(4):
                full_low(j)
            dve.wait_ge(S["h_rstd"], 1)
            rs = ab_rs.rearrange("p (h t) -> p h t", t=NT).unsqueeze(3).broadcast_to([P, AH, NT, AD])
            dve.tensor_tensor(sq, hsum, rs, ALU.mult).then_inc(S["hn_ready"], 1)
            dve.wait_ge(S["sig_ready"], 2)
            for h in range(AH):
                dve.wait_ge(S["hT_psum"], h // 2 + 1)
                dve.scalar_tensor_tensor(out=ab_cv[:, 4 + h], in0=bank[2 + h // 2][:, (h % 2) * SEQ:(h % 2) * SEQ + SEQ],
                                         scalar=pcols[:, 40 + h:41 + h], in1=ab_sig[:, h],
                                         op0=ALU.mult, op1=ALU.mult).then_inc(S["ab_full"], 1)
            for j in range(4, 8):
                full_low(j)
            c = sched["ab_out"]
            low_upto(c[-1].index + 1 + SLOTS)
            add_residual(4)
            normalise(4, x_norm)
            transposed_low(4)

            def hidden2(f, i, buf, it=0):
                dve.wait_ge(S["ff2_relu"], N2 * f + i + 1 + 2 * it)
                dve.tensor_tensor(ff_h[:], ff_act[:], ff_act[:], ALU.mult).then_inc(S["ff2_h"], 1)
                dve.wait_ge(S["ff2_h"], N2 * f + i + 1 + 2 * it)
                dve.wait_ge(S["ff2_hi"], N2 * f + i + 1 + 2 * it)
                dve.tensor_tensor(ff_lo[buf][:], ff_h[:], ff_hi[buf][:].bitcast(F32), ALU.subtract).then_inc(S["ff2_lo"], 1)

            def squared_relu(f, after):
                c = sched[ffn_phases[f]]
                low_upto(c[3].index + 1)
                hidden2(f, 0, 0)
                low_upto(c[4].index + 1)
                hidden2(f, 1, 1)
                low_upto(c[5].index + 1)
                with dve.Fori(0, N2 // 2 - 2) as it:
                    low(c[6], it, 4)
                    hidden2(f, 2, 0, it)
                    low(c[7], it, 4)
                    low(c[8], it, 4)
                    hidden2(f, 3, 1, it)
                    low(c[9], it, 4)
                split[0] = c[-3].index + 1
                low_upto(c[-2].index + 1)
                hidden2(f, N2 - 2, 0)
                low_upto(c[-1].index + 2)
                hidden2(f, N2 - 1, 1)
                low_upto(c[-1].index + 1 + after)

            squared_relu(0, 3)
            add_residual(5)
            normalise(5, x_norm)
            transposed_low(5)

            c = sched["c_in"]
            low_upto(c[0].index + SLOTS)
            low_upto(c[0].index + SLOTS + 1)
            dve.wait_ge(S["c_lat_ready"], 4)
            for t in range(NT):
                x1, x2 = c_lat[:, t, QL + KVL:QL + KVL + HALF], c_lat[:, t, QL + KVL + HALF:CIN]
                dve.wait_ge(S["rope_ready"], 1)
                dve.tensor_tensor(c_krt[:, 0, t], x1, cos[:, t], ALU.mult)
                dve.tensor_tensor(c_krt[:, 1, t], x2, sin[:, t], ALU.mult)
                dve.tensor_tensor(c_krt[:, 2, t], x1, sin[:, t], ALU.mult)
                step(dve.tensor_tensor(c_krt[:, 3, t], x2, cos[:, t], ALU.mult))
                dve.tensor_tensor(c_kr[:, t, 0:HALF], c_krt[:, 0, t], c_krt[:, 1, t], ALU.subtract)
                step(dve.tensor_tensor(c_kr[:, t, HALF:CR], c_krt[:, 2, t], c_krt[:, 3, t], ALU.add))
                kr_all = c_k[:, t].rearrange("p (h e) -> p h e", e=CD)[:, :, CN:CD]
                step(dve.tensor_copy(kr_all, c_kr[:, t:t + 1, :].broadcast_to([P, CH, CR])))
            dve.wait_ge(S["c_rstd"], 1)
            dve.wait_ge(S["cgain_loaded"], 32)
            for t in range(NT):
                for j, a, b in ((0, 0, QL), (1, QL, QL + KVL)):
                    dve.scalar_tensor_tensor(out=x_norm[:, t, a:b], in0=c_lat[:, t, a:b], scalar=c_rs[:, t, j:j + 1],
                                             in1=c_gain[:, a:b], op0=ALU.mult, op1=ALU.mult).then_inc(S["c_cn_ready"], 1)
            low_upto(c[2].index + 1 + SLOTS)
            for t in range(NT):
                for half, n in ((0, 4), (1, 1)):
                    dve.wait_ge(S["c_xh"], 2 * t + half + 1)
                    k = slice(4 * half, 4 * half + n)
                    dve.tensor_tensor(xT_lo[:, t, k, :].rearrange("p k c -> p (k c)"), bank[2 * t + half][:, 0:n * P],
                                      xT_hi[:, t, k, :].rearrange("p k c -> p (k c)").bitcast(F32),
                                      ALU.subtract).then_inc(S["c_xl"], 1)
            c = sched["c_uq"]
            for i, ch in enumerate(c):
                dve.wait_ge(S["mm_done"], ch.index + 1)
                t = 1
                dve.tensor_copy(c_q[:, t, i * 512:(i + 1) * 512], bank[(4 + 2 * i + t) % 8][:]).then_inc(S["c_q1_ready"], 1)
                low_upto(ch.index + 1 + SLOTS)
            dve.wait_ge(S["c_q_ready"], 3)
            dve.wait_ge(S["c_q1_ready"], 3)

            def rope_q(t):
                q = c_q[:, t].rearrange("p (h e) -> p h e", e=CD)
                x1, x2 = q[:, :, CN:CN + HALF], q[:, :, CN + HALF:CD]
                cs = cos[:, t:t + 1, :].broadcast_to([P, CH, HALF])
                sn = sin[:, t:t + 1, :].broadcast_to([P, CH, HALF])
                tmp = [c_tmp[:, i].rearrange("p (h e) -> p h e", e=HALF) for i in range(4)]
                dve.tensor_tensor(tmp[0], x1, cs, ALU.mult)
                dve.tensor_tensor(tmp[1], x2, sn, ALU.mult)
                dve.tensor_tensor(tmp[2], x1, sn, ALU.mult)
                step(dve.tensor_tensor(tmp[3], x2, cs, ALU.mult))
                dve.tensor_tensor(x1, tmp[0], tmp[1], ALU.subtract)
                ins = dve.tensor_tensor(x2, tmp[2], tmp[3], ALU.add)
                if t == 0:
                    step(ins)
                else:
                    ins.then_inc(S["c_rope_ready"], 1)

            def values(i, ch):
                dve.wait_ge(S["mm_done"], ch.index + 1)
                for n in range(2):
                    for src, dst in kv_parts(i, n, 1):
                        last = dve.tensor_copy(dst, src)
                last.then_inc(S["c_kv_ready"], 1)
                low_upto(ch.index + 1 + SLOTS)

            rope_q(0)
            values(0, sched["c_ukv"][0])
            rope_q(1)
            values(1, sched["c_ukv"][1])

            def mla_qk(h):
                dve.wait_ge(S["c_qkT_psum"], h + 1)
                dve.tensor_copy(c_qkT[0:CD, h % 2].rearrange("p a b -> p (a b)"), bank[h % 2][0:CD, :]).then_inc(S["c_qkT_ready"], 1)

            def mla_max(h):
                dve.wait_ge(S["c_scores"], h + 1)
                step(dve.tensor_reduce(c_mx[:, h], bank[2 + h % 2][:].rearrange("p (t k) -> p t k", t=NT), axis=AX, op=ALU.max))
                dve.tensor_scalar(c_nm[:, h], c_mx[:, h], -(CD ** -0.5), None, ALU.mult).then_inc(S["c_nmax"], 1)

            def mla_output(half):
                dve.wait_ge(S["c_o_psum"], 8 * half + 8)
                hs = slice(8 * half, 8 * half + 8)
                step(dve.reciprocal(c_rden[:, :, hs], c_sum[:, :, hs]))
                for t in range(NT):
                    r = c_rden[:, t, hs].unsqueeze(2).broadcast_to([P, 8, CV])
                    dve.tensor_tensor(x_norm[:, t, 512 * half:512 * half + 512].rearrange("p (h d) -> p h d", d=CV),
                                      bank[6 + t][:].rearrange("p (h d) -> p h d", d=CV), r, ALU.mult).then_inc(S["c_o_ready"], 1)

            for h in range(CH + 1):
                if h < CH:
                    mla_qk(h)
                if h >= 1:
                    mla_max(h - 1)
                if h == 10:
                    mla_output(0)
            mla_output(1)
            transposed_low(6)
            c = sched["c_out"]
            low_upto(c[-1].index + 1 + SLOTS)
            add_residual(6)
            normalise(6, x_norm)
            transposed_low(7)
            squared_relu(1, 0)
            add_residual(7)
            normalise(7, x_norm)

        @block.tensor
        def _(pe):
            def product(out, sh, sl, mh, ml, first, last):
                pe.matmul(out, sh, mh, start=first, stop=False)
                pe.matmul(out, sh, ml, start=False, stop=False)
                return pe.matmul(out, sl, mh, start=False, stop=last)

            def arrived(ch, it=0, stride=0):
                pe.wait_ge(S["lo_done"], ch.index + 1 + it * stride)

            def feature_major(ch, dst):
                hi, lo = view(w_hi, ch), view(w_lo, ch)
                n = ch.shape[1]
                for f in range(max(1, n // P)):
                    w = min(n, P)
                    o = dst[0:w, f * SEQ:(f + 1) * SEQ].rearrange("p (t c) -> p t c", t=NT)
                    for k in range(KT):
                        last = product(o, hi[:, k, f * w:(f + 1) * w], lo[:, k, f * w:(f + 1) * w],
                                       xT_hi[:, :, k, :], xT_lo[:, :, k, :], k == 0, k == KT - 1)
                last.then_inc(S["mm_done"], 1)

            def token_major(ch, dst, kts=KT, k0=0):
                hi, lo = view(w_hi, ch), view(w_lo, ch)
                for t in range(NT):
                    for k in range(kts):
                        last = product(dst[t], xT_hi[:, t, k0 + k, :], xT_lo[:, t, k0 + k, :], hi[:, k, :], lo[:, k, :],
                                       k == 0, k == kts - 1)
                last.then_inc(S["mm_done"], 1)

            def accumulate(ch, stat_hi, stat_lo, first, last_chunk, phase_end):
                hi, lo = view(w_hi, ch), view(w_lo, ch)
                for t in range(NT):
                    for j in range(2):
                        for k in range(2):
                            last = product(bank[4 + 2 * t + j][:], stat_hi(t, k), stat_lo(t, k),
                                           hi[:, k, 512 * j:512 * j + 512], lo[:, k, 512 * j:512 * j + 512],
                                           first and k == 0, last_chunk and k == 1)
                    if t == 0 and phase_end:
                        last.then_inc(S["acc0_done"], 1)
                last.then_inc(S["mm_done"], 1)

            def out_projection(phase):
                for i, ch in enumerate(sched[phase]):
                    arrived(ch)
                    end = i == len(sched[phase]) - 1
                    accumulate(ch, lambda t, k: xT_hi[:, t, 2 * i + k, :], lambda t, k: xT_lo[:, t, 2 * i + k, :],
                               i == 0, end, end)

            def transpose_operand(n, wait):
                for t in range(NT):
                    wait(t)
                    for half in range(2):
                        for k in range(4):
                            kk = 4 * half + k
                            last = pe.transpose(bank[2 * t + half][:, k * P:(k + 1) * P],
                                                x_norm[:, t, kk * P:(kk + 1) * P], ident[:])
                        last.then_inc(S["t_psum"], 1)

            def transpose_norm(n, norm):
                transpose_operand(n, lambda t: pe.wait_ge(S["xn_ready"], 2 * norm + t + 1))
                pe.wait_ge(S["xTl_ready"], 4 * (n + 1))

            pe.wait_ge(S["consts_ready"], 2)
            pe.wait_ge(S["small_loaded"], 64)
            pe.transpose(bank[5][:, 0:48], prows, ident[0:48, 0:48]).then_inc(S["params_psum"], 1)
            pe.wait_ge(S["ws_loaded"], 32)
            for g in range(BG):
                last = pe.transpose(bank[6][:, g * P:(g + 1) * P], ws[:, g, :], ident[:])
            last.then_inc(S["wsT_psum"], 1)

            transpose_norm(0, 0)
            c = sched["swa_in"]
            for i, ch in enumerate(c):
                arrived(ch)
                if i == 1:
                    pe.wait_ge(S["params_ready"], 1)
                if i == 2:
                    pe.wait_ge(S["wsT_ready"], 1)
                if i < 4:
                    feature_major(ch, bank[4 + i])
                elif i == 4:
                    feature_major(ch, bank[0])
                else:
                    token_major(ch, [bank[1][:, t * CW:(t + 1) * CW] for t in range(NT)])
            pe.wait_ge(S["swa_q_ready"], 4)
            pe.wait_ge(S["swa_k_ready"], 1)
            pe.wait_ge(S["swa_v_ready"], 1)

            def swa_scores(g):
                for j in range(4):
                    h = 4 * g + j
                    if h >= 4:
                        pe.wait_ge(S["swa_biased"], h - 3)
                    at = slice(64 * (h % 2), 64 * (h % 2) + 64)
                    b = bank[4 + h % 4]
                    kv = h // (NQH // NKV)
                    pe.matmul(b[:, 0:P], swa_qT[at, h // 2, 0:P], swa_kT[at, kv, 0:P], start=True, stop=True)
                    pe.matmul(b[:, P:SWA_COLS], swa_qT[at, h // 2, P:SEQ], swa_kT[at, kv, :],
                              start=True, stop=True).then_inc(S["swa_scores"], 1)

            def swa_transposes(g):
                pe.wait_ge(S["swa_probs"], 8 * (g + 1))
                for u in range(3):
                    n = 3 * g + u
                    if n >= 2:
                        pe.wait_ge(S["swa_pt_ready"], n - 1)
                    for b in range(4):
                        blk = 4 * u + b
                        j, part = blk // 3, blk % 3
                        last = pe.transpose(bank[n % 2][:, b * P:(b + 1) * P], swa_s[:, g % 2, j, part * P:(part + 1) * P], ident[:])
                    last.then_inc(S["swa_pt_psum"], 1)

            def swa_values(g):
                pe.wait_ge(S["swa_pt_ready"], 3 * (g + 1))
                if g == 2:
                    pe.wait_ge(S["swa_o_ready"], 2)
                for j in range(4):
                    h = 4 * g + j
                    o = slice((h % 8) * HD, (h % 8) * HD + HD)
                    v = [swa_v[:, t, g * HD:(g + 1) * HD] for t in range(NT)]
                    pt = swa_pT[:, g % 2]
                    pe.matmul(bank[2][:, o], pt[:, 3 * j, :], v[0], start=True, stop=True)
                    pe.matmul(bank[3][:, o], pt[:, 3 * j + 1, :], v[0], start=True, stop=False)
                    last = pe.matmul(bank[3][:, o], pt[:, 3 * j + 2, :], v[1], start=False, stop=True)
                last.then_inc(S["swa_o_psum"], 1)

            swa_scores(0)
            for g in range(4):
                if g < 3:
                    swa_scores(g + 1)
                swa_transposes(g)
                if g >= 1:
                    swa_values(g - 1)
            swa_values(3)
            transpose_operand(1, lambda t: pe.wait_ge(S["swa_o_ready"], 4))
            pe.wait_ge(S["xTl_ready"], 8)
            out_projection("swa_out")

            transpose_norm(2, 1)
            c = sched["ffn1"]

            def down(ch, i, it=0, first=False, end=False):
                arrived(ch, it, 3)
                pe.wait_ge(S["ff1_lo"], i + 1 + it)
                accumulate(ch, lambda t, k: ff_hi[0][:, k, t * P:(t + 1) * P], lambda t, k: ff_lo[0][:, k, t * P:(t + 1) * P],
                           first, end, end)

            def gate(ch, i, it=0):
                arrived(ch, it, 3)
                pe.wait_ge(S["ff1_sg"], i + it)
                feature_major(ch, bank[0])

            arrived(c[0])
            feature_major(c[0], bank[0])
            arrived(c[1])
            feature_major(c[1], bank[1])
            gate(c[2], 1)
            down(c[3], 0, first=True)
            arrived(c[4])
            feature_major(c[4], bank[1])
            with pe.Fori(0, N1 - 2) as it:
                gate(c[5], 2, it)
                down(c[6], 1, it)
                arrived(c[7], it, 3)
                feature_major(c[7], bank[1])
            down(c[-1], N1 - 1, end=True)

            transpose_norm(3, 3)
            c = sched["ab_in"]
            for i, ch in enumerate(c):
                arrived(ch)
                if i == 0:
                    feature_major(ch, bank[0])
                elif i < 5:
                    feature_major(ch, bank[i])
                elif i < 7:
                    token_major(ch, [bank[i][:, t * CW:(t + 1) * CW] for t in range(NT)])
                elif i < 9:
                    if i == 8:
                        pe.wait_ge(S["g_raw_ready"], 1)
                    feature_major(ch, bank[i % 8])
                elif i < 11:
                    pe.wait_ge(S["qk_padded"], i - 8)
                    token_major(ch, [bank[i - 8][:, t * CW:(t + 1) * CW] for t in range(NT)])
                else:
                    pe.wait_ge(S["qk_padded"], i - 8)
                    feature_major(ch, bank[i - 8])
                if i == 10:
                    pe.wait_ge(S["g_rows_ready"], 1)
                    pe.wait_ge(S["u_ready"], 1)
                    for t in range(NT):
                        for k in range(4):
                            at = 16 * t + 4 * k
                            last = pe.transpose(bank[7][:, at:at + 4], g_am[:, k, t * P:(t + 1) * P], ident[0:AH, 0:AH])
                    last.then_inc(S["g_cols_psum"], 1)
            pe.wait_ge(S["u_ready"], 2)
            pe.wait_ge(S["vb_ready"], 2)
            pe.wait_ge(S["sig_ready"], 2)
            pe.wait_ge(S["qk_ready"], 1)
            pe.wait_ge(S["v1_ready"], 2)
            pe.wait_ge(S["g_cols_ready"], 1)

            def decay_rows(h):
                if h >= 2:
                    pe.wait_ge(S["e_exp"], 4 * (h - 1))
                pe.matmul(bank[h % 2][:], sel[:, h, :], g_nM.rearrange("p d t -> p (d t)"),
                          start=True, stop=True).then_inc(S["nM_psum"], 1)

            def scores_T(h):
                if h >= 2:
                    pe.wait_ge(S["w_ready"], h - 1)
                b = bank[2 + h % 2]
                q, k = ab_pad[:, h, 0:SEQ], ab_pad[:, AH + h, 0:SEQ]
                pe.matmul(b[:, 0:SEQ], k[:, 0:P], q, start=True, stop=True)
                pe.matmul(b[:, SEQ:2 * SEQ], k[:, P:SEQ], q, start=True, stop=True).then_inc(S["st_psum"], 1)

            def summed(h):
                pe.wait_ge(S["w_ready"], h + 1)
                for d in range(2):
                    n = 2 * h + d
                    if n >= 4:
                        pe.wait_ge(S["num_ready"], n - 3)
                    b = bank[4 + n % 4]
                    w = ab_e[:, h % 2, d]
                    blocks = ((0, ((0, 0),)), (1, ((0, P), (1, 2 * P)))) if d == 0 else ((0, ((0, 0), (1, P))), (1, ((1, 2 * P),)))
                    for t, srcs in blocks:
                        for m, (s, at) in enumerate(srcs):
                            last = pe.matmul(b[:, t * (AD + 1):(t + 1) * (AD + 1)], w[:, at:at + P], ab_v1[:, s, h, :],
                                             start=m == 0, stop=m == len(srcs) - 1)
                    last.then_inc(S["num_psum"], 1)

            decay_rows(0)
            scores_T(0)
            for h in range(AH):
                if h + 1 < AH:
                    decay_rows(h + 1)
                    scores_T(h + 1)
                summed(h)
            pe.wait_ge(S["vn_ready"], 1)
            pe.wait_ge(S["e_exp"], 4 * AH)
            for g in range(BG):
                for n in range(NT):
                    at = (g % 2) * SEQ + n * P
                    last = pe.matmul(bank[g // 2][:, at:at + P], ab_vb[:, n, g * P:(g + 1) * P], wsT[:, g, :], start=True, stop=True)
            last.then_inc(S["sp_psum"], 1)
            pe.wait_ge(S["hn_ready"], 1)
            for h in range(AH):
                for t in range(NT):
                    at = (h % 2) * SEQ + t * P
                    last = pe.transpose(bank[2 + h // 2][:, at:at + P], ab_sq[:, 2 * h + t, :], ident[:])
                if h % 2:
                    last.then_inc(S["hT_psum"], 1)
            pe.wait_ge(S["ab_lo"], 8)
            out_projection("ab_out")

            def up2(ch, buf, it=0):
                arrived(ch, it, 4)
                feature_major(ch, bank[buf])

            def down2(f, ch, i, buf, it=0, first=False, end=False):
                arrived(ch, it, 4)
                pe.wait_ge(S["ff2_lo"], N2 * f + i + 1 + 2 * it)
                accumulate(ch, lambda t, k: ff_hi[buf][:, k, t * P:(t + 1) * P],
                           lambda t, k: ff_lo[buf][:, k, t * P:(t + 1) * P], first, end, end)

            def squared_relu(f):
                c = sched[ffn_phases[f]]
                up2(c[0], 0)
                up2(c[1], 1)
                down2(f, c[2], 0, 0, first=True)
                up2(c[3], 0)
                down2(f, c[4], 1, 1)
                up2(c[5], 1)
                with pe.Fori(0, N2 // 2 - 2) as it:
                    down2(f, c[6], 2, 0, it)
                    up2(c[7], 0, it)
                    down2(f, c[8], 3, 1, it)
                    up2(c[9], 1, it)
                down2(f, c[-2], N2 - 2, 0)
                down2(f, c[-1], N2 - 1, 1, end=True)

            transpose_norm(4, 4)
            squared_relu(0)

            transpose_norm(5, 5)
            c = sched["c_in"]
            for i, ch in enumerate(c):
                arrived(ch)
                n = ch.shape[1]
                token_major(ch, [bank[4 + 2 * t + i // 2][:, (i % 2) * CW:(i % 2) * CW + n] for t in range(NT)])
            for t in range(NT):
                pe.wait_ge(S["c_cn_ready"], 2 * t + 2)
                for half, n in ((0, 4), (1, 1)):
                    for k in range(n):
                        kk = 4 * half + k
                        last = pe.transpose(bank[2 * t + half][:, k * P:(k + 1) * P], x_norm[:, t, kk * P:(kk + 1) * P], ident[:])
                    last.then_inc(S["c_t_psum"], 1)
            pe.wait_ge(S["c_xl"], 4)
            for i, ch in enumerate(sched["c_uq"]):
                arrived(ch)
                token_major(ch, [bank[(4 + 2 * i + t) % 8][:] for t in range(NT)], QL // P)
            for i, ch in enumerate(sched["c_ukv"]):
                arrived(ch)
                for ready in ("c_q_ready", "c_q1_ready"):
                    pe.wait_ge(S[ready], 1 if i == 0 else 3)
                hi, lo = view(w_hi, ch), view(w_lo, ch)
                for n in range(2):
                    for t in range(NT):
                        b = bank[(2 + 4 * i + 2 * n + t) % 8]
                        for k in range(2):
                            last = product(b[:], xT_hi[:, t, 3 + k, :], xT_lo[:, t, 3 + k, :],
                                           hi[:, k, 512 * n:512 * n + 512], lo[:, k, 512 * n:512 * n + 512], k == 0, k == 1)
                last.then_inc(S["mm_done"], 1)
            pe.wait_ge(S["c_kv_ready"], 4)
            pe.wait_ge(S["c_rope_ready"], 1)

            def mla_qk(h):
                if h >= 2:
                    pe.wait_ge(S["c_qkT_ready"], h - 1)
                b = bank[h % 2]
                for i, src in enumerate((c_q, c_k)):
                    for t in range(NT):
                        at = (2 * i + t) * P
                        last = pe.transpose(b[0:CD, at:at + P], src[:, t, h * CD:(h + 1) * CD], ident[:])
                last.then_inc(S["c_qkT_psum"], 1)

            def mla_scores(h):
                pe.wait_ge(S["c_qkT_ready"], h + 1)
                if h >= 2:
                    pe.wait_ge(S["c_probs"], 2 * (h - 1))
                b = bank[2 + h % 2]
                qk = c_qkT[0:CD, h % 2]
                for t in range(NT):
                    last = pe.matmul(b[:, t * SEQ:(t + 1) * SEQ], qk[:, t, :], qk[:, 2:4, :].rearrange("p a b -> p (a b)"),
                                     start=True, stop=True)
                last.then_inc(S["c_scores"], 1)

            def mla_pT(h):
                pe.wait_ge(S["c_probs"], 2 * (h + 1))
                b = bank[4 + h % 2]
                for t in range(NT):
                    for k in range(2):
                        at = (2 * t + k) * P
                        last = pe.transpose(b[:, at:at + P], c_p[:, h % 2, t, k * P:(k + 1) * P], ident[:])
                last.then_inc(S["c_pt_psum"], 1)

            def mla_values(h):
                pe.wait_ge(S["c_pt_ready"], h + 1)
                if h == 8:
                    pe.wait_ge(S["c_o_ready"], 2)
                o = slice((h % 8) * CV, (h % 8) * CV + CV)
                for t in range(NT):
                    for k in range(2):
                        last = pe.matmul(bank[6 + t][:, o], c_pT[:, h % 2, 2 * t + k, :], c_v[:, k, h * CV:(h + 1) * CV],
                                         start=k == 0, stop=k == 1)
                last.then_inc(S["c_o_psum"], 1)

            for r in range(CH + 3):
                if r < CH:
                    mla_qk(r)
                if 0 <= r - 1 < CH:
                    mla_scores(r - 1)
                if 0 <= r - 2 < CH:
                    mla_pT(r - 2)
                if 0 <= r - 3 < CH:
                    mla_values(r - 3)
            transpose_operand(6, lambda t: pe.wait_ge(S["c_o_ready"], 4))
            pe.wait_ge(S["xTl_ready"], 28)
            out_projection("c_out")
            transpose_norm(7, 6)
            squared_relu(1)


INPUTS = ("x", "norm_mix", "norm_ffn", "swa_w_in", "swa_sinks", "swa_w_out", "ffn_w_gate_up", "ffn_w_down",
          "final_norm", "positions_2", "ab_norm_2", "ab_w_in_2", "ab_conv_2", "ab_gate_b_2", "ab_head_g_2",
          "ab_v_g_2", "ab_ws_2", "ab_bs_2", "ab_w_out_2", "c_norm_2", "c_w_in_2", "c_q_g_2", "c_kv_g_2",
          "c_w_uq_2", "c_w_ukv_2", "c_w_out_2", "ffn_norm_2", "ffn_w1_2", "ffn_w2_2", "final_norm_2")


def kernel(**inputs):
    import numpy as np
    import concourse.bacc as bacc
    from concourse.bass_utils import run_bass_kernel_spmd

    nc = bacc.Bacc("TRN2", target_bir_lowering=False, num_devices=1)
    arrays, t_in = {}, {}
    for name in INPUTS:
        a = np.ascontiguousarray(inputs[name])
        arrays[f"in_{name}"] = a
        t_in[name] = nc.dram_tensor(f"in_{name}", a.shape, mybir.dt.from_np(a.dtype), kind="ExternalInput").ap()
    out = nc.dram_tensor("out_0", (1, SEQ, DM), F32, kind="ExternalOutput").ap()
    build(nc, t_in, out)
    r = run_bass_kernel_spmd(nc, [arrays], core_ids=[0])
    return r.results[0]["out_0"]
```

```python
import math
from contextlib import ExitStack

import concourse.bass as bass
from concourse import mybir

F32 = mybir.dt.float32
F32R = mybir.dt.float32r
I32 = mybir.dt.int32
ALU = mybir.AluOpType
ACT = mybir.ActivationFunctionType
AX = mybir.AxisListType.X

P = 128
SEQ = 256
NT = SEQ // P
DM = 1024
KT = DM // P
EPS = 1e-6
NQH, NKV, HD = 16, 4, 64
SWA_COLS = P + 2 * P
BIG = 3.0e38
FF1 = 2816
FF2 = 4096
CW = 256
N1 = FF1 // CW
N2 = FF2 // CW
AH, AD = 4, 128
AW = AH * AD
BG = 4
CONV = 5
CH, CN, CR, CV = 16, 64, 32, 64
CD = CN + CR
QL, KVL = 384, 256
CIN = QL + KVL + CR
CKT = (QL + KVL) // P
HALF = CR // 2
ROPE_BASE = 10000.0
SLOTS = 4
SLOT = 2048


class Chunk:

    def __init__(self, index, slot, use, prev, shape):
        self.index, self.slot, self.use, self.prev, self.shape = index, slot, use, prev, shape


def weight_schedule():
    uses = {s: [] for s in range(SLOTS)}
    count = [0]
    cycle = list(range(SLOTS))
    at = [0]
    sched = {}

    def add(phase, shape, slot=None):
        if slot is None:
            slot = cycle[at[0] % SLOTS]
            at[0] += 1
        c = count[0]
        count[0] += 1
        prev = uses[slot][-1] if uses[slot] else None
        sched.setdefault(phase, []).append(Chunk(c, slot, len(uses[slot]), prev, shape))
        uses[slot].append(c)

    for _ in range(6):
        add("swa_in", (KT, CW))
    for _ in range(4):
        add("swa_out", (2, DM))
    up, spare, gate, down = [cycle[(at[0] + i) % SLOTS] for i in range(SLOTS)]
    add("ffn1", (KT, CW), up)
    add("ffn1", (KT, CW), spare)
    for _ in range(N1 - 2):
        add("ffn1", (KT, CW), gate)
        add("ffn1", (2, DM), down)
        add("ffn1", (KT, CW), up)
    add("ffn1", (KT, CW), gate)
    add("ffn1", (KT, CW), up)
    add("ffn1", (2, DM), down)
    add("ffn1", (2, DM), spare)
    cycle[:] = gate, up, down, spare
    at[0] = 0
    for i in range(13):
        add("ab_in", (KT, 16 if i == 2 else CW))
    for _ in range(4):
        add("ab_out", (2, DM))

    def squared_relu(phase):
        add(phase, (KT, CW))
        add(phase, (KT, CW))
        for _ in range(N2 - 2):
            add(phase, (2, DM))
            add(phase, (KT, CW))
        add(phase, (2, DM))
        add(phase, (2, DM))

    squared_relu("ffn2a")
    for n in (CW, CW, CW):
        add("c_in", (KT, n))
    for _ in range(3):
        add("c_uq", (QL // P, 512))
    for _ in range(2):
        add("c_ukv", (KVL // P, DM))
    for _ in range(4):
        add("c_out", (2, DM))
    squared_relu("ffn2b")
    return sched, count[0]


def build(nc, t_in, out):
    sched, n_chunks = weight_schedule()
    order = [c for phase in sched.values() for c in phase]
    ctx = ExitStack()
    with ctx:
        def sb(name, shape, dt=F32):
            return ctx.enter_context(nc.sbuf_tensor(name, shape, dt))

        w_raw = [sb(f"w_raw{s}", [P, SLOT]) for s in range(SLOTS)]
        w_hi = [sb(f"w_hi{s}", [P, SLOT], F32R) for s in range(SLOTS)]
        w_lo = [sb(f"w_lo{s}", [P, SLOT], F32R) for s in range(SLOTS)]

        def view(ring, ch):
            k, n = ch.shape
            return ring[ch.slot][:, 0:k * n].rearrange("p (k n) -> p k n", k=k)

        x_res = sb("x_res", [P, NT, DM])
        x_norm = sb("x_norm", [P, NT, DM])
        xT_hi = sb("xT_hi", [P, NT, KT, P], F32R)
        xT_lo = sb("xT_lo", [P, NT, KT, P], F32R)
        gain = sb("gain", [P, 2, DM])
        ssq = sb("ssq", [P, NT, 2])
        mean_sq = sb("mean_sq", [P, NT])
        rstd = sb("rstd", [P, NT])
        minus_half = sb("minus_half", [P, 16])
        ident = sb("ident", [P, P])
        sel = sb("sel", [AH, AH, P])
        one = sb("one", [AH, 1])
        dist = sb("dist", [P, SWA_COLS])
        sinks = sb("sinks", [P, NQH])
        pcols = sb("pcols", [P, 48])
        gate_b = sb("gate_b", [16, 1])
        wsT = sb("wsT", [P, BG, P])
        bs_all = sb("bs_all", [P, BG, P])
        pos_i = sb("pos_i", [P, NT], I32)
        pos_f = sb("pos_f", [P, NT])
        freq = sb("freq", [P, HALF])
        ang = sb("ang", [P, NT, HALF])
        turns = sb("turns", [P, NT, HALF])
        cosr = sb("cosr", [P, NT, HALF])
        cos = sb("cos", [P, NT, HALF])
        sin = sb("sin", [P, NT, HALF])
        ff_hi = [sb(f"ff_hi{i}", [P, 2, SEQ], F32R) for i in range(2)]
        ff_lo = [sb(f"ff_lo{i}", [P, 2, SEQ], F32R) for i in range(2)]

        ARENA = 13700
        arena = sb("arena", [P, ARENA])
        used = [0]

        def take(parts, *shape):
            n = math.prod(shape)
            a = arena[0:parts, used[0]:used[0] + n]
            used[0] += n
            assert used[0] <= ARENA, used[0]
            if len(shape) == 1:
                return a
            names = "abcd"[:len(shape)]
            return a.rearrange(f"p ({' '.join(names)}) -> p {' '.join(names)}",
                               **{names[i]: shape[i] for i in range(len(shape))})

        ff_act = take(P, 2, SEQ)
        ff_h = take(P, 2, SEQ)
        used[0] = 0
        prows = take(48, P)
        ws = take(P, BG, P)
        swa_qT = take(P, 8, SEQ)
        swa_kT = take(P, NKV, SEQ)
        swa_v = take(P, NT, NKV * HD)
        swa_s = take(P, 2, 4, SWA_COLS + 2)
        SWA_PARTS = ((0, 1 + P), (1 + P, 2 + SWA_COLS))
        swa_pT = take(P, 2, 12, P)
        swa_mx = take(P, NT, NQH)
        swa_nm = take(P, NT, NQH)
        swa_sum = take(P, NT, NQH)
        swa_rden = take(P, NT, NQH)
        used[0] = 0
        PADW = SEQ + CONV - 1
        ab_pad = take(P, 8, PADW)
        ab_cv = take(P, 8, SEQ)
        ab_v1 = take(P, NT, AH, AD + 1)
        ab_u = take(P, BG, SEQ)
        ab_vb = take(P, NT, BG * P)
        ab_sig = take(P, AH, SEQ)
        ab_e = take(P, 2, 2, SWA_COLS)
        num_at = used[0]
        ab_num = take(P, 2, AH, NT, AD + 1)
        ab_sq = take(P, NT * BG, P)
        ab_ss = take(P, 8)
        ab_ms = take(P, 8)
        ab_rs = take(P, 8)
        ab_t = take(P, NT, 4, AH)
        ab_em = take(P, 2, NT, AH)
        ab_rd = take(P, 2, AH, NT)
        ab_dd = take(P, 2, AH, NT)
        used[0] = num_at
        g_raw = take(16, SEQ)
        g_w = take(AH, 2, SEQ)
        g_B = take(AH, 2, SEQ)
        g_M = take(AH, 2, SEQ)
        g4 = x_norm[0:AH, 0, :].rearrange("p (k t) -> p k t", k=4)
        g_am = x_norm[0:AH, 1, :].rearrange("p (k t) -> p k t", k=4)
        g_nM = x_norm[0:AH, 0, 0:2 * SEQ].rearrange("p (d t) -> p d t", d=2)
        used[0] = 0
        c_lat = take(P, NT, CIN)
        c_q = take(P, NT, CH * CD)
        c_k = take(P, NT, CH * CD)
        c_v = take(P, NT, CH * CV)
        c_qkT = take(P, 2, 4, P)
        c_p = take(P, 2, NT, SEQ)
        c_pT = take(P, 2, 4, P)
        c_tmp = c_p.rearrange("p a b c -> p (a b c)").rearrange("p (i n) -> p i n", i=4)
        c_gain = take(P, QL + KVL)
        c_kr = take(P, NT, CR)
        c_krt = take(P, 4, NT, HALF)
        c_ss = take(P, NT, 2)
        c_ms = take(P, NT, 2)
        c_rs = take(P, NT, 2)
        c_mx = take(P, CH, NT)
        c_nm = take(P, CH, NT)
        c_sum = take(P, NT, CH)
        c_rden = take(P, NT, CH)

        bank = [ctx.enter_context(nc.psum_tensor(f"bank{i}", [P, 512], F32)) for i in range(8)]

        S = {n: ctx.enter_context(nc.semaphore(n)) for n in (
            "hi_done lo_done mm_done acc_done x0_loaded x1_loaded sinks_loaded small_loaded ws_loaded pos_loaded "
            "gain_loaded cgain_loaded consts_ready dist_step "
            "resid_ready ssq_ready rstd_step rstd_ready xn_ready t_psum xTh_ready xTl_ready "
            "params_psum params_ready wsT_psum wsT_ready rope_angle rope_ready "
            "act_chain dve_chain pool_chain "
            "ff1_sg ff1_h ff1_t ff1_hi ff1_lo ff2_t ff2_relu ff2_h ff2_hi ff2_lo "
            "swa_q_ready swa_k_ready swa_v_ready swa_scores swa_biased swa_nmax swa_probs swa_pt_psum "
            "swa_pt_ready swa_o_psum swa_o_ready swa_oT_psum swa_oh_ready swa_ol_ready "
            "g_raw_ready g4_loaded g_abs_ready g_ln_ready g_rows_ready g_cols_psum g_cols_ready g_em_ready "
            "qk_padded conv_ready qk_ready v1_ready u_ready vb_ready sig_ready "
            "vb_sumsq vb_rstd vn_ready sp_psum sp_read nM_psum e_exp e_ready st_psum w_ready num_psum num_ready "
            "h_sumsq h_rstd hn_ready hT_psum ab_full ab_hi ab_lo pads_ready "
            "c_in0_done c_uq0_done c_lat_ready c_ssq c_rstd c_cn_ready c_t_psum c_xh c_xl c_q_ready c_q1_ready c_kv_ready c_rope_ready "
            "c_qkT_psum c_qkT_ready c_scores c_nmax c_probs c_pt_psum c_pt_ready c_o_psum c_o_ready "
            "out_stored"
        ).split()}
        loaded = [ctx.enter_context(nc.semaphore(f"slot{s}_loaded")) for s in range(SLOTS)]
        block = ctx.enter_context(nc.Block())

        ffn_phases = ("ffn2a", "ffn2b")
        AB_OUT_ORDER = (2, 3, 0, 1)
        ab_slot = (4, 5, 6, 7, 0, 1, 2, 3)
        AB_BANK = (4, 5, 0, 1, 6, 7, 2, 3, 0, 6, 7, 6, 7)
        phase_of_norm = {1: "swa_out", 2: "ffn1", 4: "ab_out", 5: "ffn2a", 6: "c_out", 7: "ffn2b"}
        additions = {n: i for i, n in enumerate(phase_of_norm)}
        C_UQ_BANK = ((4, 5), (6, 7), (0, 1))
        C_UKV_BANK = (((4, 2), (6, 3)), ((5, 0), (7, 1)))
        norm_order = ([(n, t) for n in (0, 1) for t in range(NT)] + [(2, 0), (3, 0), (2, 1), (3, 1)]
                      + [(n, t) for n in (4, 5, 6, 7) for t in range(NT)])
        turn = {nt: i + 1 for i, nt in enumerate(norm_order)}

        SWA_PT_BANK = ((2, 2, 2), (2, 2, 2), (2, 2, 2), (2, 0, 1))
        HALF_D = (slice(0, DM // 2), slice(DM // 2, DM))

        def half_turn(n, t, j):
            return 2 * turn[n, t] - 1 + j

        def kv_parts(i, n, t):
            src = bank[C_UKV_BANK[i][n][t]][:].rearrange("p (h e) -> p h e", e=CN + CV)
            h0 = 8 * i + 4 * n
            k = c_k[:, t, h0 * CD:(h0 + 4) * CD].rearrange("p (h e) -> p h e", e=CD)
            v = c_v[:, t, h0 * CV:(h0 + 4) * CV].rearrange("p (h e) -> p h e", e=CV)
            return (src[:, :, 0:CN], k[:, :, 0:CN]), (src[:, :, CN:CN + CV], v)

        @block.sync
        def _(sp):
            sp.dma_start(x_res[:, 0], t_in["x"][0, 0:P]).then_inc(S["x0_loaded"], 16)

            def load(ch, src, it=0, stride=0):
                if ch.prev is not None:
                    sp.wait_ge(S["lo_done"], ch.prev + 1 + it * stride)
                sp.dma_start(view(w_raw, ch), src).then_inc(loaded[ch.slot], 16)

            def cols(w, at, n):
                return w.rearrange("(k p) c -> p k c", p=P)[:, :, at:at + n]

            def by_cols(w):
                return w.rearrange("(k p) (i c) -> p k i c", p=P, c=CW)

            def by_rows(w):
                return w.rearrange("(i k p) c -> p i k c", p=P, k=2)

            w = t_in["swa_w_in"][0]
            for i, ch in zip((5, 4, 0, 1, 2, 3), sched["swa_in"]):
                load(ch, cols(w, i * CW, CW))
            w = by_rows(t_in["swa_w_out"][0])
            for i, ch in enumerate(sched["swa_out"]):
                load(ch, w[:, i])
            gu, dn = by_cols(t_in["ffn_w_gate_up"][0]), by_rows(t_in["ffn_w_down"][0])
            c = sched["ffn1"]
            load(c[0], gu[:, :, 0])
            load(c[1], gu[:, :, N1])
            load(c[2], gu[:, :, 1])
            load(c[3], dn[:, 0])
            load(c[4], gu[:, :, N1 + 1])
            with sp.Fori(0, N1 - 3) as it:
                load(c[5], gu[:, :, it + 2], it, 3)
                load(c[6], dn[:, it + 1], it, 3)
                load(c[7], gu[:, :, it + (N1 + 2)], it, 3)
            load(c[-4], gu[:, :, N1 - 1])
            load(c[-3], gu[:, :, 2 * N1 - 1])
            load(c[-2], dn[:, N1 - 2])
            load(c[-1], dn[:, N1 - 1])

            w = t_in["ab_w_in_2"][0]
            uv = 4 * AW + 16
            at = [i * CW for i in (4, 5)] + [4 * AW] + [i * CW for i in range(4)] + [uv + i * CW for i in (2, 3, 0, 1)] + [3 * AW, 3 * AW + CW]
            for a, ch in zip(at, sched["ab_in"]):
                load(ch, cols(w, a, ch.shape[1]))
            w = by_rows(t_in["ab_w_out_2"][0])
            for i, ch in zip(AB_OUT_ORDER, sched["ab_out"]):
                load(ch, w[:, i])

            def squared_relu(layer):
                c = sched[ffn_phases[layer]]
                w1, w2 = by_cols(t_in["ffn_w1_2"][layer]), by_rows(t_in["ffn_w2_2"][layer])
                load(c[0], w1[:, :, 0])
                load(c[1], w1[:, :, 1])
                with sp.Fori(0, N2 // 2 - 1) as it:
                    load(c[2], w2[:, 2 * it], it, 4)
                    load(c[3], w1[:, :, 2 * it + 2], it, 4)
                    load(c[4], w2[:, 2 * it + 1], it, 4)
                    load(c[5], w1[:, :, 2 * it + 3], it, 4)
                load(c[-2], w2[:, N2 - 2])
                load(c[-1], w2[:, N2 - 1])

            squared_relu(0)
            w = t_in["c_w_in_2"][0]
            for i, ch in enumerate(sched["c_in"]):
                load(ch, cols(w, min(i * CW, CIN - CW), CW))
            for i, ch in enumerate(sched["c_uq"]):
                load(ch, cols(t_in["c_w_uq_2"][0], i * 512, 512))
            for i, ch in enumerate(sched["c_ukv"]):
                load(ch, cols(t_in["c_w_ukv_2"][0], i * DM, DM))
            w = by_rows(t_in["c_w_out_2"][0])
            for i, ch in enumerate(sched["c_out"]):
                load(ch, w[:, i])
            squared_relu(1)
            o = out[0].rearrange("(t p) d -> p t d", p=P)
            for t in range(NT):
                for j in range(2):
                    sp.wait_ge(S["xn_ready"], half_turn(7, t, j))
                    sp.dma_start(o[:, t, HALF_D[j]], x_norm[:, t, HALF_D[j]]).then_inc(S["out_stored"], 16)
            sp.wait_ge(S["out_stored"], 32 * NT)

        norm_gain = [t_in["norm_mix"][0], t_in["norm_ffn"][0], t_in["final_norm"], t_in["ab_norm_2"][0],
                     t_in["ffn_norm_2"][0], t_in["c_norm_2"][0], t_in["ffn_norm_2"][1], t_in["final_norm_2"]]

        @block.gpsimd
        def _(pool):
            chain = [0]

            def step(ins):
                chain[0] += 1
                ins.then_inc(S["pool_chain"], 1)
                pool.wait_ge(S["pool_chain"], chain[0])

            def load_gain(n):
                src = norm_gain[n].rearrange("(a d) -> a d", a=1).broadcast_to([P, DM])
                pool.dma_start(gain[:, n % 2], src).then_inc(S["gain_loaded"], 16)

            pool.memset(minus_half[:], -0.5)
            load_gain(0)
            step(pool.memset(ident[:], 0.0))
            pool.affine_select(out=ident[:], in_=ident[:], compare_op=ALU.not_equal, fill=1.0, base=0,
                               pattern=[[-1, P]], channel_multiplier=1).then_inc(S["consts_ready"], 1)
            pool.wait_ge(S["gain_loaded"], 16)
            load_gain(1)
            step(pool.memset(sel[:], 0.0))
            pool.affine_select(out=sel[:], in_=sel[:], compare_op=ALU.not_equal, fill=1.0, base=0,
                               pattern=[[-1, AH], [0, P]], channel_multiplier=1).then_inc(S["consts_ready"], 1)
            pool.memset(one[:], 1.0)
            for i in range(HALF):
                last = pool.memset(freq[:, i:i + 1], float(ROPE_BASE ** (-i / HALF)))
            last.then_inc(S["consts_ready"], 1)

            def norm(*order):
                for n, t in order:
                    pool.wait_ge(S["ssq_ready"], half_turn(n, t, 1))
                    step(pool.tensor_scalar(mean_sq[:, t:t + 1], ssq[:, t, 0:1], ssq[:, t, 1:2], EPS, ALU.add, ALU.add))
                    pool.tensor_tensor(rstd[:, t:t + 1], mean_sq[:, t:t + 1], minus_half[:, 0:1],
                                       ALU.pow).then_inc(S["rstd_ready"], 1)

            def next_gain(n):
                pool.wait_ge(S["xn_ready"], half_turn(n, 1, 1))
                pool.wait_ge(S["gain_loaded"], 16 * (n + 2))
                load_gain(n + 2)

            step(pool.iota(dist[:, 0:P], pattern=[[-1, P]], base=0, channel_multiplier=1,
                           allow_small_or_imprecise_dtypes=True))
            step(pool.iota(dist[:, P:3 * P], pattern=[[-1, 2 * P]], base=P, channel_multiplier=1,
                           allow_small_or_imprecise_dtypes=True))
            for at, sign, op in ((0, -1, ALU.is_ge), (P, 1, ALU.is_gt), (2 * P, -1, ALU.is_ge)):
                d = dist[:, at:at + P]
                ins = pool.affine_select(out=d, in_=d, compare_op=op, fill=BIG, base=0,
                                         pattern=[[sign, P]], channel_multiplier=-sign)
                ins.then_inc(S["dist_step"], 1)
            norm((0, 0), (0, 1))
            next_gain(0)
            norm((1, 0), (1, 1))
            next_gain(1)
            norm((2, 0), (3, 0), (2, 1), (3, 1))
            next_gain(2)
            next_gain(3)
            pool.memset(ab_pad[:, :, 0:2], 0.0)
            pool.memset(ab_pad[:, :, 2 + SEQ:PADW], 0.0)
            pool.memset(ab_v1[:, :, :, AD:AD + 1], 1.0).then_inc(S["pads_ready"], 1)
            def masks(h):
                pool.wait_ge(S["e_exp"], 4 * (h + 1))
                for d, at, sign in ((0, 0, 1), (0, 2 * P, 1), (1, 0, -1), (1, 2 * P, -1)):
                    e = ab_e[:, h % 2, d, at:at + P]
                    last = pool.affine_select(out=e, in_=e, compare_op=ALU.is_ge, fill=0.0, base=0,
                                              pattern=[[sign, P]], channel_multiplier=-sign)
                    last.then_inc(S["e_ready"], 1)

            def group_rstd(sumsq, ready):
                pool.wait_ge(S[sumsq], 1)
                step(pool.tensor_scalar(ab_ms, ab_ss, 1.0 / P, EPS, ALU.mult, ALU.add))
                pool.tensor_tensor(ab_rs, ab_ms, minus_half[:, 0:8], ALU.pow).then_inc(S[ready], 1)

            group_rstd("vb_sumsq", "vb_rstd")
            for h in range(AH):
                masks(h)
            pool.wait_ge(S["vn_ready"], 1)
            group_rstd("h_sumsq", "h_rstd")
            norm((4, 0), (4, 1))
            next_gain(4)
            pool.dma_start(c_gain[:, 0:QL], t_in["c_q_g_2"].broadcast_to([P, QL])).then_inc(S["cgain_loaded"], 16)
            pool.dma_start(c_gain[:, QL:QL + KVL], t_in["c_kv_g_2"].broadcast_to([P, KVL])).then_inc(S["cgain_loaded"], 16)
            norm((5, 0), (5, 1))
            next_gain(5)
            for t in range(NT):
                pool.wait_ge(S["c_ssq"], 2 * t + 2)
                for j, n in ((0, QL), (1, KVL)):
                    step(pool.tensor_scalar(c_ms[:, t, j:j + 1], c_ss[:, t, j:j + 1], 1.0 / n, EPS, ALU.mult, ALU.add))
                pool.tensor_tensor(c_rs[:, t], c_ms[:, t], minus_half[:, 0:2], ALU.pow).then_inc(S["c_rstd"], 1)
            norm((6, 0), (6, 1))
            norm((7, 0), (7, 1))

        @block.scalar
        def _(act):
            chain = [0]

            def step(ins):
                chain[0] += 1
                ins.then_inc(S["act_chain"], 1)
                act.wait_ge(S["act_chain"], chain[0])

            split = [0]

            def high(ch, it=0, stride=0):
                act.wait_ge(loaded[ch.slot], 16 * (ch.use + 1) + it * (16 if stride else 0))
                if ch.prev is not None:
                    act.wait_ge(S["mm_done"], ch.prev + 1 + it * stride)
                act.activation(view(w_hi, ch), view(w_raw, ch), ACT.Copy).then_inc(S["hi_done"], 1)

            def high_upto(index):
                while split[0] < min(index, n_chunks):
                    high(order[split[0]])
                    split[0] += 1

            act.dma_start(x_res[:, 1], t_in["x"][0, P:SEQ]).then_inc(S["x1_loaded"], 16)
            act.dma_start(pos_i[:], t_in["positions_2"][0].rearrange("(t p) -> p t", p=P),
                          allow_slow_non_contiguous=True).then_inc(S["pos_loaded"], 16)
            act.dma_start(sinks[:], t_in["swa_sinks"].broadcast_to([P, NQH])).then_inc(S["sinks_loaded"], 16)
            act.dma_start(prows[0:40, :], t_in["ab_conv_2"][0].rearrange("j (f c) -> (j f) c", c=P)).then_inc(S["small_loaded"], 16)
            act.dma_start(prows[40:44, :], t_in["ab_head_g_2"][0].rearrange("(f c) -> f c", c=P)).then_inc(S["small_loaded"], 16)
            act.dma_start(prows[44:48, :], t_in["ab_v_g_2"][0].rearrange("(f c) -> f c", c=P)).then_inc(S["small_loaded"], 16)
            act.dma_start(gate_b[:], t_in["ab_gate_b_2"][0].rearrange("(a b) -> a b", b=1),
                          allow_slow_non_contiguous=True).then_inc(S["small_loaded"], 16)
            act.dma_start(ws[:], t_in["ab_ws_2"][0].rearrange("g t s -> t g s")).then_inc(S["ws_loaded"], 16)
            act.dma_start(bs_all[:],
                          t_in["ab_bs_2"].broadcast_to([P, BG, P])).then_inc(S["ws_loaded"], 16)
            high_upto(1)

            def sum_squares(n, t):
                for j in range(2):
                    if n == 0:
                        act.wait_ge(S[("x0_loaded", "x1_loaded")[t]], 16)
                    elif n == 3:
                        act.wait_ge(S["xn_ready"], half_turn(2, t, j))
                    else:
                        act.wait_ge(S["resid_ready"], 4 * additions[n] + 2 * t + j + 1)
                    if turn[n, t] > 1 and j == 0:
                        act.wait_ge(S["ssq_ready"], half_turn(n, t, 0) - 1)
                    act.activation(x_norm[:, t, HALF_D[j]], x_res[:, t, HALF_D[j]], ACT.Square, scale=DM ** -0.5,
                                   accum_out=ssq[:, t, j:j + 1]).then_inc(S["ssq_ready"], 1)

            def transposed_high(n, t):
                for half in range(2):
                    act.wait_ge(S["t_psum"], 4 * n + 2 * t + half + 1)
                    act.activation(xT_hi[:, t, 4 * half:4 * half + 4, :].rearrange("p k c -> p (k c)"),
                                   bank[2 * t + half][:], ACT.Copy).then_inc(S["xTh_ready"], 1)

            def enter(use, n, early, then):
                sum_squares(n, 0)
                sum_squares(n, 1)
                transposed_high(use, 0)
                high_upto(early)
                transposed_high(use, 1)
                high_upto(then)

            c = sched["swa_in"]
            sum_squares(0, 0)
            high_upto(1)
            sum_squares(0, 1)
            high_upto(2)
            transposed_high(0, 0)
            transposed_high(0, 1)
            high_upto(SLOTS)

            act.wait_ge(S["mm_done"], c[0].index + 1)
            act.activation(swa_v.rearrange("p a b -> p (a b)"), bank[5][:], ACT.Copy).then_inc(S["swa_v_ready"], 1)
            high_upto(c[1].index + 1 + SLOTS)

            def queries(i):
                ch = c[2 + i]
                act.wait_ge(S["mm_done"], ch.index + 1)
                act.activation(swa_qT[:, 2 * i:2 * i + 2, :].rearrange("p a b -> p (a b)"), bank[(6, 7, 4, 5)[i]][:],
                               ACT.Copy, scale=HD ** -0.5).then_inc(S["swa_q_ready"], 1)

            def swa_probabilities(g):
                act.wait_ge(S["swa_nmax"], g + 1)
                for j in range(4):
                    h = 4 * g + j
                    for t, (a, b) in enumerate(SWA_PARTS):
                        s = swa_s[:, g % 2, j, a:b]
                        act.activation(s, s, ACT.Exp, bias=swa_nm[:, t, h:h + 1],
                                       accum_out=swa_sum[:, t, h:h + 1]).then_inc(S["swa_probs"], 1)

            def swa_transposed(g):
                for u in range(3):
                    act.wait_ge(S["swa_pt_psum"], 3 * g + u + 1)
                    act.activation(swa_pT[:, g % 2, 4 * u:4 * u + 4, :].rearrange("p a b -> p (a b)"),
                                   bank[SWA_PT_BANK[g][u]][:], ACT.Copy).then_inc(S["swa_pt_ready"], 1)
                    if u == 0 and g >= 1:
                        swa_operand(g - 1)

            def swa_operand(g):
                act.wait_ge(S["swa_oT_psum"], g + 1)
                act.activation(xT_hi[:, :, 2 * g:2 * g + 2, :], bank[3][:].rearrange("p (t k c) -> p t k c", t=NT, k=2),
                               ACT.Copy).then_inc(S["swa_oh_ready"], 1)

            o = sched["swa_out"]
            queries(0)
            queries(1)
            high_upto(c[2].index + 1 + SLOTS)
            swa_probabilities(0)
            queries(2)
            swa_transposed(0)
            high_upto(c[3].index + 1 + SLOTS)
            swa_probabilities(1)
            high_upto(c[4].index + 1 + SLOTS)
            queries(3)
            swa_transposed(1)
            high_upto(c[5].index + 1 + SLOTS)
            swa_probabilities(2)
            swa_transposed(2)
            high_upto(o[0].index + 1 + SLOTS)
            swa_probabilities(3)
            high_upto(o[1].index + 1 + SLOTS)
            swa_transposed(3)
            swa_operand(3)
            c = sched["ffn1"]
            enter(1, 1, 0, c[3].index + 1)

            def silu_gate(ch, i, it=0):
                act.wait_ge(S["mm_done"], ch.index + 1 + 3 * it)
                act.activation(ff_act[:], bank[0][:].rearrange("p (a b) -> p a b", a=2),
                               ACT.Silu).then_inc(S["ff1_sg"], 1)

            def hidden_high(i, it=0, buf=0):
                act.wait_ge(S["ff1_h"], i + 1 + it)
                act.activation(ff_hi[buf][:], ff_h[:], ACT.Copy).then_inc(S["ff1_hi"], 1)

            def first_hidden_high(transposed, count, ready):
                act.wait_ge(S[transposed], count)
                act.activation(ff_hi[0][:], bank[2][:].rearrange("p (a b) -> p a b", a=2), ACT.Copy).then_inc(S[ready], 1)

            silu_gate(c[0], 0)
            high_upto(c[3].index + 1)
            first_hidden_high("ff1_t", 1, "ff1_hi")
            high_upto(c[4].index + 1)
            silu_gate(c[2], 1)
            high(c[5])
            high(c[6])
            hidden_high(1)
            high(c[7])
            with act.Fori(0, N1 - 4) as it:
                silu_gate(c[5], 2, it)
                high(c[8], it, 3)
                high(c[9], it, 3)
                hidden_high(2, it)
                high(c[10], it, 3)
            silu_gate(c[-7], N1 - 2)
            high(c[-4])
            hidden_high(N1 - 2)
            for ch in c[-3:]:
                high(ch)
            silu_gate(c[-4], N1 - 1)
            hidden_high(N1 - 1, buf=1)
            split[0] = c[-1].index + 1
            high_upto(c[-1].index + 1 + 2)

            sum_squares(2, 0)
            sum_squares(3, 0)
            sum_squares(2, 1)
            transposed_high(2, 0)
            sum_squares(3, 1)
            c = sched["ab_in"]
            high_upto(c[2].index + 1)
            transposed_high(2, 1)
            high_upto(c[0].index + SLOTS)
            for i in range(2):
                ch = c[i]
                act.wait_ge(S["mm_done"], ch.index + 1)
                for t in range(NT):
                    last = act.activation(ab_v1[:, t, 2 * i:2 * i + 2, 0:AD],
                                          bank[AB_BANK[i]][:, t * 256:t * 256 + 256].rearrange("p (a b) -> p a b", a=2), ACT.Copy)
                last.then_inc(S["v1_ready"], 1)
                high_upto(ch.index + 1 + SLOTS)
            act.wait_ge(S["small_loaded"], 64)
            act.wait_ge(S["mm_done"], c[2].index + 1)
            act.activation(g_raw, bank[0][0:16, 0:SEQ], ACT.Identity, bias=gate_b[:]).then_inc(S["g_raw_ready"], 1)
            act.wait_ge(S["g_raw_ready"], 1)
            for k in range(4):
                act.dma_start(g4[:, k, :], g_raw[4 * k:4 * k + 4, :]).then_inc(S["g4_loaded"], 16)
            act.wait_ge(S["pads_ready"], 1)
            high_upto(c[2].index + 1 + SLOTS)

            def pairs(i):
                return bank[AB_BANK[i]][:].rearrange("p (a b) -> p a b", a=2)

            for i in range(4):
                ch = c[3 + i]
                act.wait_ge(S["mm_done"], ch.index + 1)
                act.activation(ab_pad[:, 2 * i:2 * i + 2, 2:2 + SEQ], pairs(3 + i), ACT.Copy).then_inc(S["qk_padded"], 1)
                high_upto(ch.index + 1 + SLOTS)
                if i == 1:
                    act.wait_ge(S["g_abs_ready"], 1)
                    step(act.activation(g_w, g_w, ACT.Exp))
                    act.activation(g_w, g_w, ACT.Ln, bias=1.0).then_inc(S["g_ln_ready"], 1)
            act.wait_ge(S["conv_ready"], 4)
            act.activation(ab_pad[:, :, 0:SEQ], ab_cv[:], ACT.Silu).then_inc(S["qk_ready"], 1)
            for i in range(2):
                ch = c[7 + i]
                act.wait_ge(S["mm_done"], ch.index + 1)
                act.activation(ab_vb[:, :, i * CW:(i + 1) * CW], pairs(7 + i), ACT.Gelu_apprx_tanh).then_inc(S["vb_ready"], 1)
                high_upto(ch.index + 1 + SLOTS)

            def gating_u(i):
                ch = c[9 + i]
                act.wait_ge(S["mm_done"], ch.index + 1)
                act.activation(ab_u[:, 2 * i:2 * i + 2, :], pairs(9 + i), ACT.Gelu_apprx_tanh).then_inc(S["u_ready"], 1)
                high_upto(ch.index + 1 + SLOTS)

            def output_gate(i):
                ch = c[11 + i]
                act.wait_ge(S["mm_done"], ch.index + 1)
                act.activation(ab_sig[:, 2 * i:2 * i + 2, :], pairs(11 + i), ACT.Sigmoid).then_inc(S["sig_ready"], 1)
                high_upto(ch.index + 1 + SLOTS)

            def decay_weights(h):
                act.wait_ge(S["nM_psum"], h + 1)
                b = bank[h % 2]
                for d, t, src, at in ((0, 0, 0, 0), (0, 1, P, 2 * P), (1, 0, SEQ, 0), (1, 1, SEQ, P)):
                    n = SEQ if (d, t) in ((0, 0), (1, 1)) else P
                    act.activation(ab_e[:, h % 2, d, at:at + n], b[:, src:src + n], ACT.Exp,
                                   bias=ab_t[:, t, d, h:h + 1]).then_inc(S["e_exp"], 1)

            def numerators(h):
                for d in range(2):
                    act.wait_ge(S["num_psum"], 2 * h + d + 1)
                    act.activation(ab_num[:, d, h], bank[4 + d][:, 0:2 * (AD + 1)].rearrange("p (t v) -> p t v", t=NT),
                                   ACT.Copy).then_inc(S["num_ready"], 1)

            def full_high(j):
                act.wait_ge(S["ab_full"], j + 1)
                k = ab_slot[j]
                act.activation(xT_hi[:, :, k, :], ab_cv[:, j, :].rearrange("p (t c) -> p t c", t=NT),
                               ACT.Copy).then_inc(S["ab_hi"], 1)

            act.wait_ge(S["g_cols_ready"], 1)
            act.activation(ab_em.rearrange("p d t h -> p t d h"), ab_t[:, :, 2:4, :], ACT.Exp, scale=-1.0).then_inc(S["g_em_ready"], 1)
            decay_weights(0)
            decay_weights(1)
            gating_u(0)
            gating_u(1)
            numerators(0)
            decay_weights(2)
            numerators(1)
            decay_weights(3)
            numerators(2)
            output_gate(0)
            output_gate(1)
            for j in range(4):
                full_high(j)
            numerators(3)
            o = sched["ab_out"]
            high_upto(o[0].index + 1 + SLOTS)
            high_upto(o[1].index + 1 + SLOTS)
            for j in range(4, 8):
                full_high(j)

            def relu_square(f, ch, i, buf, it=0):
                act.wait_ge(S["mm_done"], ch.index + 1 + 4 * it)
                if not (f == 0 and i == 0):
                    act.wait_ge(S["ff2_lo"], N2 * f + i + 2 * it)
                act.activation(ff_act[:], bank[buf][:].rearrange("p (a b) -> p a b", a=2), ACT.Relu).then_inc(S["ff2_relu"], 1)
                act.wait_ge(S["ff2_relu"], N2 * f + i + 1 + 2 * it)
                act.activation(ff_hi[buf][:], ff_act[:], ACT.Square).then_inc(S["ff2_hi"], 1)

            def squared_relu(f, after):
                c = sched[ffn_phases[f]]
                act.wait_ge(S["mm_done"], c[0].index + 1)
                act.activation(ff_act[:], bank[0][:].rearrange("p (a b) -> p a b", a=2), ACT.Relu).then_inc(S["ff2_relu"], 1)
                first_hidden_high("ff2_t", f + 1, "ff2_hi")
                high_upto(c[4].index + 1)
                relu_square(f, c[1], 1, 1)
                high_upto(c[5].index + 1)
                if f == 0:
                    act.wait_ge(S["rope_angle"], 1)
                    act.activation(sin[:], ang[:], ACT.Sin)
                    act.activation(cos[:], cosr[:], ACT.Sin).then_inc(S["rope_ready"], 1)
                with act.Fori(0, N2 // 2 - 2) as it:
                    high(c[6], it, 4)
                    relu_square(f, c[3], 2, 0, it)
                    high(c[7], it, 4)
                    high(c[8], it, 4)
                    relu_square(f, c[5], 3, 1, it)
                    high(c[9], it, 4)
                split[0] = c[-3].index + 1
                high_upto(c[-2].index + 1)
                relu_square(f, c[-5], N2 - 2, 0)
                high_upto(c[-1].index + 2)
                relu_square(f, c[-3], N2 - 1, 1)
                high_upto(c[-1].index + 1 + after)

            c = sched["ffn2a"]
            enter(3, 4, 0, c[3].index + 1)
            squared_relu(0, 2)

            c = sched["c_in"]
            enter(4, 5, c[2].index + 1, c[0].index + SLOTS)
            for t in range(NT):
                if t == 0:
                    act.wait_ge(S["c_in0_done"], 1)
                else:
                    act.wait_ge(S["mm_done"], c[2].index + 1)
                act.activation(c_lat[:, t, 0:512], bank[4 + 2 * t][:], ACT.Copy).then_inc(S["c_lat_ready"], 1)
                act.activation(c_lat[:, t, 512:CIN], bank[5 + 2 * t][:, 3 * CW - CIN:CW], ACT.Copy).then_inc(S["c_lat_ready"], 1)
                act.wait_ge(S["c_lat_ready"], 2 * t + 2)
                for j, a, b in ((0, 0, QL), (1, QL, QL + KVL)):
                    if j or t:
                        act.wait_ge(S["c_ssq"], 2 * t + j)
                    act.activation(x_norm[:, t, a:b], c_lat[:, t, a:b], ACT.Square, accum_out=c_ss[:, t, j:j + 1]).then_inc(S["c_ssq"], 1)
            high_upto(c[0].index + 1 + SLOTS)
            high_upto(c[1].index + 1 + SLOTS)
            q = sched["c_uq"]
            for t in range(NT):
                for half, n in ((0, 4), (1, 1)):
                    act.wait_ge(S["c_t_psum"], 2 * t + half + 1)
                    act.activation(xT_hi[:, t, 4 * half:4 * half + n, :].rearrange("p k c -> p (k c)"),
                                   bank[2 * t + half][:, 0:n * P], ACT.Copy).then_inc(S["c_xh"], 1)
                if t == 0:
                    high_upto(c[2].index + 1 + SLOTS)
                    for i in range(3):
                        act.wait_ge(S["c_uq0_done"], i + 1)
                        act.activation(c_q[:, 0, i * 512:(i + 1) * 512], bank[C_UQ_BANK[i][0]][:],
                                       ACT.Copy).then_inc(S["c_q_ready"], 1)
            for i in range(3):
                high_upto(q[i].index + 1 + SLOTS)
            c = sched["c_ukv"]
            for i, ch in enumerate(c):
                act.wait_ge(S["mm_done"], ch.index + 1)
                for n in range(2):
                    for src, dst in kv_parts(i, n, 0):
                        last = act.activation(dst, src, ACT.Copy)
                last.then_inc(S["c_kv_ready"], 1)
                high_upto(ch.index + 1 + SLOTS)

            def mla_probabilities(h):
                act.wait_ge(S["c_nmax"], h + 1)
                for t in range(NT):
                    act.activation(c_p[:, h % 2, t], bank[2 + h % 2][:, t * SEQ:(t + 1) * SEQ], ACT.Exp, scale=CD ** -0.5,
                                   bias=c_nm[:, h, t:t + 1], accum_out=c_sum[:, t, h:h + 1]).then_inc(S["c_probs"], 1)

            def mla_transposed_p(h):
                act.wait_ge(S["c_pt_psum"], h + 1)
                act.activation(c_pT[:, h % 2].rearrange("p a b -> p (a b)"), bank[4 + h % 2][:], ACT.Copy).then_inc(S["c_pt_ready"], 1)

            for h in range(CH + 1):
                if h < CH:
                    mla_probabilities(h)
                if h >= 1:
                    mla_transposed_p(h - 1)
            transposed_high(5, 0)
            transposed_high(5, 1)
            c = sched["c_out"]
            for ch in c[:2]:
                high_upto(ch.index + 1 + SLOTS)
            c = sched["ffn2b"]
            enter(6, 6, 0, c[3].index + 1)
            squared_relu(1, 0)
            sum_squares(7, 0)
            sum_squares(7, 1)

        @block.vector
        def _(dve):
            chain = [0]

            def step(ins):
                chain[0] += 1
                ins.then_inc(S["dve_chain"], 1)
                dve.wait_ge(S["dve_chain"], chain[0])

            split = [0]

            def low(ch, it=0, stride=0):
                dve.wait_ge(S["hi_done"], ch.index + 1 + it * stride)
                dve.tensor_tensor(view(w_lo, ch), view(w_raw, ch), view(w_hi, ch).bitcast(F32),
                                  ALU.subtract).then_inc(S["lo_done"], 1)

            def low_upto(index):
                while split[0] < min(index, n_chunks):
                    low(order[split[0]])
                    split[0] += 1

            def normalise(n, t, dst):
                dve.wait_ge(S["gain_loaded"], 16 * (n + 1))
                dve.wait_ge(S["rstd_ready"], turn[n, t])
                for d in HALF_D:
                    dve.scalar_tensor_tensor(out=dst[:, t, d], in0=x_res[:, t, d], scalar=rstd[:, t:t + 1],
                                             in1=gain[:, n % 2, d], op0=ALU.mult, op1=ALU.mult).then_inc(S["xn_ready"], 1)

            def transposed_low(n, t):
                for half in range(2):
                    dve.wait_ge(S["xTh_ready"], 4 * n + 2 * t + half + 1)
                    k = slice(4 * half, 4 * half + 4)
                    dve.tensor_tensor(xT_lo[:, t, k, :].rearrange("p k c -> p (k c)"), bank[2 * t + half][:],
                                      xT_hi[:, t, k, :].rearrange("p k c -> p (k c)").bitcast(F32),
                                      ALU.subtract).then_inc(S["xTl_ready"], 1)

            def add_residual(n, t):
                for j, d in enumerate(HALF_D):
                    if (t, j) == (1, 1):
                        dve.wait_ge(S["mm_done"], sched[phase_of_norm[n]][-1].index + 1)
                    else:
                        dve.wait_ge(S["acc_done"], 3 * additions[n] + 2 * t + j + 1)
                    dve.tensor_tensor(x_res[:, t, d], x_res[:, t, d], bank[4 + 2 * t + j][:],
                                      ALU.add).then_inc(S["resid_ready"], 1)

            def enter(use, n, early, then):
                add_residual(n, 0)
                normalise(n, 0, x_norm)
                add_residual(n, 1)
                transposed_low(use, 0)
                normalise(n, 1, x_norm)
                low_upto(early)
                transposed_low(use, 1)
                low_upto(then)

            def rope_angles():
                dve.wait_ge(S["pos_loaded"], 16)
                dve.wait_ge(S["consts_ready"], 3)
                step(dve.tensor_copy(pos_f[:], pos_i[:]))
                for t in range(NT):
                    step(dve.tensor_scalar(ang[:, t], freq[:], pos_f[:, t:t + 1], None, ALU.mult))
                magic = 1.5 * 2 ** 23
                step(dve.tensor_scalar(turns[:], ang[:], 1.0 / (2 * math.pi), magic, ALU.mult, ALU.add))
                step(dve.tensor_scalar(turns[:], turns[:], -magic, None, ALU.add))
                two_pi = (6.28125, 1.93500518798828125e-3, 3.01992e-7)
                two_pi = (two_pi[0], two_pi[1], 2 * math.pi - two_pi[0] - two_pi[1])
                for part in two_pi:
                    step(dve.scalar_tensor_tensor(out=ang[:], in0=turns[:], scalar=-part, in1=ang[:],
                                                  op0=ALU.mult, op1=ALU.add))
                limit = 3.141592
                step(dve.tensor_scalar(ang[:], ang[:], limit, -limit, ALU.min, ALU.max))
                step(dve.scalar_tensor_tensor(out=cosr[:], in0=ang[:], scalar=-1.0, in1=ang[:], op0=ALU.mult, op1=ALU.min))
                dve.tensor_scalar(cosr[:], cosr[:], math.pi / 2, None, ALU.add).then_inc(S["rope_angle"], 1)

            c = sched["swa_in"]
            normalise(0, 0, x_norm)
            low_upto(1)
            normalise(0, 1, x_norm)
            transposed_low(0, 0)
            low_upto(2)
            transposed_low(0, 1)
            low_upto(SLOTS)

            dve.wait_ge(S["mm_done"], c[1].index + 1)
            k_ps = bank[4][:].rearrange("p (f t) -> p f t", f=2)
            k_dst = swa_kT.rearrange("p (f r) t -> p f r t", r=2)
            for half in range(2):
                for dst in range(2):
                    last = dve.tensor_copy(k_dst[64 * dst:64 * dst + 64, :, half, :], k_ps[64 * half:64 * half + 64, :, :])
            last.then_inc(S["swa_k_ready"], 1)
            low_upto(c[1].index + 1 + SLOTS)
            dve.wait_ge(S["params_psum"], 1)
            dve.tensor_copy(pcols[:], bank[0][:, 0:48]).then_inc(S["params_ready"], 1)
            dve.wait_ge(S["wsT_psum"], 1)
            dve.tensor_copy(wsT[:], bank[1][:].rearrange("p (a b) -> p a b", a=BG)).then_inc(S["wsT_ready"], 1)
            dve.wait_ge(S["dist_step"], 3)
            dve.wait_ge(S["sinks_loaded"], 16)

            def swa_bias(g):
                hs = slice(4 * g, 4 * g + 4)
                if g >= 2:
                    dve.wait_ge(S["swa_pt_psum"], 3 * (g - 1))
                for at in (0, SWA_COLS + 1):
                    last = dve.tensor_copy(swa_s[:, g % 2, :, at:at + 1], sinks[:, hs].unsqueeze(2))
                for j in range(4):
                    h = 4 * g + j
                    dve.wait_ge(S["swa_scores"], h + 1)
                    slope = 2.0 ** (-8.0 * (h + 1) / NQH)
                    dve.scalar_tensor_tensor(out=swa_s[:, g % 2, j, 1:1 + SWA_COLS], in0=dist[:], scalar=-slope,
                                             in1=bank[h % 2][:, 0:SWA_COLS], op0=ALU.mult,
                                             op1=ALU.add).then_inc(S["swa_biased"], 1)
                    if j == 2 and g >= 2:
                        swa_operand(g - 2)
                dve.wait_ge(S["swa_biased"], 4 * g + 4)
                for t, (a, b) in enumerate(SWA_PARTS):
                    last = dve.tensor_reduce(swa_mx[:, t, hs], swa_s[:, g % 2, :, a:b], axis=AX, op=ALU.max)
                step(last)
                dve.tensor_scalar(swa_nm[:, :, hs], swa_mx[:, :, hs], -1.0, None, ALU.mult).then_inc(S["swa_nmax"], 1)

            def swa_output(g):
                hs = slice(4 * g, 4 * g + 4)
                dve.wait_ge(S["swa_probs"], 8 * (g + 1))
                step(dve.reciprocal(swa_rden[:, :, hs], swa_sum[:, :, hs]))
                dve.wait_ge(S["swa_o_psum"], g + 1)
                for t in range(NT):
                    r = swa_rden[:, t, hs].unsqueeze(2).broadcast_to([P, 4, HD])
                    dve.tensor_tensor(x_norm[:, t, 256 * g:256 * g + 256].rearrange("p (h d) -> p h d", d=HD),
                                      bank[3][:, 256 * t:256 * t + 256].rearrange("p (h d) -> p h d", d=HD), r,
                                      ALU.mult).then_inc(S["swa_o_ready"], 1)

            def swa_operand(g):
                dve.wait_ge(S["swa_oh_ready"], g + 1)
                k = slice(2 * g, 2 * g + 2)
                dve.tensor_tensor(xT_lo[:, :, k, :], bank[3][:].rearrange("p (t k c) -> p t k c", t=NT, k=2),
                                  xT_hi[:, :, k, :].bitcast(F32), ALU.subtract).then_inc(S["swa_ol_ready"], 1)

            o = sched["swa_out"]
            swa_bias(0)
            low_upto(c[2].index + 1 + SLOTS)
            swa_bias(1)
            low_upto(c[3].index + 1 + SLOTS)
            swa_output(0)
            swa_bias(2)
            low_upto(c[4].index + 1 + SLOTS)
            swa_output(1)
            swa_bias(3)
            low_upto(c[5].index + 1 + SLOTS)
            swa_output(2)
            low_upto(o[0].index + 1 + SLOTS)
            swa_operand(2)
            low_upto(o[1].index + 1 + SLOTS)
            swa_output(3)
            swa_operand(3)

            c = sched["ffn1"]

            def hidden(ch, i, it=0, buf=0):
                dve.wait_ge(S["ff1_sg"], i + 1 + it)
                dve.wait_ge(S["mm_done"], ch.index + 1 + 3 * it)
                dve.tensor_tensor(ff_h[:], ff_act[:], bank[1][:].rearrange("p (a b) -> p a b", a=2),
                                  ALU.mult).then_inc(S["ff1_h"], 1)
                dve.wait_ge(S["ff1_hi"], i + 1 + it)
                dve.tensor_tensor(ff_lo[buf][:], ff_h[:], ff_hi[buf][:].bitcast(F32), ALU.subtract).then_inc(S["ff1_lo"], 1)

            def first_hidden_low(high, count, ready):
                dve.wait_ge(S[high], count)
                dve.tensor_tensor(ff_lo[0][:], bank[2][:].rearrange("p (a b) -> p a b", a=2),
                                  ff_hi[0][:].bitcast(F32), ALU.subtract).then_inc(S[ready], 1)

            enter(1, 1, 0, c[3].index + 1)
            dve.wait_ge(S["ff1_sg"], 1)
            dve.wait_ge(S["mm_done"], c[1].index + 1)
            dve.tensor_tensor(ff_h[:], ff_act[:], bank[1][:].rearrange("p (a b) -> p a b", a=2),
                              ALU.mult).then_inc(S["ff1_h"], 1)
            first_hidden_low("ff1_hi", 1, "ff1_lo")
            low_upto(c[4].index + 1)
            low(c[5])
            low(c[6])
            hidden(c[4], 1)
            low(c[7])
            with dve.Fori(0, N1 - 4) as it:
                low(c[8], it, 3)
                low(c[9], it, 3)
                hidden(c[7], 2, it)
                low(c[10], it, 3)
            low(c[-4])
            hidden(c[-5], N1 - 2)
            for ch in c[-3:]:
                low(ch)
            hidden(c[-3], N1 - 1, buf=1)
            split[0] = c[-1].index + 1
            low_upto(c[-1].index + 1 + 2)

            c = sched["ab_in"]
            add_residual(2, 0)
            normalise(2, 0, x_res)
            normalise(3, 0, x_norm)
            add_residual(2, 1)
            transposed_low(2, 0)
            normalise(2, 1, x_res)
            low_upto(c[2].index + 1)
            normalise(3, 1, x_norm)
            transposed_low(2, 1)
            low_upto(c[0].index + SLOTS)
            dve.wait_ge(S["params_ready"], 1)
            for ch in c[0:3]:
                low_upto(ch.index + 1 + SLOTS)

            def conv(i):
                dve.wait_ge(S["qk_padded"], i + 1)
                for j in range(CONV):
                    for f in (2 * i, 2 * i + 1):
                        w = pcols[:, 8 * j + f:8 * j + f + 1]
                        src = ab_pad[:, f, j:j + SEQ]
                        if j == 0:
                            ins = dve.tensor_scalar(ab_cv[:, f], src, w, None, ALU.mult)
                        else:
                            ins = dve.scalar_tensor_tensor(out=ab_cv[:, f], in0=src, scalar=w, in1=ab_cv[:, f],
                                                           op0=ALU.mult, op1=ALU.add)
                    if j < CONV - 1:
                        step(ins)
                    else:
                        ins.then_inc(S["conv_ready"], 1)

            conv(0)
            low_upto(c[3].index + 1 + SLOTS)
            dve.wait_ge(S["g4_loaded"], 64)
            forget = g4[:, 1:4:2, :]
            dve.scalar_tensor_tensor(out=g_w, in0=forget, scalar=-1.0, in1=forget, op0=ALU.mult,
                                     op1=ALU.min).then_inc(S["g_abs_ready"], 1)
            def gate_rows():
                dve.wait_ge(S["g_ln_ready"], 1)
                step(dve.scalar_tensor_tensor(out=g_w, in0=g4[:, 1:4:2, :], scalar=0.0, in1=g_w,
                                              op0=ALU.min, op1=ALU.subtract))
                ways = (slice(None), slice(None, None, -1))
                for d, w in enumerate(ways):
                    last = dve.tensor_tensor_scan(g_B[:, d, w], one[:].broadcast_to([AH, SEQ]), g_w[:, d, w], 0.0, ALU.mult, ALU.add)
                step(last)
                step(dve.tensor_tensor(g_am[:, 0:2], g4[:, 0:4:2, :], g_B, ALU.subtract))
                for d, w in enumerate(ways):
                    last = dve.tensor_tensor_scan(g_M[:, d, w], g_am[:, d, w], g_am[:, d, w], 0.0, ALU.max, ALU.max)
                step(last)
                dve.tensor_tensor(g_am[:, 2:4], g_B, g_M, ALU.add)
                dve.tensor_scalar(g_nM, g_M, -1.0, None, ALU.mult).then_inc(S["g_rows_ready"], 1)

            for i in range(1, 4):
                conv(i)
                low_upto(c[3 + i].index + 1 + SLOTS)
                if i == 1:
                    gate_rows()
            low_upto(c[7].index + 1 + SLOTS)
            low_upto(c[8].index + 1 + SLOTS)
            dve.wait_ge(S["g_cols_psum"], 1)
            dve.tensor_copy(ab_t.rearrange("p t k h -> p (t k h)"), bank[1][:, 0:32]).then_inc(S["g_cols_ready"], 1)
            dve.wait_ge(S["vb_ready"], 2)
            vb = ab_vb.rearrange("p t (g c) -> p (t g) c", c=P)
            step(dve.tensor_tensor(ab_sq[:], vb, vb, ALU.mult))
            dve.tensor_reduce(ab_ss[:], ab_sq[:], axis=AX, op=ALU.add).then_inc(S["vb_sumsq"], 1)

            def weighted_scores(h):
                dve.wait_ge(S["st_psum"], h + 1)
                dve.wait_ge(S["e_ready"], 4 * (h + 1))
                b = bank[2 + h % 2]
                for d, src, at, n in ((0, 0, 0, SEQ), (0, SEQ + P, 2 * P, P), (1, 0, 0, P), (1, SEQ, P, SEQ)):
                    e = ab_e[:, h % 2, d, at:at + n]
                    last = dve.scalar_tensor_tensor(out=e, in0=b[:, src:src + n], scalar=AD ** -0.5, in1=e,
                                                    op0=ALU.mult, op1=ALU.mult)
                last.then_inc(S["w_ready"], 1)

            def full_low(j):
                dve.wait_ge(S["ab_hi"], j + 1)
                k = ab_slot[j]
                dve.tensor_tensor(xT_lo[:, :, k, :], ab_cv[:, j, :].rearrange("p (t c) -> p t c", t=NT),
                                  xT_hi[:, :, k, :].bitcast(F32), ALU.subtract).then_inc(S["ab_lo"], 1)

            weighted_scores(0)
            dve.wait_ge(S["vb_rstd"], 1)
            dve.tensor_tensor(vb, vb, ab_rs.unsqueeze(2).broadcast_to([P, 8, P]), ALU.mult).then_inc(S["vn_ready"], 1)
            low_upto(c[9].index + 1 + SLOTS)
            weighted_scores(1)
            low_upto(c[10].index + 1 + SLOTS)
            weighted_scores(2)
            dve.wait_ge(S["sp_psum"], 1)
            dve.wait_ge(S["u_ready"], 2)
            dve.wait_ge(S["ws_loaded"], 32)
            dve.wait_ge(S["qk_ready"], 1)
            for g in range(BG):
                sp_out = bank[6 + g // 2][:, (g % 2) * SEQ:(g % 2) * SEQ + SEQ].rearrange("p (n t) -> p n t", n=NT)
                last = dve.scalar_tensor_tensor(out=ab_sq[:, 2 * g:2 * g + 2, :], in0=sp_out, scalar=pcols[:, 44 + g:45 + g],
                                                in1=bs_all[:, g:g + 1, :].broadcast_to([P, NT, P]),
                                                op0=ALU.mult, op1=ALU.add)
                last.then_inc(S["sp_read"], 1)
            dve.wait_ge(S["sp_read"], BG)
            for g in range(BG):
                dve.tensor_tensor(ab_cv[:, g].rearrange("p (n t) -> p n t", n=NT), ab_sq[:, 2 * g:2 * g + 2, :],
                                  ab_u[:, g].rearrange("p (n t) -> p n t", n=NT), ALU.mult).then_inc(S["ab_full"], 1)
            weighted_scores(3)
            low_upto(c[11].index + 1 + SLOTS)
            for j in range(4):
                full_low(j)

            dve.wait_ge(S["num_ready"], 8)
            dve.wait_ge(S["g_em_ready"], 1)
            for d in range(2):
                den = ab_num[:, d, :, :, AD]
                step(dve.scalar_tensor_tensor(out=ab_dd[:, d], in0=den, scalar=-1.0, in1=den,
                                              op0=ALU.mult, op1=ALU.max))
                step(dve.tensor_tensor(ab_dd[:, d], ab_dd[:, d], ab_em[:, d].rearrange("p t h -> p h t"), ALU.max))
            step(dve.reciprocal(ab_rd[:], ab_dd[:]))
            for d in range(2):
                n = ab_num[:, d, :, :, 0:AD]
                last = dve.tensor_tensor(n, n, ab_rd[:, d].unsqueeze(3).broadcast_to([P, AH, NT, AD]), ALU.mult)
            step(last)
            hsum = ab_num[:, 0, :, :, 0:AD]
            step(dve.tensor_tensor(hsum, hsum, ab_num[:, 1, :, :, 0:AD], ALU.add))
            sq = ab_sq.rearrange("p (h t) c -> p h t c", t=NT)
            step(dve.tensor_tensor(sq, hsum, hsum, ALU.mult))
            dve.tensor_reduce(ab_ss, ab_sq[:], axis=AX, op=ALU.add).then_inc(S["h_sumsq"], 1)
            low_upto(c[12].index + 1 + SLOTS)
            dve.wait_ge(S["h_rstd"], 1)
            rs = ab_rs.rearrange("p (h t) -> p h t", t=NT).unsqueeze(3).broadcast_to([P, AH, NT, AD])
            dve.tensor_tensor(sq, hsum, rs, ALU.mult).then_inc(S["hn_ready"], 1)
            dve.wait_ge(S["sig_ready"], 2)
            for h in range(AH):
                dve.wait_ge(S["hT_psum"], h // 2 + 1)
                dve.scalar_tensor_tensor(out=ab_cv[:, 4 + h], in0=bank[2 + h // 2][:, (h % 2) * SEQ:(h % 2) * SEQ + SEQ],
                                         scalar=pcols[:, 40 + h:41 + h], in1=ab_sig[:, h],
                                         op0=ALU.mult, op1=ALU.mult).then_inc(S["ab_full"], 1)
            for j in range(4, 8):
                full_low(j)
            o = sched["ab_out"]
            low_upto(o[0].index + 1 + SLOTS)
            low_upto(o[1].index + 1 + SLOTS)
            enter(3, 4, 0, sched["ffn2a"][3].index + 1)

            def hidden2(f, i, buf, it=0):
                dve.wait_ge(S["ff2_relu"], N2 * f + i + 1 + 2 * it)
                dve.tensor_tensor(ff_h[:], ff_act[:], ff_act[:], ALU.mult).then_inc(S["ff2_h"], 1)
                dve.wait_ge(S["ff2_h"], N2 * f + i + 1 + 2 * it)
                dve.wait_ge(S["ff2_hi"], N2 * f + i + 1 + 2 * it)
                dve.tensor_tensor(ff_lo[buf][:], ff_h[:], ff_hi[buf][:].bitcast(F32), ALU.subtract).then_inc(S["ff2_lo"], 1)

            def squared_relu(f, after):
                c = sched[ffn_phases[f]]
                dve.wait_ge(S["ff2_relu"], N2 * f + 1)
                dve.tensor_tensor(ff_h[:], ff_act[:], ff_act[:], ALU.mult).then_inc(S["ff2_h"], 1)
                first_hidden_low("ff2_hi", N2 * f + 1, "ff2_lo")
                low_upto(c[4].index + 1)
                hidden2(f, 1, 1)
                low_upto(c[5].index + 1)
                if f == 0:
                    rope_angles()
                with dve.Fori(0, N2 // 2 - 2) as it:
                    low(c[6], it, 4)
                    hidden2(f, 2, 0, it)
                    low(c[7], it, 4)
                    low(c[8], it, 4)
                    hidden2(f, 3, 1, it)
                    low(c[9], it, 4)
                split[0] = c[-3].index + 1
                low_upto(c[-2].index + 1)
                hidden2(f, N2 - 2, 0)
                low_upto(c[-1].index + 2)
                hidden2(f, N2 - 1, 1)
                low_upto(c[-1].index + 1 + after)

            squared_relu(0, 2)

            c = sched["c_in"]
            enter(4, 5, c[2].index + 1, c[0].index + SLOTS)
            low_upto(c[0].index + 1 + SLOTS)
            low_upto(c[1].index + 1 + SLOTS)
            dve.wait_ge(S["rope_ready"], 1)
            dve.wait_ge(S["cgain_loaded"], 32)

            def latents(t):
                dve.wait_ge(S["c_rstd"], t + 1)
                for j, a, b in ((0, 0, QL), (1, QL, QL + KVL)):
                    dve.scalar_tensor_tensor(out=x_norm[:, t, a:b], in0=c_lat[:, t, a:b], scalar=c_rs[:, t, j:j + 1],
                                             in1=c_gain[:, a:b], op0=ALU.mult, op1=ALU.mult).then_inc(S["c_cn_ready"], 1)

            def latents_low(t):
                for half, n in ((0, 4), (1, 1)):
                    dve.wait_ge(S["c_xh"], 2 * t + half + 1)
                    k = slice(4 * half, 4 * half + n)
                    dve.tensor_tensor(xT_lo[:, t, k, :].rearrange("p k c -> p (k c)"), bank[2 * t + half][:, 0:n * P],
                                      xT_hi[:, t, k, :].rearrange("p k c -> p (k c)").bitcast(F32),
                                      ALU.subtract).then_inc(S["c_xl"], 1)

            def rope_key(t):
                x1, x2 = c_lat[:, t, QL + KVL:QL + KVL + HALF], c_lat[:, t, QL + KVL + HALF:CIN]
                dve.tensor_tensor(c_krt[:, 0, t], x1, cos[:, t], ALU.mult)
                dve.tensor_tensor(c_krt[:, 1, t], x2, sin[:, t], ALU.mult)
                dve.tensor_tensor(c_krt[:, 2, t], x1, sin[:, t], ALU.mult)
                step(dve.tensor_tensor(c_krt[:, 3, t], x2, cos[:, t], ALU.mult))
                dve.tensor_tensor(c_kr[:, t, 0:HALF], c_krt[:, 0, t], c_krt[:, 1, t], ALU.subtract)
                step(dve.tensor_tensor(c_kr[:, t, HALF:CR], c_krt[:, 2, t], c_krt[:, 3, t], ALU.add))
                kr_all = c_k[:, t].rearrange("p (h e) -> p h e", e=CD)[:, :, CN:CD]
                step(dve.tensor_copy(kr_all, c_kr[:, t:t + 1, :].broadcast_to([P, CH, CR])))

            latents(0)
            latents_low(0)
            latents(1)
            low_upto(c[2].index + 1 + SLOTS)
            latents_low(1)
            rope_key(0)
            rope_key(1)
            c = sched["c_uq"]
            for i, ch in enumerate(c):
                dve.wait_ge(S["mm_done"], ch.index + 1)
                t = 1
                dve.tensor_copy(c_q[:, t, i * 512:(i + 1) * 512], bank[C_UQ_BANK[i][t]][:]).then_inc(S["c_q1_ready"], 1)
                low_upto(ch.index + 1 + SLOTS)
            dve.wait_ge(S["c_q_ready"], 3)
            dve.wait_ge(S["c_q1_ready"], 3)

            def rope_q(t):
                q = c_q[:, t].rearrange("p (h e) -> p h e", e=CD)
                x1, x2 = q[:, :, CN:CN + HALF], q[:, :, CN + HALF:CD]
                cs = cos[:, t:t + 1, :].broadcast_to([P, CH, HALF])
                sn = sin[:, t:t + 1, :].broadcast_to([P, CH, HALF])
                tmp = [c_tmp[:, i].rearrange("p (h e) -> p h e", e=HALF) for i in range(4)]
                dve.tensor_tensor(tmp[0], x1, cs, ALU.mult)
                dve.tensor_tensor(tmp[1], x2, sn, ALU.mult)
                dve.tensor_tensor(tmp[2], x1, sn, ALU.mult)
                step(dve.tensor_tensor(tmp[3], x2, cs, ALU.mult))
                dve.tensor_tensor(x1, tmp[0], tmp[1], ALU.subtract)
                ins = dve.tensor_tensor(x2, tmp[2], tmp[3], ALU.add)
                if t == 0:
                    step(ins)
                else:
                    ins.then_inc(S["c_rope_ready"], 1)

            def values(i, ch):
                dve.wait_ge(S["mm_done"], ch.index + 1)
                for n in range(2):
                    for src, dst in kv_parts(i, n, 1):
                        last = dve.tensor_copy(dst, src)
                last.then_inc(S["c_kv_ready"], 1)
                low_upto(ch.index + 1 + SLOTS)

            rope_q(0)
            values(0, sched["c_ukv"][0])
            rope_q(1)
            values(1, sched["c_ukv"][1])

            def mla_qk(h):
                dve.wait_ge(S["c_qkT_psum"], h + 1)
                dve.tensor_copy(c_qkT[0:CD, h % 2].rearrange("p a b -> p (a b)"), bank[h % 2][0:CD, :]).then_inc(S["c_qkT_ready"], 1)

            def mla_max(h):
                dve.wait_ge(S["c_scores"], h + 1)
                step(dve.tensor_reduce(c_mx[:, h], bank[2 + h % 2][:].rearrange("p (t k) -> p t k", t=NT), axis=AX, op=ALU.max))
                dve.tensor_scalar(c_nm[:, h], c_mx[:, h], -(CD ** -0.5), None, ALU.mult).then_inc(S["c_nmax"], 1)

            def mla_output(half):
                dve.wait_ge(S["c_o_psum"], 8 * half + 8)
                hs = slice(8 * half, 8 * half + 8)
                step(dve.reciprocal(c_rden[:, :, hs], c_sum[:, :, hs]))
                for t in range(NT):
                    r = c_rden[:, t, hs].unsqueeze(2).broadcast_to([P, 8, CV])
                    dve.tensor_tensor(x_norm[:, t, 512 * half:512 * half + 512].rearrange("p (h d) -> p h d", d=CV),
                                      bank[6 + t][:].rearrange("p (h d) -> p h d", d=CV), r, ALU.mult).then_inc(S["c_o_ready"], 1)

            for h in range(CH + 1):
                if h < CH:
                    mla_qk(h)
                if h >= 1:
                    mla_max(h - 1)
                if h == 10:
                    mla_output(0)
            mla_output(1)
            transposed_low(5, 0)
            transposed_low(5, 1)
            c = sched["c_out"]
            low_upto(c[0].index + 1 + SLOTS)
            low_upto(c[1].index + 1 + SLOTS)
            enter(6, 6, 0, sched["ffn2b"][3].index + 1)
            squared_relu(1, 0)
            for t in range(NT):
                add_residual(7, t)
                normalise(7, t, x_norm)

        @block.tensor
        def _(pe):
            def product(out, sh, sl, mh, ml, first, last):
                pe.matmul(out, sh, mh, start=first, stop=False)
                pe.matmul(out, sh, ml, start=False, stop=False)
                return pe.matmul(out, sl, mh, start=False, stop=last)

            def arrived(ch, it=0, stride=0):
                pe.wait_ge(S["lo_done"], ch.index + 1 + it * stride)

            def feature_major(ch, dst, between=None):
                hi, lo = view(w_hi, ch), view(w_lo, ch)
                n = ch.shape[1]
                for f in range(max(1, n // P)):
                    w = min(n, P)
                    o = dst[0:w, f * SEQ:(f + 1) * SEQ].rearrange("p (t c) -> p t c", t=NT)
                    if f == 1 and between:
                        between()
                    for k in range(KT):
                        last = product(o, hi[:, k, f * w:(f + 1) * w], lo[:, k, f * w:(f + 1) * w],
                                       xT_hi[:, :, k, :], xT_lo[:, :, k, :], k == 0, k == KT - 1)
                last.then_inc(S["mm_done"], 1)

            def token_major(ch, dst, kts=KT, k0=0, ts=(0, 1), tile0=None):
                hi, lo = view(w_hi, ch), view(w_lo, ch)
                for t in ts:
                    for k in range(kts):
                        last = product(dst[t], xT_hi[:, t, k0 + k, :], xT_lo[:, t, k0 + k, :], hi[:, k, :], lo[:, k, :],
                                       k == 0, k == kts - 1)
                    if t == 0 and tile0:
                        last.then_inc(S[tile0], 1)
                    if t == NT - 1:
                        last.then_inc(S["mm_done"], 1)

            def accumulate(ch, stat_hi, stat_lo, first=False, end=False, ts=(0, 1), phase_end=False):
                hi, lo = view(w_hi, ch), view(w_lo, ch)
                for t in ts:
                    for j in range(2):
                        for k in range(2):
                            last = product(bank[4 + 2 * t + j][:], stat_hi(t, k), stat_lo(t, k),
                                           hi[:, k, 512 * j:512 * j + 512], lo[:, k, 512 * j:512 * j + 512],
                                           first and k == 0, end and k == 1)
                        if phase_end and (t, j) != (1, 1):
                            last.then_inc(S["acc_done"], 1)
                    if t == NT - 1:
                        last.then_inc(S["mm_done"], 1)

            def operand_out(ch, i, **more):
                arrived(ch)
                accumulate(ch, lambda t, k: xT_hi[:, t, 2 * i + k, :], lambda t, k: xT_lo[:, t, 2 * i + k, :], **more)

            def transpose_tile(t, n=None):
                for half in range(2):
                    if n is not None:
                        pe.wait_ge(S["xn_ready"], half_turn(n, t, half))
                    for k in range(4):
                        kk = 4 * half + k
                        last = pe.transpose(bank[2 * t + half][:, k * P:(k + 1) * P],
                                            x_norm[:, t, kk * P:(kk + 1) * P], ident[:])
                    last.then_inc(S["t_psum"], 1)

            def enter(use, n, visits=()):
                transpose_tile(0, n)
                if visits:
                    pe.wait_ge(S["xTl_ready"], 4 * use + 2)
                    visits[0](0)
                transpose_tile(1, n)
                for visit in visits[1:]:
                    visit(0)
                pe.wait_ge(S["xTl_ready"], 4 * use + 4)
                for visit in visits:
                    visit(1)

            def whole(ch, dst, **more):
                arrived(ch)
                feature_major(ch, dst, **more)

            def hidden_transposes(ready, count, done):
                def blocks():
                    pe.wait_ge(S[ready], count)
                    for k in range(2):
                        for t in range(NT):
                            at = (NT * k + t) * P
                            last = pe.transpose(bank[2][:, at:at + P], ff_h[:, t, k * P:(k + 1) * P], ident[:])
                    last.then_inc(S[done], 1)
                return blocks

            def halves(b):
                return [bank[b][:, t * CW:(t + 1) * CW] for t in range(NT)]

            def by_tile(ch, dst, **more):
                def visit(t):
                    if t == 0:
                        arrived(ch)
                    token_major(ch, dst, ts=(t,), **more)
                return visit

            pe.wait_ge(S["consts_ready"], 1)
            c = sched["swa_in"]

            enter(0, 0, [by_tile(c[0], halves(5))])
            whole(c[1], bank[4])

            def swa_queries(i):
                arrived(c[2 + i])
                if i == 2:
                    pe.wait_ge(S["swa_k_ready"], 1)
                if i == 3:
                    pe.wait_ge(S["swa_v_ready"], 1)
                feature_major(c[2 + i], bank[(6, 7, 4, 5)[i]])

            swa_queries(0)
            pe.wait_ge(S["consts_ready"], 2)
            pe.wait_ge(S["small_loaded"], 64)
            pe.transpose(bank[0][:, 0:48], prows, ident[0:48, 0:48]).then_inc(S["params_psum"], 1)
            pe.wait_ge(S["ws_loaded"], 32)
            for g in range(BG):
                last = pe.transpose(bank[1][:, g * P:(g + 1) * P], ws[:, g, :], ident[:])
            last.then_inc(S["wsT_psum"], 1)
            swa_queries(1)
            pe.wait_ge(S["params_ready"], 1)
            pe.wait_ge(S["wsT_ready"], 1)

            def swa_scores(h):
                pe.wait_ge(S["swa_q_ready"], h // 4 + 1)
                if h >= 2:
                    pe.wait_ge(S["swa_biased"], h - 1)
                at = slice(64 * (h % 2), 64 * (h % 2) + 64)
                b = bank[h % 2]
                kv = h // (NQH // NKV)
                pe.matmul(b[:, 0:P], swa_qT[at, h // 2, 0:P], swa_kT[at, kv, 0:P], start=True, stop=True)
                pe.matmul(b[:, P:SWA_COLS], swa_qT[at, h // 2, P:SEQ], swa_kT[at, kv, :],
                          start=True, stop=True).then_inc(S["swa_scores"], 1)

            def swa_transposes(g, u):
                n = 3 * g + u
                if u == 0:
                    pe.wait_ge(S["swa_probs"], 8 * (g + 1))
                if n >= 1 and SWA_PT_BANK[g][u] == 2:
                    pe.wait_ge(S["swa_pt_ready"], n)
                for b in range(4):
                    j, part = (4 * u + b) // 3, (4 * u + b) % 3
                    last = pe.transpose(bank[SWA_PT_BANK[g][u]][:, b * P:(b + 1) * P],
                                        swa_s[:, g % 2, j, 1 + part * P:1 + (part + 1) * P], ident[:])
                last.then_inc(S["swa_pt_psum"], 1)

            def scores_and_transposes(g):
                for j in range(4):
                    if g + 1 < 4:
                        swa_scores(4 * (g + 1) + j)
                    if j == 2 and g >= 1:
                        swa_operand(g - 1)
                    if 0 <= g and j < 3:
                        swa_transposes(g, j)

            def swa_values(g):
                pe.wait_ge(S["swa_pt_ready"], 3 * (g + 1))
                if g >= 1:
                    pe.wait_ge(S["swa_ol_ready"], g)
                v = [swa_v[:, t, g * HD:(g + 1) * HD] for t in range(NT)]
                pt = swa_pT[:, g % 2]
                for j in range(4):
                    o = [bank[3][:, CW * t + j * HD:CW * t + (j + 1) * HD] for t in range(NT)]
                    pe.matmul(o[0], pt[:, 3 * j, :], v[0], start=True, stop=True)
                    pe.matmul(o[1], pt[:, 3 * j + 1, :], v[0], start=True, stop=False)
                    last = pe.matmul(o[1], pt[:, 3 * j + 2, :], v[1], start=False, stop=True)
                last.then_inc(S["swa_o_psum"], 1)

            def swa_operand(g):
                pe.wait_ge(S["swa_o_ready"], 2 * (g + 1))
                for t in range(NT):
                    for k in range(2):
                        at = (2 * t + k) * P
                        kk = 2 * g + k
                        last = pe.transpose(bank[3][:, at:at + P], x_norm[:, t, kk * P:(kk + 1) * P], ident[:])
                last.then_inc(S["swa_oT_psum"], 1)

            o = sched["swa_out"]
            pe.wait_ge(S["swa_k_ready"], 1)
            scores_and_transposes(-1)
            swa_queries(2)
            scores_and_transposes(0)
            swa_queries(3)
            pe.wait_ge(S["swa_v_ready"], 1)
            swa_values(0)
            scores_and_transposes(1)
            pe.wait_ge(S["swa_q_ready"], 4)
            swa_values(1)
            operand_out(o[0], 0, first=True)
            scores_and_transposes(2)
            swa_values(2)
            operand_out(o[1], 1)
            scores_and_transposes(3)
            swa_values(3)
            operand_out(o[2], 2, ts=(0,))
            swa_operand(3)
            pe.wait_ge(S["swa_ol_ready"], 4)
            operand_out(o[3], 3, ts=(0,), end=True, phase_end=True)
            operand_out(o[2], 2, ts=(1,))
            operand_out(o[3], 3, ts=(1,), end=True, phase_end=True)

            c = sched["ffn1"]

            def down(ch, i, it=0, buf=0, **more):
                arrived(ch, it, 3)
                pe.wait_ge(S["ff1_lo"], i + 1 + it)
                accumulate(ch, lambda t, k: ff_hi[buf][:, k, t * P:(t + 1) * P],
                           lambda t, k: ff_lo[buf][:, k, t * P:(t + 1) * P], **more)

            def gate(ch, i, it=0, **more):
                arrived(ch, it, 3)
                pe.wait_ge(S["ff1_sg"], i + it)
                feature_major(ch, bank[0], **more)

            enter(1, 1, [by_tile(c[0], halves(0)), by_tile(c[1], halves(1))])
            gate(c[2], 1, between=hidden_transposes("ff1_h", 1, "ff1_t"))
            down(c[3], 0, first=True)
            arrived(c[4])
            feature_major(c[4], bank[1])
            with pe.Fori(0, N1 - 3) as it:
                gate(c[5], 2, it)
                down(c[6], 1, it)
                arrived(c[7], it, 3)
                feature_major(c[7], bank[1])
            gate(c[-4], N1 - 1)
            arrived(c[-3])
            pe.wait_ge(S["ff1_h"], N1 - 1)
            feature_major(c[-3], bank[1])
            down(c[-2], N1 - 2, ts=(0,))
            down(c[-1], N1 - 1, buf=1, ts=(0,), end=True, phase_end=True)
            down(c[-2], N1 - 2, ts=(1,))
            down(c[-1], N1 - 1, buf=1, ts=(1,), end=True, phase_end=True)

            c = sched["ab_in"]

            def projection(i):
                arrived(c[i])
                if i in (7, 8):
                    token_major(c[i], halves(AB_BANK[i]))
                else:
                    feature_major(c[i], bank[AB_BANK[i]])

            enter(2, 3, [by_tile(c[i], halves(AB_BANK[i])) for i in range(2)])
            for i in range(2, 9):
                if i == 8:
                    pe.wait_ge(S["g_raw_ready"], 1)
                projection(i)
                if i == 8:
                    pe.wait_ge(S["g_rows_ready"], 1)
                    pe.wait_ge(S["qk_padded"], 1)
                    for t in range(NT):
                        for k in range(4):
                            at = 16 * t + 4 * k
                            last = pe.transpose(bank[1][:, at:at + 4], g_am[:, k, t * P:(t + 1) * P], ident[0:AH, 0:AH])
                    last.then_inc(S["g_cols_psum"], 1)

            def decay_rows(h):
                if h == 0:
                    pe.wait_ge(S["vb_ready"], 2)
                if h == 1:
                    pe.wait_ge(S["g_cols_ready"], 1)
                if h >= 2:
                    pe.wait_ge(S["e_exp"], 4 * (h - 1))
                pe.matmul(bank[h % 2][:], sel[:, h, :], g_nM.rearrange("p d t -> p (d t)"),
                          start=True, stop=True).then_inc(S["nM_psum"], 1)

            def scores_T(h):
                if h == 0:
                    pe.wait_ge(S["qk_ready"], 1)
                    pe.wait_ge(S["v1_ready"], 2)
                if h >= 2:
                    pe.wait_ge(S["w_ready"], h - 1)
                b = bank[2 + h % 2]
                q, k = ab_pad[:, h, 0:SEQ], ab_pad[:, AH + h, 0:SEQ]
                pe.matmul(b[:, 0:SEQ], k[:, 0:P], q, start=True, stop=True)
                pe.matmul(b[:, SEQ:2 * SEQ], k[:, P:SEQ], q, start=True, stop=True).then_inc(S["st_psum"], 1)

            def summed(h):
                pe.wait_ge(S["w_ready"], h + 1)
                for d in range(2):
                    if h == 0:
                        pe.wait_ge(S["v1_ready"], 2)
                    else:
                        pe.wait_ge(S["num_ready"], 2 * (h - 1) + d + 1)
                    b = bank[4 + d]
                    w = ab_e[:, h % 2, d]
                    blocks = ((0, ((0, 0),)), (1, ((0, P), (1, 2 * P)))) if d == 0 else ((0, ((0, 0), (1, P))), (1, ((1, 2 * P),)))
                    for t, srcs in blocks:
                        for m, (s, at) in enumerate(srcs):
                            last = pe.matmul(b[:, t * (AD + 1):(t + 1) * (AD + 1)], w[:, at:at + P], ab_v1[:, s, h, :],
                                             start=m == 0, stop=m == len(srcs) - 1)
                    last.then_inc(S["num_psum"], 1)

            def spatial_mixing():
                pe.wait_ge(S["vn_ready"], 1)
                pe.wait_ge(S["u_ready"], 2)
                for g in range(BG):
                    for n in range(NT):
                        at = (g % 2) * SEQ + n * P
                        last = pe.matmul(bank[6 + g // 2][:, at:at + P], ab_vb[:, n, g * P:(g + 1) * P], wsT[:, g, :],
                                         start=True, stop=True)
                last.then_inc(S["sp_psum"], 1)

            decay_rows(0)
            scores_T(0)
            pe.wait_ge(S["qk_padded"], 4)
            decay_rows(1)
            pe.wait_ge(S["v1_ready"], 1)
            projection(9)
            scores_T(1)
            summed(0)
            projection(10)
            decay_rows(2)
            scores_T(2)
            summed(1)
            spatial_mixing()
            decay_rows(3)
            scores_T(3)
            summed(2)
            pe.wait_ge(S["sp_read"], BG)
            projection(11)
            projection(12)
            summed(3)
            o = sched["ab_out"]
            pe.wait_ge(S["ab_lo"], 4)
            pe.wait_ge(S["num_ready"], 8)
            pe.wait_ge(S["sig_ready"], 2)
            operand_out(o[0], AB_OUT_ORDER[0], first=True)
            operand_out(o[1], AB_OUT_ORDER[1])
            pe.wait_ge(S["hn_ready"], 1)
            for h in range(AH):
                for t in range(NT):
                    at = (h % 2) * SEQ + t * P
                    last = pe.transpose(bank[2 + h // 2][:, at:at + P], ab_sq[:, 2 * h + t, :], ident[:])
                if h % 2:
                    last.then_inc(S["hT_psum"], 1)
            pe.wait_ge(S["ab_lo"], 8)
            for t in range(NT):
                operand_out(o[2], AB_OUT_ORDER[2], ts=(t,))
                operand_out(o[3], AB_OUT_ORDER[3], ts=(t,), end=True, phase_end=True)

            def up2(ch, buf, it=0):
                arrived(ch, it, 4)
                feature_major(ch, bank[buf])

            def down2(f, ch, i, buf, it=0, **more):
                arrived(ch, it, 4)
                pe.wait_ge(S["ff2_lo"], N2 * f + i + 1 + 2 * it)
                accumulate(ch, lambda t, k: ff_hi[buf][:, k, t * P:(t + 1) * P],
                           lambda t, k: ff_lo[buf][:, k, t * P:(t + 1) * P], **more)

            def squared_relu(f, use, n):
                c = sched[ffn_phases[f]]
                enter(use, n, [by_tile(c[0], halves(0))])
                whole(c[1], bank[1], between=hidden_transposes("ff2_h", N2 * f + 1, "ff2_t"))
                down2(f, c[2], 0, 0, first=True)
                up2(c[3], 0)
                down2(f, c[4], 1, 1)
                up2(c[5], 1)
                with pe.Fori(0, N2 // 2 - 2) as it:
                    down2(f, c[6], 2, 0, it)
                    up2(c[7], 0, it)
                    down2(f, c[8], 3, 1, it)
                    up2(c[9], 1, it)
                for t in range(NT):
                    down2(f, c[-2], N2 - 2, 0, ts=(t,))
                    down2(f, c[-1], N2 - 1, 1, ts=(t,), end=True, phase_end=True)

            squared_relu(0, 3, 4)

            c = sched["c_in"]
            visits = []
            for i, ch in enumerate(c):
                n = ch.shape[1]
                dst = [bank[4 + 2 * t + i // 2][:, (i % 2) * CW:(i % 2) * CW + n] for t in range(NT)]
                visits.append(by_tile(ch, dst, tile0="c_in0_done" if i == 2 else None))
            enter(4, 5, visits)

            def latents(t):
                pe.wait_ge(S["c_cn_ready"], 2 * t + 2)
                for half, n in ((0, 4), (1, 1)):
                    for k in range(n):
                        kk = 4 * half + k
                        last = pe.transpose(bank[2 * t + half][:, k * P:(k + 1) * P], x_norm[:, t, kk * P:(kk + 1) * P], ident[:])
                    last.then_inc(S["c_t_psum"], 1)

            def queries(i, t):
                ch = sched["c_uq"][i]
                arrived(ch)
                token_major(ch, [bank[b][:] for b in C_UQ_BANK[i]], QL // P, ts=(t,), tile0="c_uq0_done")

            def keys_values(i, t):
                ch = sched["c_ukv"][i]
                arrived(ch)
                hi, lo = view(w_hi, ch), view(w_lo, ch)
                for n in range(2):
                    for k in range(2):
                        last = product(bank[C_UKV_BANK[i][n][t]][:], xT_hi[:, t, 3 + k, :], xT_lo[:, t, 3 + k, :],
                                       hi[:, k, 512 * n:512 * n + 512], lo[:, k, 512 * n:512 * n + 512], k == 0, k == 1)
                if t == NT - 1:
                    last.then_inc(S["mm_done"], 1)

            latents(0)
            pe.wait_ge(S["c_xl"], 2)
            pe.wait_ge(S["c_lat_ready"], 4)
            queries(0, 0)
            queries(1, 0)
            latents(1)
            queries(2, 0)
            pe.wait_ge(S["c_q_ready"], 2)
            pe.wait_ge(S["c_xl"], 4)
            keys_values(0, 0)
            for i in range(3):
                queries(i, 1)
            keys_values(0, 1)
            for ready in ("c_q_ready", "c_q1_ready"):
                pe.wait_ge(S[ready], 3)
            keys_values(1, 0)
            keys_values(1, 1)
            pe.wait_ge(S["c_kv_ready"], 4)
            pe.wait_ge(S["c_rope_ready"], 1)

            def mla_qk(h):
                if h >= 2:
                    pe.wait_ge(S["c_qkT_ready"], h - 1)
                b = bank[h % 2]
                for i, src in enumerate((c_q, c_k)):
                    for t in range(NT):
                        at = (2 * i + t) * P
                        last = pe.transpose(b[0:CD, at:at + P], src[:, t, h * CD:(h + 1) * CD], ident[:])
                last.then_inc(S["c_qkT_psum"], 1)

            def mla_scores(h):
                pe.wait_ge(S["c_qkT_ready"], h + 1)
                if h >= 2:
                    pe.wait_ge(S["c_probs"], 2 * (h - 1))
                b = bank[2 + h % 2]
                qk = c_qkT[0:CD, h % 2]
                for t in range(NT):
                    last = pe.matmul(b[:, t * SEQ:(t + 1) * SEQ], qk[:, t, :], qk[:, 2:4, :].rearrange("p a b -> p (a b)"),
                                     start=True, stop=True)
                last.then_inc(S["c_scores"], 1)

            def mla_pT(h):
                pe.wait_ge(S["c_probs"], 2 * (h + 1))
                b = bank[4 + h % 2]
                for t in range(NT):
                    for k in range(2):
                        at = (2 * t + k) * P
                        last = pe.transpose(b[:, at:at + P], c_p[:, h % 2, t, k * P:(k + 1) * P], ident[:])
                last.then_inc(S["c_pt_psum"], 1)

            def mla_values(h):
                pe.wait_ge(S["c_pt_ready"], h + 1)
                if h == 8:
                    pe.wait_ge(S["c_o_ready"], 2)
                o = slice((h % 8) * CV, (h % 8) * CV + CV)
                for t in range(NT):
                    for k in range(2):
                        last = pe.matmul(bank[6 + t][:, o], c_pT[:, h % 2, 2 * t + k, :], c_v[:, k, h * CV:(h + 1) * CV],
                                         start=k == 0, stop=k == 1)
                last.then_inc(S["c_o_psum"], 1)

            for r in range(CH + 3):
                if r < CH:
                    mla_qk(r)
                if 0 <= r - 1 < CH:
                    mla_scores(r - 1)
                if 0 <= r - 2 < CH:
                    mla_pT(r - 2)
                if 0 <= r - 3 < CH:
                    mla_values(r - 3)
            pe.wait_ge(S["c_o_ready"], 4)
            for t in range(NT):
                transpose_tile(t)
            pe.wait_ge(S["xTl_ready"], 4 * 5 + 4)
            o = sched["c_out"]
            operand_out(o[0], 0, first=True)
            operand_out(o[1], 1)
            for t in range(NT):
                operand_out(o[2], 2, ts=(t,))
                operand_out(o[3], 3, ts=(t,), end=True, phase_end=True)
            squared_relu(1, 6, 6)


INPUTS = ("x", "norm_mix", "norm_ffn", "swa_w_in", "swa_sinks", "swa_w_out", "ffn_w_gate_up", "ffn_w_down",
          "final_norm", "positions_2", "ab_norm_2", "ab_w_in_2", "ab_conv_2", "ab_gate_b_2", "ab_head_g_2",
          "ab_v_g_2", "ab_ws_2", "ab_bs_2", "ab_w_out_2", "c_norm_2", "c_w_in_2", "c_q_g_2", "c_kv_g_2",
          "c_w_uq_2", "c_w_ukv_2", "c_w_out_2", "ffn_norm_2", "ffn_w1_2", "ffn_w2_2", "final_norm_2")


def kernel(**inputs):
    import numpy as np
    import concourse.bacc as bacc
    from concourse.bass_utils import run_bass_kernel_spmd

    nc = bacc.Bacc("TRN2", target_bir_lowering=False, num_devices=1)
    arrays, t_in = {}, {}
    for name in INPUTS:
        a = np.ascontiguousarray(inputs[name])
        arrays[f"in_{name}"] = a
        t_in[name] = nc.dram_tensor(f"in_{name}", a.shape, mybir.dt.from_np(a.dtype), kind="ExternalInput").ap()
    out = nc.dram_tensor("out_0", (1, SEQ, DM), F32, kind="ExternalOutput").ap()
    build(nc, t_in, out)
    r = run_bass_kernel_spmd(nc, [arrays], core_ids=[0])
    return r.results[0]["out_0"]
```

```python
import math
from contextlib import ExitStack

import concourse.bass as bass
from concourse import mybir

F32 = mybir.dt.float32
F32R = mybir.dt.float32r
I32 = mybir.dt.int32
ALU = mybir.AluOpType
ACT = mybir.ActivationFunctionType
AX = mybir.AxisListType.X

P = 128
SEQ = 256
NT = SEQ // P
DM = 1024
KT = DM // P
EPS = 1e-6
NQH, NKV, HD = 16, 4, 64
SWA_COLS = P + 2 * P
BIG = 3.0e38
FF1 = 2816
FF2 = 4096
CW = 256
N1 = FF1 // CW
N2 = FF2 // CW
AH, AD = 4, 128
AW = AH * AD
BG = 4
CONV = 5
CH, CN, CR, CV = 16, 64, 32, 64
CD = CN + CR
QL, KVL = 384, 256
CIN = QL + KVL + CR
CKT = (QL + KVL) // P
HALF = CR // 2
ROPE_BASE = 10000.0
SLOTS = 4
SLOT = 2048


class Chunk:

    def __init__(self, index, slot, use, prev, shape):
        self.index, self.slot, self.use, self.prev, self.shape = index, slot, use, prev, shape


def weight_schedule():
    uses = {s: [] for s in range(SLOTS)}
    count = [0]
    cycle = list(range(SLOTS))
    at = [0]
    sched = {}

    def add(phase, shape, slot=None):
        if slot is None:
            slot = cycle[at[0] % SLOTS]
            at[0] += 1
        c = count[0]
        count[0] += 1
        prev = uses[slot][-1] if uses[slot] else None
        sched.setdefault(phase, []).append(Chunk(c, slot, len(uses[slot]), prev, shape))
        uses[slot].append(c)

    for _ in range(6):
        add("swa_in", (KT, CW))
    for _ in range(4):
        add("swa_out", (2, DM))
    up, spare, gate, down = [cycle[(at[0] + i) % SLOTS] for i in range(SLOTS)]
    add("ffn1", (KT, CW), up)
    add("ffn1", (KT, CW), spare)
    for _ in range(N1 - 2):
        add("ffn1", (KT, CW), gate)
        add("ffn1", (2, DM), down)
        add("ffn1", (KT, CW), up)
    add("ffn1", (KT, CW), gate)
    add("ffn1", (KT, CW), up)
    add("ffn1", (2, DM), down)
    add("ffn1", (2, DM), spare)
    cycle[:] = gate, up, down, spare
    at[0] = 0
    for i in range(13):
        add("ab_in", (KT, 16 if i == 2 else CW))
    for _ in range(4):
        add("ab_out", (2, DM))

    def squared_relu(phase):
        add(phase, (KT, CW))
        add(phase, (KT, CW))
        for _ in range(N2 - 2):
            add(phase, (2, DM))
            add(phase, (KT, CW))
        add(phase, (2, DM))
        add(phase, (2, DM))

    squared_relu("ffn2a")
    for n in (CW, CW, CW):
        add("c_in", (KT, n))
    for _ in range(3):
        add("c_uq", (QL // P, 512))
    for _ in range(2):
        add("c_ukv", (KVL // P, DM))
    for _ in range(4):
        add("c_out", (2, DM))
    squared_relu("ffn2b")
    return sched, count[0]


def build(nc, t_in, out):
    sched, n_chunks = weight_schedule()
    order = [c for phase in sched.values() for c in phase]
    ctx = ExitStack()
    with ctx:
        def sb(name, shape, dt=F32):
            return ctx.enter_context(nc.sbuf_tensor(name, shape, dt))

        w_raw = [sb(f"w_raw{s}", [P, SLOT]) for s in range(SLOTS)]
        w_hi = [sb(f"w_hi{s}", [P, SLOT], F32R) for s in range(SLOTS)]
        w_lo = [sb(f"w_lo{s}", [P, SLOT], F32R) for s in range(SLOTS)]

        def view(ring, ch):
            k, n = ch.shape
            return ring[ch.slot][:, 0:k * n].rearrange("p (k n) -> p k n", k=k)

        x_res = sb("x_res", [P, NT, DM])
        x_norm = sb("x_norm", [P, NT, DM])
        xT_hi = sb("xT_hi", [P, NT, KT, P], F32R)
        xT_lo = sb("xT_lo", [P, NT, KT, P], F32R)
        gain = sb("gain", [P, 2, DM])
        ssq = sb("ssq", [P, NT, 2])
        mean_sq = sb("mean_sq", [P, NT])
        rstd = sb("rstd", [P, NT])
        minus_half = sb("minus_half", [P, 16])
        ident = sb("ident", [P, P])
        sel = sb("sel", [AH, AH, P])
        one = sb("one", [AH, 1])
        dist = sb("dist", [P, SWA_COLS])
        sinks = sb("sinks", [P, NQH])
        pcols = sb("pcols", [P, 48])
        gate_b = sb("gate_b", [16, 1])
        wsT = sb("wsT", [P, BG, P])
        bs_all = sb("bs_all", [P, BG, P])
        pos_i = sb("pos_i", [P, NT], I32)
        pos_f = sb("pos_f", [P, NT])
        freq = sb("freq", [P, HALF])
        ang = sb("ang", [P, NT, HALF])
        turns = sb("turns", [P, NT, HALF])
        cosr = sb("cosr", [P, NT, HALF])
        cos = sb("cos", [P, NT, HALF])
        sin = sb("sin", [P, NT, HALF])
        ff_hi = [sb(f"ff_hi{i}", [P, 2, SEQ], F32R) for i in range(2)]
        ff_lo = [sb(f"ff_lo{i}", [P, 2, SEQ], F32R) for i in range(2)]

        ARENA = 13700
        arena = sb("arena", [P, ARENA])
        used = [0]

        def take(parts, *shape):
            n = math.prod(shape)
            a = arena[0:parts, used[0]:used[0] + n]
            used[0] += n
            assert used[0] <= ARENA, used[0]
            if len(shape) == 1:
                return a
            names = "abcd"[:len(shape)]
            return a.rearrange(f"p ({' '.join(names)}) -> p {' '.join(names)}",
                               **{names[i]: shape[i] for i in range(len(shape))})

        ff_act = take(P, 2, SEQ)
        ff_h = take(P, 2, SEQ)
        used[0] = 0
        prows = take(48, P)
        ws = take(P, BG, P)
        swa_qT = take(P, 8, SEQ)
        swa_kT = take(P, NKV, SEQ)
        swa_v = take(P, NT, NKV * HD)
        swa_s = take(P, 2, 4, SWA_COLS + 2)
        SWA_PARTS = ((0, 1 + P), (1 + P, 2 + SWA_COLS))
        swa_pT = take(P, 2, 12, P)
        swa_mx = take(P, NT, NQH)
        swa_nm = take(P, NT, NQH)
        swa_sum = take(P, NT, NQH)
        swa_rden = take(P, NT, NQH)
        used[0] = 0
        PADW = SEQ + CONV - 1
        ab_pad = take(P, 8, PADW)
        ab_cv = take(P, 8, SEQ)
        ab_v1 = take(P, NT, AH, AD + 1)
        ab_u = take(P, BG, SEQ)
        ab_vb = take(P, NT, BG * P)
        ab_sig = take(P, AH, SEQ)
        ab_e = take(P, 2, 2, SWA_COLS)
        num_at = used[0]
        ab_num = take(P, 2, AH, NT, AD + 1)
        ab_sq = take(P, NT * BG, P)
        ab_ss = take(P, 8)
        ab_ms = take(P, 8)
        ab_rs = take(P, 8)
        ab_t = take(P, NT, 4, AH)
        ab_em = take(P, 2, NT, AH)
        ab_rd = take(P, 2, AH, NT)
        ab_dd = take(P, 2, AH, NT)
        used[0] = num_at
        g_raw = take(16, SEQ)
        g_w = take(AH, 2, SEQ)
        g_B = take(AH, 2, SEQ)
        g_M = take(AH, 2, SEQ)
        g4 = x_norm[0:AH, 0, :].rearrange("p (k t) -> p k t", k=4)
        g_am = x_norm[0:AH, 1, :].rearrange("p (k t) -> p k t", k=4)
        g_nM = x_norm[0:AH, 0, 0:2 * SEQ].rearrange("p (d t) -> p d t", d=2)
        used[0] = 0
        c_lat = take(P, NT, CIN)
        c_q = take(P, NT, CH * CD)
        c_k = take(P, NT, CH * CD)
        c_v = take(P, NT, CH * CV)
        c_qkT = take(P, 2, 4, P)
        c_p = take(P, 2, NT, SEQ)
        c_pT = take(P, 2, 4, P)
        c_tmp = c_p.rearrange("p a b c -> p (a b c)").rearrange("p (i n) -> p i n", i=4)
        c_gain = take(P, QL + KVL)
        c_kr = take(P, NT, CR)
        c_krt = take(P, 4, NT, HALF)
        c_ss = take(P, NT, 2)
        c_ms = take(P, NT, 2)
        c_rs = take(P, NT, 2)
        c_mx = take(P, CH, NT)
        c_nm = take(P, CH, NT)
        c_sum = take(P, NT, CH)
        c_rden = take(P, NT, CH)

        bank = [ctx.enter_context(nc.psum_tensor(f"bank{i}", [P, 512], F32)) for i in range(8)]

        S = {n: ctx.enter_context(nc.semaphore(n)) for n in (
            "hi_done lo_done mm_done acc_done head_loaded head_hi head_lo x0_loaded x1_loaded sinks_loaded small_loaded ws_loaded pos_loaded "
            "gain_loaded cgain_loaded consts_ready dist_step "
            "resid_ready ssq_ready rstd_ready xn_ready t_psum xTh_ready xTl_ready "
            "params_psum params_ready wsT_psum wsT_ready rope_angle rope_ready "
            "act_chain dve_chain pool_chain "
            "ff1_sg ff1_h ff1_t ff1_hi ff1_lo ff2_t ff2_relu ff2_h ff2_hi ff2_lo "
            "swa_q_ready swa_k_ready swa_v_ready swa_scores swa_biased swa_nmax swa_probs swa_pt_psum "
            "swa_pt_ready swa_o_psum swa_o_ready swa_oT_psum swa_oh_ready swa_ol_ready "
            "g_raw_ready g4_loaded g_abs_ready g_ln_ready g_rows_ready g_cols_psum g_cols_ready g_em_ready "
            "qk_padded conv_begun conv_ready qk_ready v1_ready u_ready vb_ready sig_ready "
            "vb_sumsq vb_rstd vn_ready sp_psum sp_read nM_psum e_exp e_ready st_psum w_ready num_psum num_ready "
            "h_sumsq h_rstd hn_ready hT_psum ab_full ab_hi ab_lo pads_ready "
            "c_in0_done c_uq0_done c_lat_ready c_ssq c_rstd c_cn_ready c_t_psum c_xh c_xl c_q_ready c_q1_ready c_kv0_ready c_kv1_ready c_rope_ready "
            "c_qkT_psum c_qkT_ready c_scores c_nmax c_probs c_pt_psum c_pt_ready c_o_psum c_o_ready "
            "out_stored"
        ).split()}
        loaded = [ctx.enter_context(nc.semaphore(f"slot{s}_loaded")) for s in range(SLOTS)]
        block = ctx.enter_context(nc.Block())

        ffn_phases = ("ffn2a", "ffn2b")
        AB_OUT_ORDER = (2, 3, 0, 1)
        ab_slot = (4, 5, 6, 7, 0, 1, 2, 3)
        AB_BANK = (4, 5, 0, 1, 6, 7, 2, 3, 0, 6, 7, 6, 7)
        phase_of_norm = {1: "swa_out", 2: "ffn1", 4: "ab_out", 5: "ffn2a", 6: "c_out", 7: "ffn2b"}
        additions = {n: i for i, n in enumerate(phase_of_norm)}
        C_UQ_BANK = ((4, 5), (6, 7), (0, 1))
        C_UKV_BANK = (((4, 2), (6, 3)), ((5, 4), (7, 6)))
        norm_order = ([(n, t) for n in (0, 1) for t in range(NT)] + [(2, 0), (3, 0), (2, 1), (3, 1)]
                      + [(n, t) for n in (4, 5, 6, 7) for t in range(NT)])
        turn = {nt: i + 1 for i, nt in enumerate(norm_order)}

        SWA_PT_BANK = ((2, 2, 2), (2, 2, 2), (2, 2, 2), (2, 0, 1))
        HALF_D = (slice(0, DM // 2), slice(DM // 2, DM))

        def half_turn(n, t, j):
            return 2 * turn[n, t] - 1 + j

        def kv_parts(i, n, t):
            src = bank[C_UKV_BANK[i][n][t]][:].rearrange("p (h e) -> p h e", e=CN + CV)
            h0 = 8 * i + 4 * n
            k = c_k[:, t, h0 * CD:(h0 + 4) * CD].rearrange("p (h e) -> p h e", e=CD)
            v = c_v[:, t, h0 * CV:(h0 + 4) * CV].rearrange("p (h e) -> p h e", e=CV)
            return (src[:, :, 0:CN], k[:, :, 0:CN]), (src[:, :, CN:CN + CV], v)

        @block.sync
        def _(sp):
            sp.dma_start(x_res[:, 0], t_in["x"][0, 0:P]).then_inc(S["x0_loaded"], 16)

            def small_inputs():
                sp.dma_start(pos_i[:], t_in["positions_2"][0].rearrange("(t p) -> p t", p=P),
                              allow_slow_non_contiguous=True).then_inc(S["pos_loaded"], 16)
                sp.dma_start(sinks[:], t_in["swa_sinks"].broadcast_to([P, NQH])).then_inc(S["sinks_loaded"], 16)
                sp.dma_start(prows[0:40, :], t_in["ab_conv_2"][0].rearrange("j (f c) -> (j f) c", c=P)).then_inc(S["small_loaded"], 16)
                sp.dma_start(prows[40:44, :], t_in["ab_head_g_2"][0].rearrange("(f c) -> f c", c=P)).then_inc(S["small_loaded"], 16)
                sp.dma_start(prows[44:48, :], t_in["ab_v_g_2"][0].rearrange("(f c) -> f c", c=P)).then_inc(S["small_loaded"], 16)
                sp.dma_start(gate_b[:], t_in["ab_gate_b_2"][0].rearrange("(a b) -> a b", b=1),
                              allow_slow_non_contiguous=True).then_inc(S["small_loaded"], 16)
                sp.dma_start(ws[:], t_in["ab_ws_2"][0].rearrange("g t s -> t g s")).then_inc(S["ws_loaded"], 16)
                sp.dma_start(bs_all[:],
                              t_in["ab_bs_2"].broadcast_to([P, BG, P])).then_inc(S["ws_loaded"], 16)

            def load(ch, src, it=0, stride=0):
                if ch.prev is not None:
                    sp.wait_ge(S["lo_done"], ch.prev + 1 + it * stride)
                sp.dma_start(view(w_raw, ch), src).then_inc(loaded[ch.slot], 16)

            def cols(w, at, n):
                return w.rearrange("(k p) c -> p k c", p=P)[:, :, at:at + n]

            def by_cols(w):
                return w.rearrange("(k p) (i c) -> p k i c", p=P, c=CW)

            def by_rows(w):
                return w.rearrange("(i k p) c -> p i k c", p=P, k=2)

            w = t_in["swa_w_in"][0]
            for i, ch in zip((5, 4, 0, 1, 2, 3), sched["swa_in"]):
                if ch.index == 0:
                    sp.dma_start(view(w_raw, ch)[:, 0:KT // 2],
                                 cols(w, i * CW, CW)[:, 0:KT // 2]).then_inc(S["head_loaded"], 16)
                    sp.dma_start(x_res[:, 1], t_in["x"][0, P:SEQ]).then_inc(S["x1_loaded"], 16)
                    sp.dma_start(view(w_raw, ch)[:, KT // 2:], cols(w, i * CW, CW)[:, KT // 2:]).then_inc(loaded[ch.slot], 16)
                    continue
                if ch.index == SLOTS:
                    small_inputs()
                load(ch, cols(w, i * CW, CW))
            w = by_rows(t_in["swa_w_out"][0])
            for i, ch in enumerate(sched["swa_out"]):
                load(ch, w[:, i])
            gu, dn = by_cols(t_in["ffn_w_gate_up"][0]), by_rows(t_in["ffn_w_down"][0])
            c = sched["ffn1"]
            load(c[0], gu[:, :, 0])
            load(c[1], gu[:, :, N1])
            load(c[2], gu[:, :, 1])
            load(c[3], dn[:, 0])
            load(c[4], gu[:, :, N1 + 1])
            with sp.Fori(0, N1 - 3) as it:
                load(c[5], gu[:, :, it + 2], it, 3)
                load(c[6], dn[:, it + 1], it, 3)
                load(c[7], gu[:, :, it + (N1 + 2)], it, 3)
            load(c[-4], gu[:, :, N1 - 1])
            load(c[-3], gu[:, :, 2 * N1 - 1])
            load(c[-2], dn[:, N1 - 2])
            load(c[-1], dn[:, N1 - 1])

            w = t_in["ab_w_in_2"][0]
            uv = 4 * AW + 16
            at = [i * CW for i in (4, 5)] + [4 * AW] + [i * CW for i in range(4)] + [uv + i * CW for i in (2, 3, 0, 1)] + [3 * AW, 3 * AW + CW]
            for a, ch in zip(at, sched["ab_in"]):
                load(ch, cols(w, a, ch.shape[1]))
            w = by_rows(t_in["ab_w_out_2"][0])
            for i, ch in zip(AB_OUT_ORDER, sched["ab_out"]):
                load(ch, w[:, i])

            def squared_relu(layer):
                c = sched[ffn_phases[layer]]
                w1, w2 = by_cols(t_in["ffn_w1_2"][layer]), by_rows(t_in["ffn_w2_2"][layer])
                load(c[0], w1[:, :, 0])
                load(c[1], w1[:, :, 1])
                with sp.Fori(0, N2 // 2 - 1) as it:
                    load(c[2], w2[:, 2 * it], it, 4)
                    load(c[3], w1[:, :, 2 * it + 2], it, 4)
                    load(c[4], w2[:, 2 * it + 1], it, 4)
                    load(c[5], w1[:, :, 2 * it + 3], it, 4)
                load(c[-2], w2[:, N2 - 2])
                load(c[-1], w2[:, N2 - 1])

            squared_relu(0)
            w = t_in["c_w_in_2"][0]
            for i, ch in enumerate(sched["c_in"]):
                load(ch, cols(w, min(i * CW, CIN - CW), CW))
            for i, ch in enumerate(sched["c_uq"]):
                load(ch, cols(t_in["c_w_uq_2"][0], i * 512, 512))
            for i, ch in enumerate(sched["c_ukv"]):
                load(ch, cols(t_in["c_w_ukv_2"][0], i * DM, DM))
            w = by_rows(t_in["c_w_out_2"][0])
            for i, ch in enumerate(sched["c_out"]):
                load(ch, w[:, i])
            squared_relu(1)
            o = out[0].rearrange("(t p) d -> p t d", p=P)
            for t in range(NT):
                for j in range(2):
                    sp.wait_ge(S["xn_ready"], half_turn(7, t, j))
                    sp.dma_start(o[:, t, HALF_D[j]], x_norm[:, t, HALF_D[j]]).then_inc(S["out_stored"], 16)
            sp.wait_ge(S["out_stored"], 32 * NT)

        norm_gain = [t_in["norm_mix"][0], t_in["norm_ffn"][0], t_in["final_norm"], t_in["ab_norm_2"][0],
                     t_in["ffn_norm_2"][0], t_in["c_norm_2"][0], t_in["ffn_norm_2"][1], t_in["final_norm_2"]]

        @block.gpsimd
        def _(pool):
            chain = [0]

            def step(ins):
                chain[0] += 1
                ins.then_inc(S["pool_chain"], 1)
                pool.wait_ge(S["pool_chain"], chain[0])

            def load_gain(n):
                src = norm_gain[n].rearrange("(a d) -> a d", a=1).broadcast_to([P, DM])
                pool.dma_start(gain[:, n % 2], src).then_inc(S["gain_loaded"], 16)

            def norm(*order):
                for n, t in order:
                    pool.wait_ge(S["ssq_ready"], half_turn(n, t, 1))
                    step(pool.tensor_scalar(mean_sq[:, t:t + 1], ssq[:, t, 0:1], ssq[:, t, 1:2], EPS, ALU.add, ALU.add))
                    pool.tensor_tensor(rstd[:, t:t + 1], mean_sq[:, t:t + 1], minus_half[:, 0:1],
                                       ALU.pow).then_inc(S["rstd_ready"], 1)

            pool.memset(minus_half[:], -0.5)
            load_gain(0)
            step(pool.memset(ident[:], 0.0))
            pool.affine_select(out=ident[:], in_=ident[:], compare_op=ALU.not_equal, fill=1.0, base=0,
                               pattern=[[-1, P]], channel_multiplier=1).then_inc(S["consts_ready"], 1)
            norm((0, 0), (0, 1))
            pool.wait_ge(S["gain_loaded"], 16)
            load_gain(1)
            step(pool.memset(sel[:], 0.0))
            pool.affine_select(out=sel[:], in_=sel[:], compare_op=ALU.not_equal, fill=1.0, base=0,
                               pattern=[[-1, AH], [0, P]], channel_multiplier=1).then_inc(S["consts_ready"], 1)
            pool.memset(one[:], 1.0)
            for i in range(HALF):
                last = pool.memset(freq[:, i:i + 1], float(ROPE_BASE ** (-i / HALF)))
            last.then_inc(S["consts_ready"], 1)

            def next_gain(n):
                pool.wait_ge(S["xn_ready"], half_turn(n, 1, 1))
                pool.wait_ge(S["gain_loaded"], 16 * (n + 2))
                load_gain(n + 2)

            step(pool.iota(dist[:, 0:P], pattern=[[-1, P]], base=0, channel_multiplier=1,
                           allow_small_or_imprecise_dtypes=True))
            step(pool.iota(dist[:, P:3 * P], pattern=[[-1, 2 * P]], base=P, channel_multiplier=1,
                           allow_small_or_imprecise_dtypes=True))
            for at, sign, op in ((0, -1, ALU.is_ge), (P, 1, ALU.is_gt), (2 * P, -1, ALU.is_ge)):
                d = dist[:, at:at + P]
                ins = pool.affine_select(out=d, in_=d, compare_op=op, fill=BIG, base=0,
                                         pattern=[[sign, P]], channel_multiplier=-sign)
                ins.then_inc(S["dist_step"], 1)
            next_gain(0)
            norm((1, 0), (1, 1))
            next_gain(1)
            norm((2, 0), (3, 0), (2, 1), (3, 1))
            next_gain(2)
            next_gain(3)
            pool.memset(ab_pad[:, :, 0:2], 0.0)
            pool.memset(ab_pad[:, :, 2 + SEQ:PADW], 0.0)
            pool.memset(ab_v1[:, :, :, AD:AD + 1], 1.0).then_inc(S["pads_ready"], 1)
            def masks(h):
                pool.wait_ge(S["e_exp"], 4 * (h + 1))
                for d, at, sign in ((0, 0, 1), (0, 2 * P, 1), (1, 0, -1), (1, 2 * P, -1)):
                    e = ab_e[:, h % 2, d, at:at + P]
                    last = pool.affine_select(out=e, in_=e, compare_op=ALU.is_ge, fill=0.0, base=0,
                                              pattern=[[sign, P]], channel_multiplier=-sign)
                    last.then_inc(S["e_ready"], 1)

            def group_rstd(sumsq, ready, count=1, at=slice(0, 8)):
                pool.wait_ge(S[sumsq], count)
                step(pool.tensor_scalar(ab_ms[:, at], ab_ss[:, at], 1.0 / P, EPS, ALU.mult, ALU.add))
                pool.tensor_tensor(ab_rs[:, at], ab_ms[:, at], minus_half[:, at], ALU.pow).then_inc(S[ready], 1)

            masks(0)
            masks(1)
            group_rstd("vb_sumsq", "vb_rstd")
            masks(2)
            masks(3)
            pool.wait_ge(S["vn_ready"], 1)
            for p in range(2):
                group_rstd("h_sumsq", "h_rstd", p + 1, slice(4 * p, 4 * p + 4))
            norm((4, 0), (4, 1))
            next_gain(4)
            pool.dma_start(c_gain[:, 0:QL], t_in["c_q_g_2"].broadcast_to([P, QL])).then_inc(S["cgain_loaded"], 16)
            pool.dma_start(c_gain[:, QL:QL + KVL], t_in["c_kv_g_2"].broadcast_to([P, KVL])).then_inc(S["cgain_loaded"], 16)
            norm((5, 0), (5, 1))
            next_gain(5)
            for t in range(NT):
                pool.wait_ge(S["c_ssq"], 2 * t + 2)
                for j, n in ((0, QL), (1, KVL)):
                    step(pool.tensor_scalar(c_ms[:, t, j:j + 1], c_ss[:, t, j:j + 1], 1.0 / n, EPS, ALU.mult, ALU.add))
                pool.tensor_tensor(c_rs[:, t], c_ms[:, t], minus_half[:, 0:2], ALU.pow).then_inc(S["c_rstd"], 1)
            norm((6, 0), (6, 1))
            norm((7, 0), (7, 1))

        @block.scalar
        def _(act):
            chain = [0]

            def step(ins):
                chain[0] += 1
                ins.then_inc(S["act_chain"], 1)
                act.wait_ge(S["act_chain"], chain[0])

            split = [0]

            def high(ch, it=0, stride=0):
                act.wait_ge(loaded[ch.slot], 16 * (ch.use + 1) + it * (16 if stride else 0))
                if ch.prev is not None:
                    act.wait_ge(S["mm_done"], ch.prev + 1 + it * stride)
                act.activation(view(w_hi, ch), view(w_raw, ch), ACT.Copy).then_inc(S["hi_done"], 1)

            def high_half(ch, half):
                if half == 0:
                    act.wait_ge(loaded[ch.slot], 16 * (ch.use + 1))
                    act.wait_ge(S["mm_done"], ch.prev + 1)
                ins = act.activation(view(w_hi, ch)[:, half], view(w_raw, ch)[:, half], ACT.Copy)
                if half:
                    ins.then_inc(S["hi_done"], 1)

            def high_upto(index):
                while split[0] < min(index, n_chunks):
                    high(order[split[0]])
                    split[0] += 1


            def sum_squares(n, t, js=(0, 1)):
                for j in js:
                    if n == 0:
                        act.wait_ge(S[("x0_loaded", "x1_loaded")[t]], 16)
                    elif n == 3:
                        act.wait_ge(S["xn_ready"], half_turn(2, t, j))
                    else:
                        act.wait_ge(S["resid_ready"], 4 * additions[n] + 2 * t + j + 1)
                    if turn[n, t] > 1 and j == 0:
                        act.wait_ge(S["ssq_ready"], half_turn(n, t, 0) - 1)
                    act.activation(x_norm[:, t, HALF_D[j]], x_res[:, t, HALF_D[j]], ACT.Square, scale=DM ** -0.5,
                                   accum_out=ssq[:, t, j:j + 1]).then_inc(S["ssq_ready"], 1)

            def transposed_high(n, t, halves=(0, 1)):
                for half in halves:
                    act.wait_ge(S["t_psum"], 4 * n + 2 * t + half + 1)
                    act.activation(xT_hi[:, t, 4 * half:4 * half + 4, :].rearrange("p k c -> p (k c)"),
                                   bank[2 * t + half][:], ACT.Copy).then_inc(S["xTh_ready"], 1)

            def enter(use, n, early, then):
                sum_squares(n, 0)
                transposed_high(use, 0, (0,))
                sum_squares(n, 1, (0,))
                transposed_high(use, 0, (1,))
                sum_squares(n, 1, (1,))
                high_upto(early)
                transposed_high(use, 1)
                high_upto(then)

            c = sched["swa_in"]
            sum_squares(0, 0)
            for at, ready, done in ((slice(0, KT // 2), S["head_loaded"], "head_hi"), (slice(KT // 2, KT), loaded[0], "hi_done")):
                act.wait_ge(ready, 16)
                act.activation(view(w_hi, c[0])[:, at], view(w_raw, c[0])[:, at], ACT.Copy).then_inc(S[done], 1)
                if done == "head_hi":
                    transposed_high(0, 0)
            split[0] = 1
            sum_squares(0, 1)
            high_upto(2)
            transposed_high(0, 1)
            high_upto(SLOTS)

            act.wait_ge(S["mm_done"], c[0].index + 1)
            act.activation(swa_v.rearrange("p a b -> p (a b)"), bank[5][:], ACT.Copy).then_inc(S["swa_v_ready"], 1)
            high_upto(c[1].index + 1 + SLOTS)

            def queries(i):
                ch = c[2 + i]
                act.wait_ge(S["mm_done"], ch.index + 1)
                act.activation(swa_qT[:, 2 * i:2 * i + 2, :].rearrange("p a b -> p (a b)"), bank[(6, 7, 4, 5)[i]][:],
                               ACT.Copy, scale=HD ** -0.5).then_inc(S["swa_q_ready"], 1)

            def swa_probabilities(g):
                act.wait_ge(S["swa_nmax"], g + 1)
                for j in range(4):
                    h = 4 * g + j
                    for t, (a, b) in enumerate(SWA_PARTS):
                        s = swa_s[:, g % 2, j, a:b]
                        act.activation(s, s, ACT.Exp, bias=swa_nm[:, t, h:h + 1],
                                       accum_out=swa_sum[:, t, h:h + 1]).then_inc(S["swa_probs"], 1)

            def swa_transposed(g):
                for u in range(3):
                    act.wait_ge(S["swa_pt_psum"], 3 * g + u + 1)
                    act.activation(swa_pT[:, g % 2, 4 * u:4 * u + 4, :].rearrange("p a b -> p (a b)"),
                                   bank[SWA_PT_BANK[g][u]][:], ACT.Copy).then_inc(S["swa_pt_ready"], 1)
                    if u == 1 and g >= 1:
                        swa_operand(g - 1)

            def swa_operand(g):
                act.wait_ge(S["swa_oT_psum"], g + 1)
                act.activation(xT_hi[:, :, 2 * g:2 * g + 2, :], bank[3][:].rearrange("p (t k c) -> p t k c", t=NT, k=2),
                               ACT.Copy).then_inc(S["swa_oh_ready"], 1)

            o = sched["swa_out"]
            queries(0)
            queries(1)
            high_upto(c[2].index + 1 + SLOTS)
            swa_probabilities(0)
            queries(2)
            swa_transposed(0)
            high_upto(c[3].index + 1 + SLOTS)
            swa_probabilities(1)
            high_upto(c[4].index + 1 + SLOTS)
            queries(3)
            swa_transposed(1)
            high_upto(c[5].index + 1 + SLOTS)
            swa_probabilities(2)
            swa_transposed(2)
            high_upto(o[0].index + 1 + SLOTS)
            swa_probabilities(3)
            swa_transposed(3)
            high_upto(o[1].index + 1 + SLOTS)
            swa_operand(3)
            c = sched["ffn1"]
            enter(1, 1, 0, c[3].index + 1)

            def silu_gate(ch, i, it=0):
                act.wait_ge(S["mm_done"], ch.index + 1 + 3 * it)
                act.activation(ff_act[:], bank[0][:].rearrange("p (a b) -> p a b", a=2),
                               ACT.Silu).then_inc(S["ff1_sg"], 1)

            def hidden_high(i, it=0, buf=0):
                act.wait_ge(S["ff1_h"], i + 1 + it)
                act.activation(ff_hi[buf][:], ff_h[:], ACT.Copy).then_inc(S["ff1_hi"], 1)

            def first_hidden_high(transposed, count, ready):
                act.wait_ge(S[transposed], count)
                act.activation(ff_hi[0][:], bank[2][:].rearrange("p (a b) -> p a b", a=2), ACT.Copy).then_inc(S[ready], 1)

            silu_gate(c[0], 0)
            high_upto(c[3].index + 1)
            first_hidden_high("ff1_t", 1, "ff1_hi")
            high_upto(c[4].index + 1)
            silu_gate(c[2], 1)
            high(c[5])
            high(c[6])
            hidden_high(1)
            high(c[7])
            with act.Fori(0, N1 - 4) as it:
                silu_gate(c[5], 2, it)
                high(c[8], it, 3)
                high(c[9], it, 3)
                hidden_high(2, it)
                high(c[10], it, 3)
            silu_gate(c[-7], N1 - 2)
            high(c[-4])
            hidden_high(N1 - 2)
            for ch in c[-3:]:
                high(ch)
            silu_gate(c[-4], N1 - 1)
            hidden_high(N1 - 1, buf=1)
            split[0] = c[-1].index + 1
            high_upto(c[-1].index + 1 + 2)

            sum_squares(2, 0)
            sum_squares(3, 0)
            sum_squares(2, 1)
            transposed_high(2, 0)
            sum_squares(3, 1)
            c = sched["ab_in"]
            high_upto(c[2].index + 1)
            transposed_high(2, 1)
            high_upto(c[0].index + SLOTS)
            for i in range(2):
                ch = c[i]
                act.wait_ge(S["mm_done"], ch.index + 1)
                for t in range(NT):
                    last = act.activation(ab_v1[:, t, 2 * i:2 * i + 2, 0:AD],
                                          bank[AB_BANK[i]][:, t * 256:t * 256 + 256].rearrange("p (a b) -> p a b", a=2), ACT.Copy)
                last.then_inc(S["v1_ready"], 1)
                high_upto(ch.index + 1 + SLOTS)
            act.wait_ge(S["small_loaded"], 64)
            act.wait_ge(S["mm_done"], c[2].index + 1)
            act.activation(g_raw, bank[0][0:16, 0:SEQ], ACT.Identity, bias=gate_b[:]).then_inc(S["g_raw_ready"], 1)
            act.wait_ge(S["g_raw_ready"], 1)
            for k in range(4):
                act.dma_start(g4[:, k, :], g_raw[4 * k:4 * k + 4, :]).then_inc(S["g4_loaded"], 16)
            act.wait_ge(S["pads_ready"], 1)
            act.wait_ge(S["params_ready"], 1)
            high_upto(c[2].index + 1 + SLOTS)

            def pairs(i):
                return bank[AB_BANK[i]][:].rearrange("p (a b) -> p a b", a=2)

            for i in range(4):
                ch = c[3 + i]
                act.wait_ge(S["mm_done"], ch.index + 1)
                act.activation(ab_pad[:, 2 * i:2 * i + 2, 2:2 + SEQ], pairs(3 + i), ACT.Copy).then_inc(S["qk_padded"], 1)
                for f in range(2):
                    j = 8 * (CONV // 2) + 2 * i + f
                    last = act.activation(ab_cv[:, 2 * i + f], pairs(3 + i)[:, f], ACT.Copy, scale=pcols[:, j:j + 1])
                last.then_inc(S["conv_begun"], 1)
                high_upto(ch.index + 1 + SLOTS)
                if i == 1:
                    act.wait_ge(S["g_abs_ready"], 1)
                    step(act.activation(g_w, g_w, ACT.Exp))
                    act.activation(g_w, g_w, ACT.Ln, bias=1.0).then_inc(S["g_ln_ready"], 1)
            for i in range(2):
                ch = c[7 + i]
                act.wait_ge(S["mm_done"], ch.index + 1)
                act.activation(ab_vb[:, :, i * CW:(i + 1) * CW], pairs(7 + i), ACT.Gelu_apprx_tanh).then_inc(S["vb_ready"], 1)
                high_upto(ch.index + 1 + SLOTS)

            def gating_u(i):
                ch = c[9 + i]
                act.wait_ge(S["mm_done"], ch.index + 1)
                act.activation(ab_u[:, 2 * i:2 * i + 2, :], pairs(9 + i), ACT.Gelu_apprx_tanh).then_inc(S["u_ready"], 1)

            def output_gate(i):
                ch = c[11 + i]
                act.wait_ge(S["mm_done"], ch.index + 1)
                act.activation(ab_sig[:, 2 * i:2 * i + 2, :], pairs(11 + i), ACT.Sigmoid).then_inc(S["sig_ready"], 1)

            def decay_weights(h):
                act.wait_ge(S["nM_psum"], h + 1)
                b = bank[h % 2]
                for d, t, src, at in ((0, 0, 0, 0), (0, 1, P, 2 * P), (1, 0, SEQ, 0), (1, 1, SEQ, P)):
                    n = SEQ if (d, t) in ((0, 0), (1, 1)) else P
                    act.activation(ab_e[:, h % 2, d, at:at + n], b[:, src:src + n], ACT.Exp,
                                   bias=ab_t[:, t, d, h:h + 1]).then_inc(S["e_exp"], 1)

            def numerators(h):
                for d in range(2):
                    act.wait_ge(S["num_psum"], 2 * h + d + 1)
                    act.activation(ab_num[:, d, h], bank[4 + d][:, 0:2 * (AD + 1)].rearrange("p (t v) -> p t v", t=NT),
                                   ACT.Copy).then_inc(S["num_ready"], 1)

            def full_high(j):
                act.wait_ge(S["ab_full"], j + 1)
                k = ab_slot[j]
                act.activation(xT_hi[:, :, k, :], ab_cv[:, j, :].rearrange("p (t c) -> p t c", t=NT),
                               ACT.Copy).then_inc(S["ab_hi"], 1)

            act.wait_ge(S["conv_ready"], 4)
            act.activation(ab_pad[:, :, 0:SEQ], ab_cv[:], ACT.Silu).then_inc(S["qk_ready"], 1)
            act.wait_ge(S["g_cols_ready"], 1)
            act.activation(ab_em.rearrange("p d t h -> p t d h"), ab_t[:, :, 2:4, :], ACT.Exp, scale=-1.0).then_inc(S["g_em_ready"], 1)
            decay_weights(0)
            decay_weights(1)
            gating_u(0)
            gating_u(1)
            numerators(0)
            decay_weights(2)
            high_upto(c[9].index + 1 + SLOTS)
            numerators(1)
            decay_weights(3)
            high_upto(c[10].index + 1 + SLOTS)
            numerators(2)
            output_gate(0)
            output_gate(1)
            for j in range(4):
                full_high(j)
            numerators(3)
            high_upto(c[11].index + 1 + SLOTS)
            full_high(4)
            full_high(5)
            high_upto(c[12].index + 1 + SLOTS)
            full_high(6)
            full_high(7)
            o = sched["ab_out"]
            high_upto(o[0].index + 1 + SLOTS)
            high_upto(o[1].index + 1 + SLOTS)

            def relu_square(f, ch, i, buf, it=0):
                act.wait_ge(S["mm_done"], ch.index + 1 + 4 * it)
                if not (f == 0 and i == 0):
                    act.wait_ge(S["ff2_lo"], N2 * f + i + 2 * it)
                act.activation(ff_act[:], bank[buf][:].rearrange("p (a b) -> p a b", a=2), ACT.Relu).then_inc(S["ff2_relu"], 1)
                act.wait_ge(S["ff2_relu"], N2 * f + i + 1 + 2 * it)
                act.activation(ff_hi[buf][:], ff_act[:], ACT.Square).then_inc(S["ff2_hi"], 1)

            def squared_relu(f, after):
                c = sched[ffn_phases[f]]
                act.wait_ge(S["mm_done"], c[0].index + 1)
                act.activation(ff_act[:], bank[0][:].rearrange("p (a b) -> p a b", a=2), ACT.Relu).then_inc(S["ff2_relu"], 1)
                first_hidden_high("ff2_t", f + 1, "ff2_hi")
                high_upto(c[4].index + 1)
                relu_square(f, c[1], 1, 1)
                high_upto(c[5].index + 1)
                if f == 0:
                    act.wait_ge(S["rope_angle"], 1)
                    act.activation(sin[:], ang[:], ACT.Sin)
                    act.activation(cos[:], cosr[:], ACT.Sin).then_inc(S["rope_ready"], 1)
                with act.Fori(0, N2 // 2 - 2) as it:
                    high(c[6], it, 4)
                    relu_square(f, c[3], 2, 0, it)
                    high(c[7], it, 4)
                    high(c[8], it, 4)
                    relu_square(f, c[5], 3, 1, it)
                    high(c[9], it, 4)
                split[0] = c[-3].index + 1
                high_upto(c[-2].index + 1)
                relu_square(f, c[-5], N2 - 2, 0)
                high_upto(c[-1].index + 2)
                relu_square(f, c[-3], N2 - 1, 1)
                high_upto(c[-1].index + 1 + after)

            c = sched["ffn2a"]
            enter(3, 4, 0, c[2].index + 1)
            squared_relu(0, 2)

            c = sched["c_in"]
            enter(4, 5, c[2].index + 1, c[0].index + SLOTS)

            def latents_in(t):
                if t == 0:
                    act.wait_ge(S["c_in0_done"], 1)
                else:
                    act.wait_ge(S["mm_done"], sched["c_in"][2].index + 1)
                act.activation(c_lat[:, t, 0:512], bank[4 + 2 * t][:], ACT.Copy).then_inc(S["c_lat_ready"], 1)
                act.activation(c_lat[:, t, 512:CIN], bank[5 + 2 * t][:, 3 * CW - CIN:CW], ACT.Copy).then_inc(S["c_lat_ready"], 1)
                act.wait_ge(S["c_lat_ready"], 2 * t + 2)
                for j, a, b in ((0, 0, QL), (1, QL, QL + KVL)):
                    if j or t:
                        act.wait_ge(S["c_ssq"], 2 * t + j)
                    act.activation(x_norm[:, t, a:b], c_lat[:, t, a:b], ACT.Square, accum_out=c_ss[:, t, j:j + 1]).then_inc(S["c_ssq"], 1)

            def latents_high(t):
                for half, n in ((0, 4), (1, 1)):
                    act.wait_ge(S["c_t_psum"], 2 * t + half + 1)
                    act.activation(xT_hi[:, t, 4 * half:4 * half + n, :].rearrange("p k c -> p (k c)"),
                                   bank[2 * t + half][:, 0:n * P], ACT.Copy).then_inc(S["c_xh"], 1)

            def queries(i):
                act.wait_ge(S["c_uq0_done"], i + 1)
                act.activation(c_q[:, 0, i * 512:(i + 1) * 512], bank[C_UQ_BANK[i][0]][:],
                               ACT.Copy).then_inc(S["c_q_ready"], 1)

            def keys_values(i):
                act.wait_ge(S["mm_done"], sched["c_ukv"][i].index + 1)
                for n in range(2):
                    for src, dst in kv_parts(i, n, 0):
                        last = act.activation(dst, src, ACT.Copy)
                last.then_inc(S["c_kv0_ready"], 1)

            q = sched["c_uq"]
            latents_in(0)
            high_upto(c[0].index + 1 + SLOTS)
            high_upto(c[1].index + 1 + SLOTS)
            latents_high(0)
            latents_in(1)
            high_upto(c[2].index + 1 + SLOTS)
            queries(0)
            queries(1)
            queries(2)
            latents_high(1)
            high_upto(q[0].index + 1 + SLOTS)
            high_upto(q[1].index + 1 + SLOTS)
            keys_values(0)
            keys_values(1)

            def mla_probabilities(h):
                act.wait_ge(S["c_nmax"], h + 1)
                for t in range(NT):
                    act.activation(c_p[:, h % 2, t], bank[2 + h % 2][:, t * SEQ:(t + 1) * SEQ], ACT.Exp, scale=CD ** -0.5,
                                   bias=c_nm[:, h, t:t + 1], accum_out=c_sum[:, t, h:h + 1]).then_inc(S["c_probs"], 1)

            def output_high(half):
                for t in range(NT):
                    act.wait_ge(S["t_psum"], 4 * 5 + 2 * half + t + 1)
                    act.activation(xT_hi[:, t, 4 * half:4 * half + 4, :].rearrange("p k c -> p (k c)"),
                                   bank[2 * half + t][:], ACT.Copy).then_inc(S["xTh_ready"], 1)

            def mla_transposed_p(h):
                act.wait_ge(S["c_pt_psum"], h + 1)
                act.activation(c_pT[:, h % 2].rearrange("p a b -> p (a b)"), bank[4 + h % 2][:], ACT.Copy).then_inc(S["c_pt_ready"], 1)

            for h in range(CH + 1):
                if h < CH:
                    mla_probabilities(h)
                if h == CH:
                    output_high(0)
                if h >= 1:
                    mla_transposed_p(h - 1)
                if h in (3, 7):
                    high_half(sched["c_out"][1], h // 4)
            split[0] = sched["c_out"][1].index + 1
            output_high(1)
            c = sched["c_out"]
            high_upto(c[3].index + 1)
            for ch in c[:2]:
                high_upto(ch.index + 1 + SLOTS)
            c = sched["ffn2b"]
            enter(6, 6, 0, c[2].index + 1)
            squared_relu(1, 0)
            sum_squares(7, 0)
            sum_squares(7, 1)

        @block.vector
        def _(dve):
            chain = [0]

            def step(ins):
                chain[0] += 1
                ins.then_inc(S["dve_chain"], 1)
                dve.wait_ge(S["dve_chain"], chain[0])

            split = [0]

            def low(ch, it=0, stride=0):
                dve.wait_ge(S["hi_done"], ch.index + 1 + it * stride)
                dve.tensor_tensor(view(w_lo, ch), view(w_raw, ch), view(w_hi, ch).bitcast(F32),
                                  ALU.subtract).then_inc(S["lo_done"], 1)

            def low_half(ch, half):
                if half == 0:
                    dve.wait_ge(S["hi_done"], ch.index + 1)
                ins = dve.tensor_tensor(view(w_lo, ch)[:, half], view(w_raw, ch)[:, half],
                                        view(w_hi, ch)[:, half].bitcast(F32), ALU.subtract)
                if half:
                    ins.then_inc(S["lo_done"], 1)

            def low_upto(index):
                while split[0] < min(index, n_chunks):
                    low(order[split[0]])
                    split[0] += 1

            def normalise(n, t, dst):
                dve.wait_ge(S["gain_loaded"], 16 * (n + 1))
                dve.wait_ge(S["rstd_ready"], turn[n, t])
                for d in HALF_D:
                    dve.scalar_tensor_tensor(out=dst[:, t, d], in0=x_res[:, t, d], scalar=rstd[:, t:t + 1],
                                             in1=gain[:, n % 2, d], op0=ALU.mult, op1=ALU.mult).then_inc(S["xn_ready"], 1)

            def transposed_low(n, t, halves=(0, 1)):
                for half in halves:
                    dve.wait_ge(S["xTh_ready"], 4 * n + 2 * t + half + 1)
                    k = slice(4 * half, 4 * half + 4)
                    dve.tensor_tensor(xT_lo[:, t, k, :].rearrange("p k c -> p (k c)"), bank[2 * t + half][:],
                                      xT_hi[:, t, k, :].rearrange("p k c -> p (k c)").bitcast(F32),
                                      ALU.subtract).then_inc(S["xTl_ready"], 1)

            def add_residual(n, t, js=(0, 1)):
                for j in js:
                    d = HALF_D[j]
                    if (t, j) == (1, 1):
                        dve.wait_ge(S["mm_done"], sched[phase_of_norm[n]][-1].index + 1)
                    else:
                        dve.wait_ge(S["acc_done"], 3 * additions[n] + 2 * t + j + 1)
                    dve.tensor_tensor(x_res[:, t, d], x_res[:, t, d], bank[4 + 2 * t + j][:],
                                      ALU.add).then_inc(S["resid_ready"], 1)

            def enter(use, n, early, then):
                add_residual(n, 0)
                normalise(n, 0, x_norm)
                add_residual(n, 1, (0,))
                transposed_low(use, 0, (0,))
                add_residual(n, 1, (1,))
                transposed_low(use, 0, (1,))
                normalise(n, 1, x_norm)
                low_upto(early)
                transposed_low(use, 1)
                low_upto(then)

            def rope_angles():
                dve.wait_ge(S["pos_loaded"], 16)
                dve.wait_ge(S["consts_ready"], 3)
                step(dve.tensor_copy(pos_f[:], pos_i[:]))
                for t in range(NT):
                    step(dve.tensor_scalar(ang[:, t], freq[:], pos_f[:, t:t + 1], None, ALU.mult))
                magic = 1.5 * 2 ** 23
                step(dve.tensor_scalar(turns[:], ang[:], 1.0 / (2 * math.pi), magic, ALU.mult, ALU.add))
                step(dve.tensor_scalar(turns[:], turns[:], -magic, None, ALU.add))
                two_pi = (6.28125, 1.93500518798828125e-3, 3.01992e-7)
                two_pi = (two_pi[0], two_pi[1], 2 * math.pi - two_pi[0] - two_pi[1])
                for part in two_pi:
                    step(dve.scalar_tensor_tensor(out=ang[:], in0=turns[:], scalar=-part, in1=ang[:],
                                                  op0=ALU.mult, op1=ALU.add))
                limit = 3.141592
                step(dve.tensor_scalar(ang[:], ang[:], limit, -limit, ALU.min, ALU.max))
                step(dve.scalar_tensor_tensor(out=cosr[:], in0=ang[:], scalar=-1.0, in1=ang[:], op0=ALU.mult, op1=ALU.min))
                dve.tensor_scalar(cosr[:], cosr[:], math.pi / 2, None, ALU.add).then_inc(S["rope_angle"], 1)

            c = sched["swa_in"]
            normalise(0, 0, x_norm)
            for at, ready, done in ((slice(0, KT // 2), "head_hi", "head_lo"), (slice(KT // 2, KT), "hi_done", "lo_done")):
                dve.wait_ge(S[ready], 1)
                dve.tensor_tensor(view(w_lo, c[0])[:, at], view(w_raw, c[0])[:, at],
                                  view(w_hi, c[0])[:, at].bitcast(F32), ALU.subtract).then_inc(S[done], 1)
                if done == "head_lo":
                    transposed_low(0, 0)
            split[0] = 1
            normalise(0, 1, x_norm)
            transposed_low(0, 1)
            low_upto(2)
            low_upto(SLOTS)

            dve.wait_ge(S["mm_done"], c[1].index + 1)
            k_ps = bank[4][:].rearrange("p (f t) -> p f t", f=2)
            k_dst = swa_kT.rearrange("p (f r) t -> p f r t", r=2)
            for half in range(2):
                for dst in range(2):
                    last = dve.tensor_copy(k_dst[64 * dst:64 * dst + 64, :, half, :], k_ps[64 * half:64 * half + 64, :, :])
            last.then_inc(S["swa_k_ready"], 1)
            low_upto(c[1].index + 1 + SLOTS)
            dve.wait_ge(S["params_psum"], 1)
            dve.tensor_copy(pcols[:], bank[0][:, 0:48]).then_inc(S["params_ready"], 1)
            dve.wait_ge(S["wsT_psum"], 1)
            dve.tensor_copy(wsT[:], bank[1][:].rearrange("p (a b) -> p a b", a=BG)).then_inc(S["wsT_ready"], 1)
            dve.wait_ge(S["dist_step"], 3)
            dve.wait_ge(S["sinks_loaded"], 16)

            def swa_bias(g):
                hs = slice(4 * g, 4 * g + 4)
                if g >= 2:
                    dve.wait_ge(S["swa_pt_psum"], 3 * (g - 1))
                for at in (0, SWA_COLS + 1):
                    last = dve.tensor_copy(swa_s[:, g % 2, :, at:at + 1], sinks[:, hs].unsqueeze(2))
                for j in range(4):
                    h = 4 * g + j
                    dve.wait_ge(S["swa_scores"], h + 1)
                    slope = 2.0 ** (-8.0 * (h + 1) / NQH)
                    dve.scalar_tensor_tensor(out=swa_s[:, g % 2, j, 1:1 + SWA_COLS], in0=dist[:], scalar=-slope,
                                             in1=bank[h % 2][:, 0:SWA_COLS], op0=ALU.mult,
                                             op1=ALU.add).then_inc(S["swa_biased"], 1)
                    if j == 2 and g >= 2:
                        swa_operand(g - 2)
                dve.wait_ge(S["swa_biased"], 4 * g + 4)
                for t, (a, b) in enumerate(SWA_PARTS):
                    last = dve.tensor_reduce(swa_mx[:, t, hs], swa_s[:, g % 2, :, a:b], axis=AX, op=ALU.max)
                step(last)
                dve.tensor_scalar(swa_nm[:, :, hs], swa_mx[:, :, hs], -1.0, None, ALU.mult).then_inc(S["swa_nmax"], 1)

            def swa_output(g):
                hs = slice(4 * g, 4 * g + 4)
                dve.wait_ge(S["swa_probs"], 8 * (g + 1))
                step(dve.reciprocal(swa_rden[:, :, hs], swa_sum[:, :, hs]))
                dve.wait_ge(S["swa_o_psum"], g + 1)
                for t in range(NT):
                    r = swa_rden[:, t, hs].unsqueeze(2).broadcast_to([P, 4, HD])
                    dve.tensor_tensor(x_norm[:, t, 256 * g:256 * g + 256].rearrange("p (h d) -> p h d", d=HD),
                                      bank[3][:, 256 * t:256 * t + 256].rearrange("p (h d) -> p h d", d=HD), r,
                                      ALU.mult).then_inc(S["swa_o_ready"], 1)

            def swa_operand(g):
                dve.wait_ge(S["swa_oh_ready"], g + 1)
                k = slice(2 * g, 2 * g + 2)
                dve.tensor_tensor(xT_lo[:, :, k, :], bank[3][:].rearrange("p (t k c) -> p t k c", t=NT, k=2),
                                  xT_hi[:, :, k, :].bitcast(F32), ALU.subtract).then_inc(S["swa_ol_ready"], 1)

            o = sched["swa_out"]
            swa_bias(0)
            low_upto(c[2].index + 1 + SLOTS)
            swa_bias(1)
            low_upto(c[3].index + 1 + SLOTS)
            swa_output(0)
            swa_bias(2)
            low_upto(c[4].index + 1 + SLOTS)
            swa_output(1)
            swa_bias(3)
            low_upto(c[5].index + 1 + SLOTS)
            swa_output(2)
            low_upto(o[0].index + 1 + SLOTS)
            swa_operand(2)
            swa_output(3)
            swa_operand(3)
            low_upto(o[1].index + 1 + SLOTS)

            c = sched["ffn1"]

            def hidden(ch, i, it=0, buf=0):
                dve.wait_ge(S["ff1_sg"], i + 1 + it)
                dve.wait_ge(S["mm_done"], ch.index + 1 + 3 * it)
                dve.tensor_tensor(ff_h[:], ff_act[:], bank[1][:].rearrange("p (a b) -> p a b", a=2),
                                  ALU.mult).then_inc(S["ff1_h"], 1)
                dve.wait_ge(S["ff1_hi"], i + 1 + it)
                dve.tensor_tensor(ff_lo[buf][:], ff_h[:], ff_hi[buf][:].bitcast(F32), ALU.subtract).then_inc(S["ff1_lo"], 1)

            def first_hidden_low(high, count, ready):
                dve.wait_ge(S[high], count)
                dve.tensor_tensor(ff_lo[0][:], bank[2][:].rearrange("p (a b) -> p a b", a=2),
                                  ff_hi[0][:].bitcast(F32), ALU.subtract).then_inc(S[ready], 1)

            enter(1, 1, 0, c[3].index + 1)
            dve.wait_ge(S["ff1_sg"], 1)
            dve.wait_ge(S["mm_done"], c[1].index + 1)
            dve.tensor_tensor(ff_h[:], ff_act[:], bank[1][:].rearrange("p (a b) -> p a b", a=2),
                              ALU.mult).then_inc(S["ff1_h"], 1)
            first_hidden_low("ff1_hi", 1, "ff1_lo")
            low_upto(c[4].index + 1)
            low(c[5])
            low(c[6])
            hidden(c[4], 1)
            low(c[7])
            with dve.Fori(0, N1 - 4) as it:
                low(c[8], it, 3)
                low(c[9], it, 3)
                hidden(c[7], 2, it)
                low(c[10], it, 3)
            low(c[-4])
            hidden(c[-5], N1 - 2)
            for ch in c[-3:]:
                low(ch)
            hidden(c[-3], N1 - 1, buf=1)
            split[0] = c[-1].index + 1
            low_upto(c[-1].index + 1 + 1)

            c = sched["ab_in"]
            add_residual(2, 0)
            low_upto(c[1].index + 1)
            normalise(2, 0, x_res)
            add_residual(2, 1)
            normalise(3, 0, x_norm)
            normalise(2, 1, x_res)
            transposed_low(2, 0)
            normalise(3, 1, x_norm)
            low_upto(c[2].index + 1)
            transposed_low(2, 1)
            low_upto(c[0].index + SLOTS)
            dve.wait_ge(S["params_ready"], 1)
            for ch in c[0:3]:
                low_upto(ch.index + 1 + SLOTS)

            def conv(i):
                dve.wait_ge(S["qk_padded"], i + 1)
                dve.wait_ge(S["conv_begun"], i + 1)
                taps = [j for j in range(CONV) if j != CONV // 2]
                for j in taps:
                    for f in (2 * i, 2 * i + 1):
                        ins = dve.scalar_tensor_tensor(out=ab_cv[:, f], in0=ab_pad[:, f, j:j + SEQ],
                                                       scalar=pcols[:, 8 * j + f:8 * j + f + 1], in1=ab_cv[:, f],
                                                       op0=ALU.mult, op1=ALU.add)
                    if j != taps[-1]:
                        step(ins)
                    else:
                        ins.then_inc(S["conv_ready"], 1)

            conv(0)
            low_upto(c[3].index + 1 + SLOTS)
            dve.wait_ge(S["g4_loaded"], 64)
            forget = g4[:, 1:4:2, :]
            dve.scalar_tensor_tensor(out=g_w, in0=forget, scalar=-1.0, in1=forget, op0=ALU.mult,
                                     op1=ALU.min).then_inc(S["g_abs_ready"], 1)
            def gate_rows():
                dve.wait_ge(S["g_ln_ready"], 1)
                step(dve.scalar_tensor_tensor(out=g_w, in0=g4[:, 1:4:2, :], scalar=0.0, in1=g_w,
                                              op0=ALU.min, op1=ALU.subtract))
                ways = (slice(None), slice(None, None, -1))
                for d, w in enumerate(ways):
                    last = dve.tensor_tensor_scan(g_B[:, d, w], one[:].broadcast_to([AH, SEQ]), g_w[:, d, w], 0.0, ALU.mult, ALU.add)
                step(last)
                step(dve.tensor_tensor(g_am[:, 0:2], g4[:, 0:4:2, :], g_B, ALU.subtract))
                for d, w in enumerate(ways):
                    last = dve.tensor_tensor_scan(g_M[:, d, w], g_am[:, d, w], g_am[:, d, w], 0.0, ALU.max, ALU.max)
                step(last)
                dve.tensor_tensor(g_am[:, 2:4], g_B, g_M, ALU.add)
                dve.tensor_scalar(g_nM, g_M, -1.0, None, ALU.mult).then_inc(S["g_rows_ready"], 1)

            for i in range(1, 4):
                conv(i)
                low_upto(c[3 + i].index + 1 + SLOTS)
                if i == 1:
                    gate_rows()
            dve.wait_ge(S["g_cols_psum"], 1)
            dve.tensor_copy(ab_t.rearrange("p t k h -> p (t k h)"), bank[1][:, 0:32]).then_inc(S["g_cols_ready"], 1)
            low_upto(c[7].index + 1 + SLOTS)
            low_upto(c[8].index + 1 + SLOTS)
            dve.wait_ge(S["vb_ready"], 2)
            vb = ab_vb.rearrange("p t (g c) -> p (t g) c", c=P)
            step(dve.tensor_tensor(ab_sq[:], vb, vb, ALU.mult))
            dve.tensor_reduce(ab_ss[:], ab_sq[:], axis=AX, op=ALU.add).then_inc(S["vb_sumsq"], 1)

            def weighted_scores(h):
                dve.wait_ge(S["st_psum"], h + 1)
                dve.wait_ge(S["e_ready"], 4 * (h + 1))
                b = bank[2 + h % 2]
                for d, src, at, n in ((0, 0, 0, SEQ), (0, SEQ + P, 2 * P, P), (1, 0, 0, P), (1, SEQ, P, SEQ)):
                    e = ab_e[:, h % 2, d, at:at + n]
                    last = dve.scalar_tensor_tensor(out=e, in0=b[:, src:src + n], scalar=AD ** -0.5, in1=e,
                                                    op0=ALU.mult, op1=ALU.mult)
                last.then_inc(S["w_ready"], 1)

            def full_low(j):
                dve.wait_ge(S["ab_hi"], j + 1)
                k = ab_slot[j]
                dve.tensor_tensor(xT_lo[:, :, k, :], ab_cv[:, j, :].rearrange("p (t c) -> p t c", t=NT),
                                  xT_hi[:, :, k, :].bitcast(F32), ALU.subtract).then_inc(S["ab_lo"], 1)

            weighted_scores(0)
            dve.wait_ge(S["vb_rstd"], 1)
            dve.tensor_tensor(vb, vb, ab_rs.unsqueeze(2).broadcast_to([P, 8, P]), ALU.mult).then_inc(S["vn_ready"], 1)
            weighted_scores(1)
            dve.wait_ge(S["sp_psum"], 1)
            dve.wait_ge(S["u_ready"], 2)
            dve.wait_ge(S["ws_loaded"], 32)
            dve.wait_ge(S["qk_ready"], 1)
            for g in range(BG):
                sp_out = bank[6 + g // 2][:, (g % 2) * SEQ:(g % 2) * SEQ + SEQ].rearrange("p (n t) -> p n t", n=NT)
                last = dve.scalar_tensor_tensor(out=ab_sq[:, 2 * g:2 * g + 2, :], in0=sp_out, scalar=pcols[:, 44 + g:45 + g],
                                                in1=bs_all[:, g:g + 1, :].broadcast_to([P, NT, P]),
                                                op0=ALU.mult, op1=ALU.add)
                last.then_inc(S["sp_read"], 1)
            dve.wait_ge(S["sp_read"], BG)
            for g in range(BG):
                dve.tensor_tensor(ab_cv[:, g].rearrange("p (n t) -> p n t", n=NT), ab_sq[:, 2 * g:2 * g + 2, :],
                                  ab_u[:, g].rearrange("p (n t) -> p n t", n=NT), ALU.mult).then_inc(S["ab_full"], 1)
            weighted_scores(2)
            low_upto(c[9].index + 1 + SLOTS)

            def sumsq_of_outputs(p):
                hs = slice(2 * p, 2 * p + 2)
                dve.wait_ge(S["num_ready"], 4 * (p + 1))
                dve.wait_ge(S["g_em_ready"], 1)
                for d in range(2):
                    den = ab_num[:, d, hs, :, AD]
                    last = dve.scalar_tensor_tensor(out=ab_dd[:, d, hs], in0=den, scalar=-1.0, in1=den,
                                                    op0=ALU.mult, op1=ALU.max)
                step(last)
                for d in range(2):
                    last = dve.tensor_tensor(ab_dd[:, d, hs], ab_dd[:, d, hs], ab_em[:, d, :, hs].rearrange("p t h -> p h t"),
                                             ALU.max)
                step(last)
                step(dve.reciprocal(ab_rd[:, :, hs], ab_dd[:, :, hs]))
                for d in range(2):
                    n = ab_num[:, d, hs, :, 0:AD]
                    last = dve.tensor_tensor(n, n, ab_rd[:, d, hs].unsqueeze(3).broadcast_to([P, 2, NT, AD]), ALU.mult)
                step(last)
                hsum = ab_num[:, 0, hs, :, 0:AD]
                step(dve.tensor_tensor(hsum, hsum, ab_num[:, 1, hs, :, 0:AD], ALU.add))
                step(dve.tensor_tensor(sq[:, hs], hsum, hsum, ALU.mult))
                dve.tensor_reduce(ab_ss[:, 4 * p:4 * p + 4], ab_sq[:, 4 * p:4 * p + 4], axis=AX,
                                  op=ALU.add).then_inc(S["h_sumsq"], 1)

            def normalised_outputs(p):
                hs = slice(2 * p, 2 * p + 2)
                dve.wait_ge(S["h_rstd"], p + 1)
                rs = ab_rs[:, 4 * p:4 * p + 4].rearrange("p (h t) -> p h t", t=NT).unsqueeze(3).broadcast_to([P, 2, NT, AD])
                dve.tensor_tensor(sq[:, hs], ab_num[:, 0, hs, :, 0:AD], rs, ALU.mult).then_inc(S["hn_ready"], 1)

            def gated_outputs(p):
                dve.wait_ge(S["sig_ready"], p + 1)
                dve.wait_ge(S["hT_psum"], p + 1)
                for h in (2 * p, 2 * p + 1):
                    dve.scalar_tensor_tensor(out=ab_cv[:, 4 + h], in0=bank[2 + p][:, (h % 2) * SEQ:(h % 2) * SEQ + SEQ],
                                             scalar=pcols[:, 40 + h:41 + h], in1=ab_sig[:, h],
                                             op0=ALU.mult, op1=ALU.mult).then_inc(S["ab_full"], 1)

            sq = ab_sq.rearrange("p (h t) c -> p h t c", t=NT)
            sumsq_of_outputs(0)
            weighted_scores(3)
            low_upto(c[10].index + 1 + SLOTS)
            normalised_outputs(0)
            for j in range(4):
                full_low(j)
            gated_outputs(0)
            sumsq_of_outputs(1)
            low_upto(c[11].index + 1 + SLOTS)
            normalised_outputs(1)
            full_low(4)
            full_low(5)
            gated_outputs(1)
            low_upto(c[12].index + 1 + SLOTS)
            full_low(6)
            full_low(7)
            o = sched["ab_out"]
            low_upto(o[0].index + 1 + SLOTS)
            low_upto(o[1].index + 1 + SLOTS)
            enter(3, 4, 0, sched["ffn2a"][2].index + 1)

            def hidden2(f, i, buf, it=0):
                dve.wait_ge(S["ff2_relu"], N2 * f + i + 1 + 2 * it)
                dve.tensor_tensor(ff_h[:], ff_act[:], ff_act[:], ALU.mult).then_inc(S["ff2_h"], 1)
                dve.wait_ge(S["ff2_h"], N2 * f + i + 1 + 2 * it)
                dve.wait_ge(S["ff2_hi"], N2 * f + i + 1 + 2 * it)
                dve.tensor_tensor(ff_lo[buf][:], ff_h[:], ff_hi[buf][:].bitcast(F32), ALU.subtract).then_inc(S["ff2_lo"], 1)

            def squared_relu(f, after):
                c = sched[ffn_phases[f]]
                dve.wait_ge(S["ff2_relu"], N2 * f + 1)
                dve.tensor_tensor(ff_h[:], ff_act[:], ff_act[:], ALU.mult).then_inc(S["ff2_h"], 1)
                first_hidden_low("ff2_hi", N2 * f + 1, "ff2_lo")
                low_upto(c[4].index + 1)
                hidden2(f, 1, 1)
                low_upto(c[5].index + 1)
                if f == 0:
                    rope_angles()
                with dve.Fori(0, N2 // 2 - 2) as it:
                    low(c[6], it, 4)
                    hidden2(f, 2, 0, it)
                    low(c[7], it, 4)
                    low(c[8], it, 4)
                    hidden2(f, 3, 1, it)
                    low(c[9], it, 4)
                split[0] = c[-3].index + 1
                low_upto(c[-2].index + 1)
                hidden2(f, N2 - 2, 0)
                low_upto(c[-1].index + 2)
                hidden2(f, N2 - 1, 1)
                low_upto(c[-1].index + 1 + after)

            squared_relu(0, 2)

            c = sched["c_in"]
            enter(4, 5, c[2].index + 1, c[0].index + SLOTS)
            dve.wait_ge(S["rope_ready"], 1)
            dve.wait_ge(S["cgain_loaded"], 32)

            def latents(t):
                dve.wait_ge(S["c_rstd"], t + 1)
                for j, a, b in ((0, 0, QL), (1, QL, QL + KVL)):
                    dve.scalar_tensor_tensor(out=x_norm[:, t, a:b], in0=c_lat[:, t, a:b], scalar=c_rs[:, t, j:j + 1],
                                             in1=c_gain[:, a:b], op0=ALU.mult, op1=ALU.mult).then_inc(S["c_cn_ready"], 1)

            def latents_low(t):
                for half, n in ((0, 4), (1, 1)):
                    dve.wait_ge(S["c_xh"], 2 * t + half + 1)
                    k = slice(4 * half, 4 * half + n)
                    dve.tensor_tensor(xT_lo[:, t, k, :].rearrange("p k c -> p (k c)"), bank[2 * t + half][:, 0:n * P],
                                      xT_hi[:, t, k, :].rearrange("p k c -> p (k c)").bitcast(F32),
                                      ALU.subtract).then_inc(S["c_xl"], 1)

            def rope_key(t):
                x1, x2 = c_lat[:, t, QL + KVL:QL + KVL + HALF], c_lat[:, t, QL + KVL + HALF:CIN]
                dve.tensor_tensor(c_krt[:, 0, t], x1, cos[:, t], ALU.mult)
                dve.tensor_tensor(c_krt[:, 1, t], x2, sin[:, t], ALU.mult)
                dve.tensor_tensor(c_krt[:, 2, t], x1, sin[:, t], ALU.mult)
                step(dve.tensor_tensor(c_krt[:, 3, t], x2, cos[:, t], ALU.mult))
                dve.tensor_tensor(c_kr[:, t, 0:HALF], c_krt[:, 0, t], c_krt[:, 1, t], ALU.subtract)
                step(dve.tensor_tensor(c_kr[:, t, HALF:CR], c_krt[:, 2, t], c_krt[:, 3, t], ALU.add))
                kr_all = c_k[:, t].rearrange("p (h e) -> p h e", e=CD)[:, :, CN:CD]
                step(dve.tensor_copy(kr_all, c_kr[:, t:t + 1, :].broadcast_to([P, CH, CR])))

            def rope_q(t):
                q = c_q[:, t].rearrange("p (h e) -> p h e", e=CD)
                x1, x2 = q[:, :, CN:CN + HALF], q[:, :, CN + HALF:CD]
                cs = cos[:, t:t + 1, :].broadcast_to([P, CH, HALF])
                sn = sin[:, t:t + 1, :].broadcast_to([P, CH, HALF])
                tmp = [c_tmp[:, i].rearrange("p (h e) -> p h e", e=HALF) for i in range(4)]
                dve.tensor_tensor(tmp[0], x1, cs, ALU.mult)
                dve.tensor_tensor(tmp[1], x2, sn, ALU.mult)
                dve.tensor_tensor(tmp[2], x1, sn, ALU.mult)
                step(dve.tensor_tensor(tmp[3], x2, cs, ALU.mult))
                dve.tensor_tensor(x1, tmp[0], tmp[1], ALU.subtract)
                ins = dve.tensor_tensor(x2, tmp[2], tmp[3], ALU.add)
                if t == 0:
                    step(ins)
                else:
                    ins.then_inc(S["c_rope_ready"], 1)

            def queries(i):
                dve.wait_ge(S["mm_done"], sched["c_uq"][i].index + 1)
                dve.tensor_copy(c_q[:, 1, i * 512:(i + 1) * 512], bank[C_UQ_BANK[i][1]][:]).then_inc(S["c_q1_ready"], 1)

            def keys_values(i):
                dve.wait_ge(S["mm_done"], sched["c_ukv"][i].index + 1)
                for n in range(2):
                    for src, dst in kv_parts(i, n, 1):
                        last = dve.tensor_copy(dst, src)
                last.then_inc(S["c_kv1_ready"], 1)

            q = sched["c_uq"]
            latents(0)
            low_upto(c[0].index + 1 + SLOTS)
            latents_low(0)
            low_upto(c[1].index + 1 + SLOTS)
            latents(1)
            low_upto(c[2].index + 1 + SLOTS)
            rope_key(0)
            latents_low(1)
            rope_key(1)
            dve.wait_ge(S["c_q_ready"], 3)
            rope_q(0)
            queries(0)
            low_upto(q[0].index + 1 + SLOTS)
            queries(1)
            queries(2)
            dve.wait_ge(S["c_q1_ready"], 3)
            rope_q(1)
            keys_values(0)
            def mla_qk(h):
                dve.wait_ge(S["c_qkT_psum"], h + 1)
                dve.tensor_copy(c_qkT[0:CD, h % 2].rearrange("p a b -> p (a b)"), bank[h % 2][0:CD, :]).then_inc(S["c_qkT_ready"], 1)

            mla_qk(0)
            low_upto(q[1].index + 1 + SLOTS)
            keys_values(1)

            def mla_max(h):
                dve.wait_ge(S["c_scores"], h + 1)
                step(dve.tensor_reduce(c_mx[:, h], bank[2 + h % 2][:].rearrange("p (t k) -> p t k", t=NT), axis=AX, op=ALU.max))
                dve.tensor_scalar(c_nm[:, h], c_mx[:, h], -(CD ** -0.5), None, ALU.mult).then_inc(S["c_nmax"], 1)

            def output_low(half):
                for t in range(NT):
                    dve.wait_ge(S["xTh_ready"], 4 * 5 + 2 * half + t + 1)
                    k = slice(4 * half, 4 * half + 4)
                    dve.tensor_tensor(xT_lo[:, t, k, :].rearrange("p k c -> p (k c)"), bank[2 * half + t][:],
                                      xT_hi[:, t, k, :].rearrange("p k c -> p (k c)").bitcast(F32),
                                      ALU.subtract).then_inc(S["xTl_ready"], 1)

            def mla_output(half):
                dve.wait_ge(S["c_o_psum"], 8 * half + 8)
                hs = slice(8 * half, 8 * half + 8)
                step(dve.reciprocal(c_rden[:, :, hs], c_sum[:, :, hs]))
                for t in range(NT):
                    r = c_rden[:, t, hs].unsqueeze(2).broadcast_to([P, 8, CV])
                    dve.tensor_tensor(x_norm[:, t, 512 * half:512 * half + 512].rearrange("p (h d) -> p h d", d=CV),
                                      bank[6 + t][:].rearrange("p (h d) -> p h d", d=CV), r, ALU.mult).then_inc(S["c_o_ready"], 1)

            for h in range(CH + 1):
                if 0 < h < CH:
                    mla_qk(h)
                if h >= 1:
                    mla_max(h - 1)
                if h in (9, 13):
                    low_half(sched["c_out"][1], h // 13)
                if h == 10:
                    mla_output(0)
            split[0] = sched["c_out"][1].index + 1
            output_low(0)
            mla_output(1)
            output_low(1)
            c = sched["c_out"]
            low_upto(c[3].index + 1)
            low_upto(c[0].index + 1 + SLOTS)
            low_upto(c[1].index + 1 + SLOTS)
            enter(6, 6, 0, sched["ffn2b"][2].index + 1)
            squared_relu(1, 0)
            for t in range(NT):
                add_residual(7, t)
                normalise(7, t, x_norm)

        @block.tensor
        def _(pe):
            def product(out, sh, sl, mh, ml, first, last):
                pe.matmul(out, sh, mh, start=first, stop=False)
                pe.matmul(out, sh, ml, start=False, stop=False)
                return pe.matmul(out, sl, mh, start=False, stop=last)

            def arrived(ch, it=0, stride=0):
                pe.wait_ge(S["lo_done"], ch.index + 1 + it * stride)

            def feature_major(ch, dst, between=None):
                hi, lo = view(w_hi, ch), view(w_lo, ch)
                n = ch.shape[1]
                for f in range(max(1, n // P)):
                    w = min(n, P)
                    o = dst[0:w, f * SEQ:(f + 1) * SEQ].rearrange("p (t c) -> p t c", t=NT)
                    if f == 1 and between:
                        between()
                    for k in range(KT):
                        last = product(o, hi[:, k, f * w:(f + 1) * w], lo[:, k, f * w:(f + 1) * w],
                                       xT_hi[:, :, k, :], xT_lo[:, :, k, :], k == 0, k == KT - 1)
                last.then_inc(S["mm_done"], 1)

            def token_major(ch, dst, kts=KT, k0=0, ts=(0, 1), tile0=None, low_count=None):
                hi, lo = view(w_hi, ch), view(w_lo, ch)
                for t in ts:
                    for k in range(kts):
                        if low_count and k % 4 == 0:
                            pe.wait_ge(S["xTl_ready"], low_count + k // 4)
                        if ch.index == 0 and t == 0 and k == KT // 2:
                            arrived(ch)
                        last = product(dst[t], xT_hi[:, t, k0 + k, :], xT_lo[:, t, k0 + k, :], hi[:, k, :], lo[:, k, :],
                                       k == 0, k == kts - 1)
                    if t == 0 and tile0:
                        last.then_inc(S[tile0], 1)
                    if t == NT - 1:
                        last.then_inc(S["mm_done"], 1)

            def accumulate(ch, stat_hi, stat_lo, first=False, end=False, ts=(0, 1), phase_end=False, norm=None,
                           before=()):
                hi, lo = view(w_hi, ch), view(w_lo, ch)
                for t in ts:
                    for j in range(2):
                        if before and before[0] == (t, j):
                            before[1]()
                        if norm and (t, j) == (1, 1):
                            transpose_tile(0, norm)
                        for k in range(2):
                            last = product(bank[4 + 2 * t + j][:], stat_hi(t, k), stat_lo(t, k),
                                           hi[:, k, 512 * j:512 * j + 512], lo[:, k, 512 * j:512 * j + 512],
                                           first and k == 0, end and k == 1)
                        if phase_end and (t, j) != (1, 1):
                            last.then_inc(S["acc_done"], 1)
                    if t == NT - 1:
                        last.then_inc(S["mm_done"], 1)

            def operand_out(ch, i, **more):
                arrived(ch)
                accumulate(ch, lambda t, k: xT_hi[:, t, 2 * i + k, :], lambda t, k: xT_lo[:, t, 2 * i + k, :], **more)

            def transpose_tile(t, n=None):
                for half in range(2):
                    if n is not None:
                        pe.wait_ge(S["xn_ready"], half_turn(n, t, half))
                    for k in range(4):
                        kk = 4 * half + k
                        last = pe.transpose(bank[2 * t + half][:, k * P:(k + 1) * P],
                                            x_norm[:, t, kk * P:(kk + 1) * P], ident[:])
                    last.then_inc(S["t_psum"], 1)

            def enter(use, n, visits, before_last=None):
                if n in (0, 3):
                    transpose_tile(0, n)
                visits[0](0, low_count=4 * use + 1)
                transpose_tile(1, n)
                for visit in visits[1:]:
                    visit(0)
                for visit in visits:
                    if before_last and visit is visits[-1]:
                        before_last()
                    if visit is visits[0]:
                        visit(1, low_count=4 * use + 3)
                    else:
                        visit(1)

            def whole(ch, dst, **more):
                arrived(ch)
                feature_major(ch, dst, **more)

            def hidden_transposes(ready, count, done):
                def blocks():
                    pe.wait_ge(S[ready], count)
                    for k in range(2):
                        for t in range(NT):
                            at = (NT * k + t) * P
                            last = pe.transpose(bank[2][:, at:at + P], ff_h[:, t, k * P:(k + 1) * P], ident[:])
                    last.then_inc(S[done], 1)
                return blocks

            def halves(b):
                return [bank[b][:, t * CW:(t + 1) * CW] for t in range(NT)]

            def by_tile(ch, dst, **more):
                def visit(t, low_count=None):
                    if t == 0 and ch.index == 0:
                        pe.wait_ge(S["head_lo"], 1)
                    elif t == 0:
                        arrived(ch)
                    token_major(ch, dst, ts=(t,), low_count=low_count, **more)
                return visit

            pe.wait_ge(S["consts_ready"], 1)
            c = sched["swa_in"]

            enter(0, 0, [by_tile(c[0], halves(5))])
            whole(c[1], bank[4])

            def swa_queries(i):
                arrived(c[2 + i])
                if i == 2:
                    pe.wait_ge(S["swa_k_ready"], 1)
                if i == 3:
                    pe.wait_ge(S["swa_v_ready"], 1)
                feature_major(c[2 + i], bank[(6, 7, 4, 5)[i]])

            swa_queries(0)
            pe.wait_ge(S["consts_ready"], 2)
            pe.wait_ge(S["small_loaded"], 64)
            pe.transpose(bank[0][:, 0:48], prows, ident[0:48, 0:48]).then_inc(S["params_psum"], 1)
            pe.wait_ge(S["ws_loaded"], 32)
            for g in range(BG):
                last = pe.transpose(bank[1][:, g * P:(g + 1) * P], ws[:, g, :], ident[:])
            last.then_inc(S["wsT_psum"], 1)
            swa_queries(1)
            pe.wait_ge(S["params_ready"], 1)
            pe.wait_ge(S["wsT_ready"], 1)

            def swa_scores(h):
                pe.wait_ge(S["swa_q_ready"], h // 4 + 1)
                if h >= 2:
                    pe.wait_ge(S["swa_biased"], h - 1)
                at = slice(64 * (h % 2), 64 * (h % 2) + 64)
                b = bank[h % 2]
                kv = h // (NQH // NKV)
                pe.matmul(b[:, 0:P], swa_qT[at, h // 2, 0:P], swa_kT[at, kv, 0:P], start=True, stop=True)
                pe.matmul(b[:, P:SWA_COLS], swa_qT[at, h // 2, P:SEQ], swa_kT[at, kv, :],
                          start=True, stop=True).then_inc(S["swa_scores"], 1)

            def swa_transposes(g, u):
                n = 3 * g + u
                if u == 0:
                    pe.wait_ge(S["swa_probs"], 8 * (g + 1))
                if n >= 1 and SWA_PT_BANK[g][u] == 2:
                    pe.wait_ge(S["swa_pt_ready"], n)
                for b in range(4):
                    j, part = (4 * u + b) // 3, (4 * u + b) % 3
                    last = pe.transpose(bank[SWA_PT_BANK[g][u]][:, b * P:(b + 1) * P],
                                        swa_s[:, g % 2, j, 1 + part * P:1 + (part + 1) * P], ident[:])
                last.then_inc(S["swa_pt_psum"], 1)

            def scores_and_transposes(g):
                for j in range(4):
                    if g + 1 < 4:
                        swa_scores(4 * (g + 1) + j)
                    if j == 2 and g >= 1:
                        swa_operand(g - 1)
                    if 0 <= g and j < 3:
                        swa_transposes(g, j)

            def swa_values(g):
                pe.wait_ge(S["swa_pt_ready"], 3 * (g + 1))
                if g >= 1:
                    pe.wait_ge(S["swa_ol_ready"], g)
                v = [swa_v[:, t, g * HD:(g + 1) * HD] for t in range(NT)]
                pt = swa_pT[:, g % 2]
                for j in range(4):
                    o = [bank[3][:, CW * t + j * HD:CW * t + (j + 1) * HD] for t in range(NT)]
                    pe.matmul(o[0], pt[:, 3 * j, :], v[0], start=True, stop=True)
                    pe.matmul(o[1], pt[:, 3 * j + 1, :], v[0], start=True, stop=False)
                    last = pe.matmul(o[1], pt[:, 3 * j + 2, :], v[1], start=False, stop=True)
                last.then_inc(S["swa_o_psum"], 1)

            def swa_operand(g):
                pe.wait_ge(S["swa_o_ready"], 2 * (g + 1))
                for t in range(NT):
                    for k in range(2):
                        at = (2 * t + k) * P
                        kk = 2 * g + k
                        last = pe.transpose(bank[3][:, at:at + P], x_norm[:, t, kk * P:(kk + 1) * P], ident[:])
                last.then_inc(S["swa_oT_psum"], 1)

            o = sched["swa_out"]
            pe.wait_ge(S["swa_k_ready"], 1)
            scores_and_transposes(-1)
            swa_queries(2)
            scores_and_transposes(0)
            swa_queries(3)
            pe.wait_ge(S["swa_v_ready"], 1)
            swa_values(0)
            scores_and_transposes(1)
            pe.wait_ge(S["swa_q_ready"], 4)
            swa_values(1)
            operand_out(o[0], 0, first=True)
            scores_and_transposes(2)
            swa_values(2)
            operand_out(o[1], 1, before=((1, 1), lambda: scores_and_transposes(3)))
            swa_values(3)
            pe.wait_ge(S["swa_ol_ready"], 3)
            operand_out(o[2], 2, ts=(0,), before=((0, 1), lambda: swa_operand(3)))
            pe.wait_ge(S["swa_ol_ready"], 4)
            operand_out(o[3], 3, ts=(0,), end=True, phase_end=True)
            operand_out(o[2], 2, ts=(1,))
            operand_out(o[3], 3, ts=(1,), end=True, phase_end=True, norm=1)

            c = sched["ffn1"]

            def down(ch, i, it=0, buf=0, **more):
                arrived(ch, it, 3)
                pe.wait_ge(S["ff1_lo"], i + 1 + it)
                accumulate(ch, lambda t, k: ff_hi[buf][:, k, t * P:(t + 1) * P],
                           lambda t, k: ff_lo[buf][:, k, t * P:(t + 1) * P], **more)

            def gate(ch, i, it=0, **more):
                arrived(ch, it, 3)
                pe.wait_ge(S["ff1_sg"], i + it)
                feature_major(ch, bank[0], **more)

            enter(1, 1, [by_tile(c[0], halves(0)), by_tile(c[1], halves(1))])
            gate(c[2], 1, between=hidden_transposes("ff1_h", 1, "ff1_t"))
            down(c[3], 0, first=True)
            arrived(c[4])
            feature_major(c[4], bank[1])
            with pe.Fori(0, N1 - 3) as it:
                gate(c[5], 2, it)
                down(c[6], 1, it)
                arrived(c[7], it, 3)
                feature_major(c[7], bank[1])
            gate(c[-4], N1 - 1)
            arrived(c[-3])
            pe.wait_ge(S["ff1_h"], N1 - 1)
            feature_major(c[-3], bank[1])
            down(c[-2], N1 - 2, ts=(0,))
            down(c[-1], N1 - 1, buf=1, ts=(0,), end=True, phase_end=True)
            down(c[-2], N1 - 2, ts=(1,))
            down(c[-1], N1 - 1, buf=1, ts=(1,), end=True, phase_end=True)

            c = sched["ab_in"]

            def projection(i):
                arrived(c[i])
                if i in (7, 8):
                    token_major(c[i], halves(AB_BANK[i]))
                else:
                    feature_major(c[i], bank[AB_BANK[i]])

            enter(2, 3, [by_tile(c[i], halves(AB_BANK[i])) for i in range(2)])
            for i in range(2, 9):
                if i == 8:
                    pe.wait_ge(S["g_raw_ready"], 1)
                projection(i)
                if i == 8:
                    pe.wait_ge(S["g_rows_ready"], 1)
                    pe.wait_ge(S["qk_padded"], 1)
                    for t in range(NT):
                        for k in range(4):
                            at = 16 * t + 4 * k
                            last = pe.transpose(bank[1][:, at:at + 4], g_am[:, k, t * P:(t + 1) * P], ident[0:AH, 0:AH])
                    last.then_inc(S["g_cols_psum"], 1)

            def decay_rows(h):
                if h == 0:
                    pe.wait_ge(S["vb_ready"], 2)
                if h == 1:
                    pe.wait_ge(S["g_cols_ready"], 1)
                if h >= 2:
                    pe.wait_ge(S["e_exp"], 4 * (h - 1))
                pe.matmul(bank[h % 2][:], sel[:, h, :], g_nM.rearrange("p d t -> p (d t)"),
                          start=True, stop=True).then_inc(S["nM_psum"], 1)

            def scores_T(h):
                if h == 0:
                    pe.wait_ge(S["qk_ready"], 1)
                    pe.wait_ge(S["v1_ready"], 2)
                if h >= 2:
                    pe.wait_ge(S["w_ready"], h - 1)
                b = bank[2 + h % 2]
                q, k = ab_pad[:, h, 0:SEQ], ab_pad[:, AH + h, 0:SEQ]
                pe.matmul(b[:, 0:SEQ], k[:, 0:P], q, start=True, stop=True)
                pe.matmul(b[:, SEQ:2 * SEQ], k[:, P:SEQ], q, start=True, stop=True).then_inc(S["st_psum"], 1)

            def summed(h):
                pe.wait_ge(S["w_ready"], h + 1)
                for d in range(2):
                    if h == 0:
                        pe.wait_ge(S["v1_ready"], 2)
                    else:
                        pe.wait_ge(S["num_ready"], 2 * (h - 1) + d + 1)
                    b = bank[4 + d]
                    w = ab_e[:, h % 2, d]
                    blocks = ((0, ((0, 0),)), (1, ((0, P), (1, 2 * P)))) if d == 0 else ((0, ((0, 0), (1, P))), (1, ((1, 2 * P),)))
                    for t, srcs in blocks:
                        for m, (s, at) in enumerate(srcs):
                            last = pe.matmul(b[:, t * (AD + 1):(t + 1) * (AD + 1)], w[:, at:at + P], ab_v1[:, s, h, :],
                                             start=m == 0, stop=m == len(srcs) - 1)
                    last.then_inc(S["num_psum"], 1)

            def spatial_mixing():
                pe.wait_ge(S["vn_ready"], 1)
                pe.wait_ge(S["u_ready"], 2)
                for g in range(BG):
                    for n in range(NT):
                        at = (g % 2) * SEQ + n * P
                        last = pe.matmul(bank[6 + g // 2][:, at:at + P], ab_vb[:, n, g * P:(g + 1) * P], wsT[:, g, :],
                                         start=True, stop=True)
                last.then_inc(S["sp_psum"], 1)

            pe.wait_ge(S["qk_padded"], 4)
            projection(9)
            decay_rows(0)
            decay_rows(1)
            projection(10)
            scores_T(0)
            scores_T(1)
            summed(0)
            decay_rows(2)
            spatial_mixing()
            scores_T(2)
            summed(1)
            decay_rows(3)
            pe.wait_ge(S["sp_read"], BG)
            projection(11)
            scores_T(3)
            summed(2)

            def outputs_T(p):
                pe.wait_ge(S["hn_ready"], p + 1)
                for h in (2 * p, 2 * p + 1):
                    for t in range(NT):
                        at = (h % 2) * SEQ + t * P
                        last = pe.transpose(bank[2 + p][:, at:at + P], ab_sq[:, 2 * h + t, :], ident[:])
                last.then_inc(S["hT_psum"], 1)

            projection(12)
            outputs_T(0)
            summed(3)
            o = sched["ab_out"]
            pe.wait_ge(S["ab_lo"], 4)
            pe.wait_ge(S["num_ready"], 8)
            pe.wait_ge(S["sig_ready"], 2)
            operand_out(o[0], AB_OUT_ORDER[0], first=True)
            operand_out(o[1], AB_OUT_ORDER[1], ts=(0,))
            outputs_T(1)
            operand_out(o[1], AB_OUT_ORDER[1], ts=(1,))
            for t in range(NT):
                if t == 0:
                    pe.wait_ge(S["ab_lo"], 6)
                operand_out(o[2], AB_OUT_ORDER[2], ts=(t,))
                if t == 0:
                    pe.wait_ge(S["ab_lo"], 8)
                operand_out(o[3], AB_OUT_ORDER[3], ts=(t,), end=True, phase_end=True, norm=4)

            def up2(ch, buf, it=0):
                arrived(ch, it, 4)
                feature_major(ch, bank[buf])

            def down2(f, ch, i, buf, it=0, **more):
                arrived(ch, it, 4)
                pe.wait_ge(S["ff2_lo"], N2 * f + i + 1 + 2 * it)
                accumulate(ch, lambda t, k: ff_hi[buf][:, k, t * P:(t + 1) * P],
                           lambda t, k: ff_lo[buf][:, k, t * P:(t + 1) * P], **more)

            def squared_relu(f, use, n):
                c = sched[ffn_phases[f]]
                enter(use, n, [by_tile(c[0], halves(0))])
                whole(c[1], bank[1], between=hidden_transposes("ff2_h", N2 * f + 1, "ff2_t"))
                down2(f, c[2], 0, 0, first=True)
                up2(c[3], 0)
                down2(f, c[4], 1, 1)
                up2(c[5], 1)
                with pe.Fori(0, N2 // 2 - 2) as it:
                    down2(f, c[6], 2, 0, it)
                    up2(c[7], 0, it)
                    down2(f, c[8], 3, 1, it)
                    up2(c[9], 1, it)
                for t in range(NT):
                    down2(f, c[-2], N2 - 2, 0, ts=(t,))
                    down2(f, c[-1], N2 - 1, 1, ts=(t,), end=True, phase_end=True, norm=(5, None)[f])

            squared_relu(0, 3, 4)

            c = sched["c_in"]
            visits = []
            for i, ch in enumerate(c):
                n = ch.shape[1]
                dst = [bank[4 + 2 * t + i // 2][:, (i % 2) * CW:(i % 2) * CW + n] for t in range(NT)]
                visits.append(by_tile(ch, dst, tile0="c_in0_done" if i == 2 else None))
            def latents(t):
                pe.wait_ge(S["c_cn_ready"], 2 * t + 2)
                for half, n in ((0, 4), (1, 1)):
                    for k in range(n):
                        kk = 4 * half + k
                        last = pe.transpose(bank[2 * t + half][:, k * P:(k + 1) * P], x_norm[:, t, kk * P:(kk + 1) * P], ident[:])
                    last.then_inc(S["c_t_psum"], 1)

            enter(4, 5, visits, before_last=lambda: latents(0))

            def queries(i, t):
                ch = sched["c_uq"][i]
                arrived(ch)
                token_major(ch, [bank[b][:] for b in C_UQ_BANK[i]], QL // P, ts=(t,), tile0="c_uq0_done")

            def keys_values(i, t):
                ch = sched["c_ukv"][i]
                arrived(ch)
                hi, lo = view(w_hi, ch), view(w_lo, ch)
                for n in range(2):
                    for k in range(2):
                        last = product(bank[C_UKV_BANK[i][n][t]][:], xT_hi[:, t, 3 + k, :], xT_lo[:, t, 3 + k, :],
                                       hi[:, k, 512 * n:512 * n + 512], lo[:, k, 512 * n:512 * n + 512], k == 0, k == 1)
                if t == NT - 1:
                    last.then_inc(S["mm_done"], 1)

            pe.wait_ge(S["c_xl"], 2)
            queries(0, 0)
            pe.wait_ge(S["c_lat_ready"], 4)
            queries(1, 0)
            queries(2, 0)
            latents(1)
            pe.wait_ge(S["c_q_ready"], 2)
            keys_values(0, 0)
            pe.wait_ge(S["c_xl"], 4)
            for i in range(3):
                queries(i, 1)
            keys_values(0, 1)
            pe.wait_ge(S["c_q1_ready"], 2)
            keys_values(1, 0)

            def mla_qk(h):
                if h == 0:
                    pe.wait_ge(S["c_q_ready"], 3)
                    pe.wait_ge(S["c_rope_ready"], 1)
                if h in (0, CH // 2):
                    pe.wait_ge(S["c_kv0_ready"], 2 * h // CH + 1)
                    pe.wait_ge(S["c_kv1_ready"], 2 * h // CH + 1)
                if h >= 2:
                    pe.wait_ge(S["c_qkT_ready"], h - 1)
                b = bank[h % 2]
                for i, src in enumerate((c_q, c_k)):
                    for t in range(NT):
                        at = (2 * i + t) * P
                        last = pe.transpose(b[0:CD, at:at + P], src[:, t, h * CD:(h + 1) * CD], ident[:])
                last.then_inc(S["c_qkT_psum"], 1)

            def mla_scores(h):
                pe.wait_ge(S["c_qkT_ready"], h + 1)
                if h >= 2:
                    pe.wait_ge(S["c_probs"], 2 * (h - 1))
                b = bank[2 + h % 2]
                qk = c_qkT[0:CD, h % 2]
                for t in range(NT):
                    last = pe.matmul(b[:, t * SEQ:(t + 1) * SEQ], qk[:, t, :], qk[:, 2:4, :].rearrange("p a b -> p (a b)"),
                                     start=True, stop=True)
                last.then_inc(S["c_scores"], 1)

            def mla_pT(h):
                pe.wait_ge(S["c_probs"], 2 * (h + 1))
                if h == 0:
                    pe.wait_ge(S["c_kv0_ready"], 2)
                    pe.wait_ge(S["c_kv1_ready"], 2)
                b = bank[4 + h % 2]
                for t in range(NT):
                    for k in range(2):
                        at = (2 * t + k) * P
                        last = pe.transpose(b[:, at:at + P], c_p[:, h % 2, t, k * P:(k + 1) * P], ident[:])
                last.then_inc(S["c_pt_psum"], 1)

            def mla_values(h):
                pe.wait_ge(S["c_pt_ready"], h + 1)
                if h == 8:
                    pe.wait_ge(S["c_o_ready"], 2)
                o = slice((h % 8) * CV, (h % 8) * CV + CV)
                for t in range(NT):
                    for k in range(2):
                        last = pe.matmul(bank[6 + t][:, o], c_pT[:, h % 2, 2 * t + k, :], c_v[:, k, h * CV:(h + 1) * CV],
                                         start=k == 0, stop=k == 1)
                last.then_inc(S["c_o_psum"], 1)

            def output_T(half):
                pe.wait_ge(S["c_o_ready"], 2 * (half + 1))
                for t in range(NT):
                    for k in range(4):
                        kk = 4 * half + k
                        last = pe.transpose(bank[2 * half + t][:, k * P:(k + 1) * P],
                                            x_norm[:, t, kk * P:(kk + 1) * P], ident[:])
                    last.then_inc(S["t_psum"], 1)

            mla_qk(0)
            pe.wait_ge(S["c_kv0_ready"], 1)
            keys_values(1, 1)
            for r in range(1, CH + 3):
                if r < CH:
                    mla_qk(r)
                if 0 <= r - 1 < CH:
                    mla_scores(r - 1)
                if r == CH:
                    output_T(0)
                if 0 <= r - 2 < CH:
                    mla_pT(r - 2)
                if 0 <= r - 3 < CH:
                    mla_values(r - 3)
            o = sched["c_out"]
            pe.wait_ge(S["xTl_ready"], 4 * 5 + 2)
            operand_out(o[0], 0, first=True, ts=(0,))
            output_T(1)
            operand_out(o[1], 1, ts=(0,))
            operand_out(o[0], 0, first=True, ts=(1,))
            operand_out(o[1], 1, ts=(1,))
            pe.wait_ge(S["xTl_ready"], 4 * 5 + 4)
            for t in range(NT):
                operand_out(o[2], 2, ts=(t,))
                operand_out(o[3], 3, ts=(t,), end=True, phase_end=True, norm=6)
            squared_relu(1, 6, 6)


INPUTS = ("x", "norm_mix", "norm_ffn", "swa_w_in", "swa_sinks", "swa_w_out", "ffn_w_gate_up", "ffn_w_down",
          "final_norm", "positions_2", "ab_norm_2", "ab_w_in_2", "ab_conv_2", "ab_gate_b_2", "ab_head_g_2",
          "ab_v_g_2", "ab_ws_2", "ab_bs_2", "ab_w_out_2", "c_norm_2", "c_w_in_2", "c_q_g_2", "c_kv_g_2",
          "c_w_uq_2", "c_w_ukv_2", "c_w_out_2", "ffn_norm_2", "ffn_w1_2", "ffn_w2_2", "final_norm_2")


def kernel(**inputs):
    import numpy as np
    import concourse.bacc as bacc
    from concourse.bass_utils import run_bass_kernel_spmd

    nc = bacc.Bacc("TRN2", target_bir_lowering=False, num_devices=1)
    arrays, t_in = {}, {}
    for name in INPUTS:
        a = np.ascontiguousarray(inputs[name])
        arrays[f"in_{name}"] = a
        t_in[name] = nc.dram_tensor(f"in_{name}", a.shape, mybir.dt.from_np(a.dtype), kind="ExternalInput").ap()
    out = nc.dram_tensor("out_0", (1, SEQ, DM), F32, kind="ExternalOutput").ap()
    build(nc, t_in, out)
    r = run_bass_kernel_spmd(nc, [arrays], core_ids=[0])
    return r.results[0]["out_0"]
```
